# Optimizing a Trainium2 kernel written in Bass

```python
import jax
import jax.numpy as jnp
from jax import lax
import numpy as np
import math
import jax, jax.numpy as jnp

D_MODEL = 2048
BATCH = 1
SEQ = 256
DEPTH = 1

HEAD_DIM = 64
N_MIX_HEADS = D_MODEL // HEAD_DIM
A_HEADS = 3 * N_MIX_HEADS // 8
B_GROUPS = N_MIX_HEADS // 4
C_HEADS = N_MIX_HEADS - A_HEADS - B_GROUPS
A_WIDTH = A_HEADS * HEAD_DIM
B_WIDTH = B_GROUPS * HEAD_DIM
C_WIDTH = C_HEADS * HEAD_DIM
D_MIX = A_WIDTH + B_WIDTH + C_WIDTH

DILATED_PATTERNS = ((128, 1), (512, 4), (2048, 16))
BLOCK = 128
REL_BUCKETS = 32
REL_MAX_DISTANCE = 2048

CHUNK = 128

W_LORA = 64
A_LORA = 64
G_LORA = 256
C_LORA = W_LORA + A_LORA + G_LORA
C_IN_COLS = 3 * C_WIDTH + C_LORA
RWKV_GN_EPS = 64e-5

MEM_TOKENS = 256
MEM_HEADS = 4
MEM_HEAD_DIM = 128
MEM_INNER = MEM_HEADS * MEM_HEAD_DIM

D_FF = 5632
CONV_WIDTH = 3

IN_COLS = 3 * A_WIDTH + 2 * B_WIDTH + C_IN_COLS
NORM_EPS = 1e-6
NEG_INF = -1e30


def rmsnorm(x, gain):
    xf = x.astype(jnp.float32)
    y = xf * lax.rsqrt(jnp.mean(xf * xf, axis=-1, keepdims=True) + NORM_EPS)
    return (y * gain.astype(jnp.float32)).astype(x.dtype)

def layernorm(x, gain):
    xf = x.astype(jnp.float32)
    xc = xf - jnp.mean(xf, axis=-1, keepdims=True)
    y = xc * lax.rsqrt(jnp.mean(xc * xc, axis=-1, keepdims=True) + NORM_EPS)
    return (y * gain.astype(jnp.float32)).astype(x.dtype)

def t5_causal_bucket(dist):
    max_exact = REL_BUCKETS // 2
    d = np.maximum(dist, 0)
    scaled = np.log(np.maximum(d, 1) / max_exact) / np.log(REL_MAX_DISTANCE / max_exact)
    large = np.minimum(max_exact + (scaled * (REL_BUCKETS - max_exact)).astype(np.int32), REL_BUCKETS - 1)
    return np.where(d < max_exact, d, large).astype(np.int32)

def dilated_pattern(q, k, v, rel_bias_table, window, dilation):
    b, s, h, dh = q.shape
    steps = window // dilation
    sub_len = s // dilation
    n_blk = -(-sub_len // BLOCK)
    pad = n_blk * BLOCK - sub_len

    def strided(z):
        z = z.reshape(b, sub_len, dilation, h, dh).transpose(0, 2, 3, 1, 4)
        z = jnp.pad(z, ((0, 0), (0, 0), (0, 0), (0, pad), (0, 0)))
        return z.reshape(b, dilation, h, n_blk, BLOCK, dh)

    def with_prev(z):
        prev = jnp.pad(z, ((0, 0), (0, 0), (0, 0), (1, 0), (0, 0), (0, 0)))[:, :, :, :-1]
        return jnp.concatenate([prev, z], axis=4)

    qb = strided(q)
    kw = with_prev(strided(k))
    vw = with_prev(strided(v))

    qi = np.arange(BLOCK)[:, None]
    kj = np.arange(2 * BLOCK)[None, :]
    delta = qi + BLOCK - kj
    band = (delta >= 0) & (delta <= steps)
    valid = np.where((np.arange(n_blk) == 0)[:, None, None], band & (kj >= BLOCK), band)
    bucket = t5_causal_bucket(np.clip(delta, 0, steps) * dilation)
    bias = jnp.transpose(rel_bias_table.astype(jnp.float32)[bucket], (2, 0, 1))

    scores = jnp.einsum('brhnqd,brhnkd->brhnqk', qb, kw).astype(jnp.float32) * (dh ** -0.5)
    scores = jnp.where(valid, scores + bias[None, None, :, None], NEG_INF)
    m = jnp.max(scores, axis=-1, keepdims=True)
    p = jnp.exp(scores - m)
    den = jnp.sum(p, axis=-1, keepdims=True)
    o = jnp.einsum('brhnqk,brhnkd->brhnqd', p, vw.astype(jnp.float32)) / den
    lse = (m + jnp.log(den))[..., 0]

    def unstrided(z):
        z = z.reshape(b, dilation, h, n_blk * BLOCK, *z.shape[5:])[:, :, :, :sub_len]
        z = jnp.moveaxis(z, 3, 1)
        return z.reshape(b, s, h, *z.shape[4:])

    return unstrided(o), unstrided(lse)

def dilated_attention(q, k, v, rel_bias_table):
    outs, lses = [], []
    for window, dilation in DILATED_PATTERNS:
        o, lse = dilated_pattern(q, k, v, rel_bias_table, window, dilation)
        outs.append(o)
        lses.append(lse)
    weights = jax.nn.softmax(jnp.stack(lses), axis=0)
    return jnp.sum(weights[..., None] * jnp.stack(outs), axis=0)

def spatial_gating(zb, norm_gain, w_s, b_s):
    b, s, _ = zb.shape
    u, g = jnp.split(jax.nn.gelu(zb), 2, axis=-1)
    g = layernorm(g, norm_gain).reshape(b, s // CHUNK, CHUNK, B_GROUPS, HEAD_DIM)
    w_causal = jnp.where(np.tril(np.ones((CHUNK, CHUNK), dtype=bool)), w_s, 0)
    mixed = jnp.einsum('gij,bcjgd->bcigd', w_causal, g) + b_s.T[None, None, :, :, None]
    return u * mixed.reshape(b, s, B_WIDTH)

def rwkv7_scan(r, decay, k, v, kk, a):
    b, s, h, n = r.shape

    def step(state, inp):
        r_t, w_t, k_t, v_t, kk_t, a_t = inp
        sa = jnp.einsum('bhvk,bhk->bhv', state, -kk_t)
        state = (state * w_t[:, :, None, :] + sa[..., None] * (kk_t * a_t)[:, :, None, :]
                 + v_t[..., None] * k_t[:, :, None, :])
        return state, jnp.einsum('bhvk,bhk->bhv', state, r_t)

    xs = tuple(jnp.moveaxis(z, 1, 0) for z in (r, decay, k, v, kk, a))
    _, ys = lax.scan(step, jnp.zeros((b, h, n, n), jnp.float32), xs)
    return jnp.moveaxis(ys, 0, 1)

def rwkv7_time_mix(zc, mu, w0, w_up, a0, a_up, g_up, k_k, k_a, r_k, ln_gain, ln_bias):
    b, s, _ = zc.shape
    zc = zc.astype(jnp.float32)
    prev = jnp.pad(zc, ((0, 0), (1, 0), (0, 0)))[:, :-1]
    zc = zc + (prev - zc) * mu
    cuts = [C_WIDTH, 2 * C_WIDTH, 3 * C_WIDTH, 3 * C_WIDTH + W_LORA, 3 * C_WIDTH + W_LORA + A_LORA]
    r, k, v, w_lo, a_lo, g_lo = jnp.split(zc, cuts, axis=-1)
    w_log = -jax.nn.softplus(-(w0 + jnp.tanh(w_lo) @ w_up)) - 0.5
    decay = jnp.exp(-jnp.exp(w_log))
    a = jax.nn.sigmoid(a0 + a_lo @ a_up)
    g = jax.nn.sigmoid(g_lo) @ g_up
    kk = k * k_k
    k = k * (1.0 + (a - 1.0) * k_a)

    def heads(z):
        return z.reshape(b, s, C_HEADS, HEAD_DIM)

    r, k, v, kk, a, decay = heads(r), heads(k), heads(v), heads(kk), heads(a), heads(decay)
    kk = kk / jnp.maximum(jnp.linalg.norm(kk, axis=-1, keepdims=True), 1e-12)
    y = rwkv7_scan(r, decay, k, v, kk, a)
    mean = jnp.mean(y, axis=-1, keepdims=True)
    yc = y - mean
    y = yc * lax.rsqrt(jnp.mean(yc * yc, axis=-1, keepdims=True) + RWKV_GN_EPS)
    y = y * ln_gain.reshape(C_HEADS, HEAD_DIM) + ln_bias.reshape(C_HEADS, HEAD_DIM)
    y = y + jnp.sum(r * k * r_k, axis=-1, keepdims=True) * v
    return y.reshape(b, s, C_WIDTH) * g

def hybrid_mixer(h, rel_bias_table, w_in, w_out, attn_out_gain, sgu_norm_gain, sgu_w, sgu_b,
                 sgu_out_gain, rwkv_mu, rwkv_w0, rwkv_w_up, rwkv_a0, rwkv_a_up, rwkv_g_up,
                 rwkv_k_k, rwkv_k_a, rwkv_r_k, rwkv_ln_gain, rwkv_ln_bias):
    b, s, _ = h.shape
    z = h @ w_in
    za, zb, zc = jnp.split(z, [3 * A_WIDTH, 3 * A_WIDTH + 2 * B_WIDTH], axis=-1)
    qkv = za.reshape(b, s, 3, A_HEADS, HEAD_DIM)
    oa = dilated_attention(qkv[:, :, 0], qkv[:, :, 1], qkv[:, :, 2], rel_bias_table)
    oa = rmsnorm(oa.reshape(b, s, A_WIDTH), attn_out_gain).astype(h.dtype)
    ob = rmsnorm(spatial_gating(zb, sgu_norm_gain, sgu_w, sgu_b), sgu_out_gain).astype(h.dtype)
    oc = rwkv7_time_mix(zc, rwkv_mu, rwkv_w0, rwkv_w_up, rwkv_a0, rwkv_a_up, rwkv_g_up,
                        rwkv_k_k, rwkv_k_a, rwkv_r_k, rwkv_ln_gain, rwkv_ln_bias).astype(h.dtype)
    return jnp.concatenate([oa, ob, oc], axis=-1) @ w_out

def memory_cross_attention(h, mem_n, wq, wkv, wo):
    b, s, _ = h.shape
    q = (h @ wq).reshape(b, s, MEM_HEADS, MEM_HEAD_DIM)
    kv = (mem_n @ wkv).reshape(b, mem_n.shape[1], 2, MEM_HEADS, MEM_HEAD_DIM)
    scores = jnp.einsum('bshd,bmhd->bhsm', q, kv[:, :, 0]).astype(jnp.float32) * (MEM_HEAD_DIM ** -0.5)
    p = jax.nn.softmax(scores, axis=-1).astype(h.dtype)
    o = jnp.einsum('bhsm,bmhd->bshd', p, kv[:, :, 1]).reshape(b, s, MEM_INNER)
    return o @ wo

def conv_ffn(h, w_up, conv_w, conv_b, w_down):
    s = h.shape[1]
    up = h @ w_up
    up_pad = jnp.pad(up, ((0, 0), (CONV_WIDTH - 1, 0), (0, 0)))
    conv = conv_b + sum(up_pad[:, j:j + s] * conv_w[j] for j in range(CONV_WIDTH))
    gate, val = jnp.split(conv, 2, axis=-1)
    return (jax.nn.gelu(gate, approximate=True) * val) @ w_down

def first_inputs(seed: int = 0) -> dict:
    key = jax.random.key(seed)
    keys = jax.random.split(key, 40)
    counter = [0]

    def nxt():
        kk = keys[counter[0]]
        counter[0] += 1
        return kk

    def nrm(shape, scale=1.0):
        return scale * jax.random.normal(nxt(), shape, jnp.float32)

    def gain(shape):
        return 1.0 + nrm(shape, 0.1)

    L = DEPTH
    return {
        'x': nrm((BATCH, SEQ, D_MODEL)),
        'mem': nrm((BATCH, MEM_TOKENS, D_MODEL)),
        'rel_bias_table': nrm((REL_BUCKETS, A_HEADS), 0.5),
        'sandwich_gains': gain((L, 6, D_MODEL)),
        'mem_src_gain': gain((L, D_MODEL)),
        'w_in': nrm((L, D_MODEL, IN_COLS), D_MODEL ** -0.5),
        'w_out': nrm((L, D_MIX, D_MODEL), D_MIX ** -0.5),
        'attn_out_gain': gain((L, A_WIDTH)),
        'sgu_norm_gain': gain((L, B_WIDTH)),
        'sgu_w': nrm((L, B_GROUPS, CHUNK, CHUNK), CHUNK ** -0.5),
        'sgu_b': gain((L, B_GROUPS, CHUNK)),
        'sgu_out_gain': gain((L, B_WIDTH)),
        'rwkv_mu': jax.random.uniform(nxt(), (L, C_IN_COLS), jnp.float32),
        'rwkv_w0': nrm((L, C_WIDTH), 0.5),
        'rwkv_w_up': nrm((L, W_LORA, C_WIDTH), W_LORA ** -0.5),
        'rwkv_a0': nrm((L, C_WIDTH), 0.1),
        'rwkv_a_up': nrm((L, A_LORA, C_WIDTH), A_LORA ** -0.5),
        'rwkv_g_up': nrm((L, G_LORA, C_WIDTH), G_LORA ** -0.5),
        'rwkv_k_k': gain((L, C_WIDTH)),
        'rwkv_k_a': gain((L, C_WIDTH)),
        'rwkv_r_k': nrm((L, C_HEADS, HEAD_DIM), 0.1),
        'rwkv_ln_gain': gain((L, C_WIDTH)),
        'rwkv_ln_bias': nrm((L, C_WIDTH), 0.01),
        'mem_wq': nrm((L, D_MODEL, MEM_INNER), D_MODEL ** -0.5),
        'mem_wkv': nrm((L, D_MODEL, 2 * MEM_INNER), D_MODEL ** -0.5),
        'mem_wo': nrm((L, MEM_INNER, D_MODEL), MEM_INNER ** -0.5),
        'ffn_w_up': nrm((L, D_MODEL, 2 * D_FF), D_MODEL ** -0.5),
        'ffn_conv_w': nrm((L, CONV_WIDTH, 2 * D_FF), CONV_WIDTH ** -0.5),
        'ffn_conv_b': nrm((L, 2 * D_FF), 0.01),
        'ffn_w_down': nrm((L, D_FF, D_MODEL), D_FF ** -0.5),
    }

def first_block(x, mem, rel_bias_table, sandwich_gains, mem_src_gain, w_in, w_out, attn_out_gain,
              sgu_norm_gain, sgu_w, sgu_b, sgu_out_gain, rwkv_mu, rwkv_w0, rwkv_w_up, rwkv_a0,
              rwkv_a_up, rwkv_g_up, rwkv_k_k, rwkv_k_a, rwkv_r_k, rwkv_ln_gain, rwkv_ln_bias,
              mem_wq, mem_wkv, mem_wo, ffn_w_up, ffn_conv_w, ffn_conv_b, ffn_w_down):
    for l in range(DEPTH):
        g = sandwich_gains[l]
        h = rmsnorm(x, g[0])
        y = hybrid_mixer(h, rel_bias_table, w_in[l], w_out[l], attn_out_gain[l], sgu_norm_gain[l],
                         sgu_w[l], sgu_b[l], sgu_out_gain[l], rwkv_mu[l], rwkv_w0[l], rwkv_w_up[l],
                         rwkv_a0[l], rwkv_a_up[l], rwkv_g_up[l], rwkv_k_k[l], rwkv_k_a[l], rwkv_r_k[l],
                         rwkv_ln_gain[l], rwkv_ln_bias[l])
        x = x + rmsnorm(y, g[1])
        h = rmsnorm(x, g[2])
        y = memory_cross_attention(h, rmsnorm(mem, mem_src_gain[l]), mem_wq[l], mem_wkv[l], mem_wo[l])
        x = x + rmsnorm(y, g[3])
        h = rmsnorm(x, g[4])
        y = conv_ffn(h, ffn_w_up[l], ffn_conv_w[l], ffn_conv_b[l], ffn_w_down[l])
        x = x + rmsnorm(y, g[5])
    return x


DEPTH_2 = 2

HEAD_DIM_2 = 128
WINDOW = 128
RMS_EPS = 1e-6
NEG_INF_2 = -1e30
SWA_HEADS = 8
SWA_KV_HEADS = 2
SWA_WIDTH = SWA_HEADS * HEAD_DIM_2
SWA_KV_WIDTH = SWA_KV_HEADS * HEAD_DIM_2
MLA_HEADS = 4
MLA_NOPE_DIM = 128
MLA_ROPE_DIM = 64
MLA_V_DIM = 128
MLA_Q_RANK = 384
MLA_KV_RANK = 256
MLA_WIDTH = MLA_HEADS * MLA_V_DIM
ROPE_THETA = 10000.0
DIFF_HEADS = 4
DIFF_QK_DIM = 64
DIFF_V_DIM = 128
DIFF_QK_WIDTH = DIFF_HEADS * 2 * DIFF_QK_DIM
DIFF_WIDTH = DIFF_HEADS * DIFF_V_DIM

D_MIX_2 = SWA_WIDTH + MLA_WIDTH + DIFF_WIDTH
SPLIT_SIZES = (SWA_WIDTH, SWA_KV_WIDTH, SWA_KV_WIDTH, SWA_WIDTH,
               MLA_Q_RANK, MLA_KV_RANK, MLA_ROPE_DIM, MLA_WIDTH,
               DIFF_QK_WIDTH, DIFF_QK_WIDTH, DIFF_WIDTH, DIFF_WIDTH)
SPLIT_OFFSETS = tuple(int(o) for o in np.cumsum(SPLIT_SIZES)[:-1])
D_IN = int(sum(SPLIT_SIZES))


def rmsnorm_2(x, g):
    xf = x.astype(jnp.float32)
    xf = xf * lax.rsqrt(jnp.mean(xf * xf, axis=-1, keepdims=True) + RMS_EPS)
    return xf.astype(x.dtype) * g

def alibi_slopes(n):
    return jnp.asarray(np.array([2.0 ** (-8.0 * (i + 1) / n) for i in range(n)], dtype=np.float32))

def rope(x, positions):
    d = x.shape[-1]
    inv = ROPE_THETA ** (-jnp.arange(0, d, 2, dtype=jnp.float32) / d)
    ang = positions.astype(jnp.float32)[:, None] * inv[None, :]
    shape = (ang.shape[0],) + (1,) * (x.ndim - 3) + (d // 2,)
    cos = jnp.cos(ang).reshape(shape).astype(x.dtype)
    sin = jnp.sin(ang).reshape(shape).astype(x.dtype)
    x1, x2 = x[..., : d // 2], x[..., d // 2:]
    return jnp.concatenate([x1 * cos - x2 * sin, x1 * sin + x2 * cos], axis=-1)

def to_blocks(t):
    b, s = t.shape[:2]
    return jnp.moveaxis(t.reshape((b, s // BLOCK, BLOCK) + t.shape[2:]), 1, 0)

def from_blocks(t):
    nb, b = t.shape[:2]
    return jnp.moveaxis(t, 0, 1).reshape((b, nb * BLOCK) + t.shape[3:])

def swa_attention(q, k, v, sink, positions):
    b, s = q.shape[:2]
    nb = s // BLOCK
    g = SWA_HEADS // SWA_KV_HEADS
    qb = q.reshape(b, nb, BLOCK, SWA_KV_HEADS, g, HEAD_DIM_2)

    def band(t):
        pad = [(0, 0), (BLOCK, BLOCK)] + [(0, 0)] * (t.ndim - 2)
        tp = jnp.pad(t, pad).reshape((b, nb + 2, BLOCK) + t.shape[2:])
        return jnp.concatenate([tp[:, :-2], tp[:, 1:-1], tp[:, 2:]], axis=2)

    def band1d(t):
        tp = jnp.pad(t, (BLOCK, BLOCK)).reshape(nb + 2, BLOCK)
        return jnp.concatenate([tp[:-2], tp[1:-1], tp[2:]], axis=1)

    kb, vb = band(k), band(v)
    kpos = band1d(positions)
    valid = band1d(jnp.ones((s,), dtype=jnp.bool_))
    qpos = positions.reshape(nb, BLOCK)
    dist = jnp.abs(qpos[:, :, None] - kpos[:, None, :])
    mask = valid[:, None, :] & (dist <= WINDOW)

    scale = HEAD_DIM_2 ** -0.5
    sc = jnp.einsum('bnqhgd,bnkhd->bnhgqk', qb, kb).astype(jnp.float32) * scale
    slopes = alibi_slopes(SWA_HEADS).reshape(SWA_KV_HEADS, g)
    sc = sc - slopes[None, None, :, :, None, None] * dist.astype(jnp.float32)[None, :, None, None]
    sc = jnp.where(mask[None, :, None, None], sc, NEG_INF_2)
    sk = sink.astype(jnp.float32).reshape(SWA_KV_HEADS, g)[None, None, :, :, None, None]
    m = jnp.maximum(jnp.max(sc, axis=-1, keepdims=True), sk)
    p = jnp.exp(sc - m)
    p = p / (jnp.sum(p, axis=-1, keepdims=True) + jnp.exp(sk - m))
    out = jnp.einsum('bnhgqk,bnkhd->bnqhgd', p.astype(v.dtype), vb)
    return out.reshape(b, s, SWA_WIDTH)

def mla_attention(c_q, c_kv, k_rope, q_norm, w_uq, kv_norm, w_ukv, positions):
    b, s = c_q.shape[:2]
    q = jnp.einsum('bsr,re->bse', rmsnorm_2(c_q, q_norm), w_uq)
    q = q.reshape(b, s, MLA_HEADS, MLA_NOPE_DIM + MLA_ROPE_DIM)
    q_nope = q[..., :MLA_NOPE_DIM]
    q_rope = rope(q[..., MLA_NOPE_DIM:], positions)
    kv = jnp.einsum('bsr,re->bse', rmsnorm_2(c_kv, kv_norm), w_ukv)
    kv = kv.reshape(b, s, MLA_HEADS, MLA_NOPE_DIM + MLA_V_DIM)
    k_nope, v = kv[..., :MLA_NOPE_DIM], kv[..., MLA_NOPE_DIM:]
    k_r = rope(k_rope, positions)
    scale = (MLA_NOPE_DIM + MLA_ROPE_DIM) ** -0.5

    def block(xs):
        qn, qr = xs
        sc = (jnp.einsum('bqhd,bkhd->bhqk', qn, k_nope)
              + jnp.einsum('bqhd,bkd->bhqk', qr, k_r)).astype(jnp.float32) * scale
        a = jax.nn.softmax(sc, axis=-1).astype(v.dtype)
        return jnp.einsum('bhqk,bkhd->bqhd', a, v)

    out = from_blocks(lax.map(block, (to_blocks(q_nope), to_blocks(q_rope))))
    return out.reshape(b, s, MLA_WIDTH)

def diff_attention(q, k, v, lam_params, subln_g, positions, lam_init):
    b, s = q.shape[:2]
    nb = s // BLOCK
    lp = lam_params.astype(jnp.float32)
    lam = jnp.exp(jnp.sum(lp[0] * lp[1])) - jnp.exp(jnp.sum(lp[2] * lp[3])) + lam_init
    slopes = alibi_slopes(DIFF_HEADS)
    scale = DIFF_QK_DIM ** -0.5

    def block(xs):
        qb, qpos = xs
        sc = jnp.einsum('bqhcd,bkhcd->bhcqk', qb, k).astype(jnp.float32) * scale
        dist = jnp.abs(qpos[:, None] - positions[None, :]).astype(jnp.float32)
        sc = sc - slopes[None, :, None, None, None] * dist[None, None, None]
        a = jax.nn.softmax(sc, axis=-1)
        attn = (a[:, :, 0] - lam * a[:, :, 1]).astype(v.dtype)
        return jnp.einsum('bhqk,bkhd->bqhd', attn, v)

    out = from_blocks(lax.map(block, (to_blocks(q), positions.reshape(nb, BLOCK))))
    out = rmsnorm_2(out, subln_g) * (1.0 - lam_init)
    return out.reshape(b, s, DIFF_WIDTH)

def second_inputs(seed: int = 0) -> dict:
    key = jax.random.key(seed)
    ks = jax.random.split(key, 16)
    f32 = jnp.float32
    nrm = lambda k, shape, sc: jax.random.normal(k, shape, dtype=f32) * sc
    return {
        "x": nrm(ks[0], (BATCH, SEQ, D_MODEL), 1.0),
        "positions": jnp.arange(SEQ, dtype=jnp.int32),
        "norm_g": 1.0 + nrm(ks[1], (DEPTH_2, D_MODEL), 0.02),
        "w_in": nrm(ks[2], (DEPTH_2, D_MODEL, D_IN), D_MODEL ** -0.5),
        "swa_sink": nrm(ks[3], (DEPTH_2, SWA_HEADS), 0.5),
        "mla_q_norm": 1.0 + nrm(ks[4], (DEPTH_2, MLA_Q_RANK), 0.02),
        "mla_w_uq": nrm(ks[5], (DEPTH_2, MLA_Q_RANK, MLA_HEADS * (MLA_NOPE_DIM + MLA_ROPE_DIM)), MLA_Q_RANK ** -0.5),
        "mla_kv_norm": 1.0 + nrm(ks[6], (DEPTH_2, MLA_KV_RANK), 0.02),
        "mla_w_ukv": nrm(ks[7], (DEPTH_2, MLA_KV_RANK, MLA_HEADS * (MLA_NOPE_DIM + MLA_V_DIM)), MLA_KV_RANK ** -0.5),
        "diff_lambda": nrm(ks[8], (DEPTH_2, 4, DIFF_QK_DIM), 0.1),
        "diff_subln": 1.0 + nrm(ks[9], (DEPTH_2, DIFF_V_DIM), 0.02),
        "w_out": nrm(ks[10], (DEPTH_2, D_MIX_2, D_MODEL), D_MIX_2 ** -0.5),
        "final_norm": 1.0 + nrm(ks[11], (D_MODEL,), 0.02),
    }

def second_block(x, positions, norm_g, w_in, swa_sink, mla_q_norm, mla_w_uq, mla_kv_norm,
              mla_w_ukv, diff_lambda, diff_subln, w_out, final_norm):
    b, s, _ = x.shape
    for l in range(DEPTH_2):
        h = rmsnorm_2(x, norm_g[l])
        proj = jnp.einsum('bsd,de->bse', h, w_in[l])
        (a_q, a_k, a_v, a_g, b_cq, b_ckv, b_kr, b_g,
         c_q, c_k, c_v, c_g) = jnp.split(proj, SPLIT_OFFSETS, axis=-1)
        ya = swa_attention(a_q.reshape(b, s, SWA_HEADS, HEAD_DIM_2),
                           a_k.reshape(b, s, SWA_KV_HEADS, HEAD_DIM_2),
                           a_v.reshape(b, s, SWA_KV_HEADS, HEAD_DIM_2),
                           swa_sink[l], positions)
        yb = mla_attention(b_cq, b_ckv, b_kr, mla_q_norm[l], mla_w_uq[l],
                           mla_kv_norm[l], mla_w_ukv[l], positions)
        lam_init = 0.8 - 0.6 * math.exp(-0.3 * l)
        yc = diff_attention(c_q.reshape(b, s, DIFF_HEADS, 2, DIFF_QK_DIM),
                            c_k.reshape(b, s, DIFF_HEADS, 2, DIFF_QK_DIM),
                            c_v.reshape(b, s, DIFF_HEADS, DIFF_V_DIM),
                            diff_lambda[l], diff_subln[l], positions, lam_init)
        y = jnp.concatenate([ya * jax.nn.silu(a_g), yb * jax.nn.silu(b_g),
                             yc * jax.nn.silu(c_g)], axis=-1)
        x = x + jnp.einsum('bse,ed->bsd', y, w_out[l])
    return rmsnorm_2(x, final_norm)


def setup_inputs(seed=0):
    out = dict(first_inputs(seed))
    for name, value in second_inputs(seed + 1).items():
        if name != "x":
            out[name + "_2"] = value
    return out


def reference(
    x, mem, rel_bias_table, sandwich_gains, mem_src_gain, w_in, w_out, attn_out_gain,
    sgu_norm_gain, sgu_w, sgu_b, sgu_out_gain, rwkv_mu, rwkv_w0, rwkv_w_up, rwkv_a0, rwkv_a_up,
    rwkv_g_up, rwkv_k_k, rwkv_k_a, rwkv_r_k, rwkv_ln_gain, rwkv_ln_bias, mem_wq, mem_wkv,
    mem_wo, ffn_w_up, ffn_conv_w, ffn_conv_b, ffn_w_down, positions_2, norm_g_2, w_in_2,
    swa_sink_2, mla_q_norm_2, mla_w_uq_2, mla_kv_norm_2, mla_w_ukv_2, diff_lambda_2,
    diff_subln_2, w_out_2, final_norm_2,
):
    x = first_block(
        x, mem, rel_bias_table, sandwich_gains, mem_src_gain, w_in, w_out, attn_out_gain,
        sgu_norm_gain, sgu_w, sgu_b, sgu_out_gain, rwkv_mu, rwkv_w0, rwkv_w_up, rwkv_a0,
        rwkv_a_up, rwkv_g_up, rwkv_k_k, rwkv_k_a, rwkv_r_k, rwkv_ln_gain, rwkv_ln_bias, mem_wq,
        mem_wkv, mem_wo, ffn_w_up, ffn_conv_w, ffn_conv_b, ffn_w_down,
    )
    return second_block(
        x, positions_2, norm_g_2, w_in_2, swa_sink_2, mla_q_norm_2, mla_w_uq_2, mla_kv_norm_2,
        mla_w_ukv_2, diff_lambda_2, diff_subln_2, w_out_2, final_norm_2,
    )


_drawn_inputs = setup_inputs


def setup_inputs(seed=0):
    import zlib

    import numpy as np

    out = dict(_drawn_inputs(seed))
    spreads = {}
    factors = {'rwkv_a0': 3.366,
     'rwkv_k_k': 8.0,
     'rwkv_ln_bias': 8.0,
     'ffn_conv_b': 7.701,
     'norm_g_2': 8.0,
     'swa_sink_2': 8.0,
     'mla_q_norm_2': 8.0,
     'mla_w_uq_2': 3.237,
     'mla_kv_norm_2': 8.0,
     'diff_lambda_2': 2.766,
     'diff_subln_2': 8.0,
     'final_norm_2': 2.865}
    for name, (base, spread) in spreads.items():
        noise = np.random.default_rng([zlib.crc32(name.encode()), seed]).standard_normal(out[name].shape)
        drawn = base * np.exp(spread * noise) if base else spread * noise
        out[name] = jnp.asarray(drawn.astype(out[name].dtype))
    for name, factor in factors.items():
        out[name] = (out[name] * factor).astype(out[name].dtype)
    return out
```

```python
from contextlib import ExitStack
import math

import numpy as np
import concourse.bass as bass
from concourse import mybir

F32 = mybir.dt.float32
F32R = mybir.dt.float32r
I32 = mybir.dt.int32
ALU = mybir.AluOpType
ACT = mybir.ActivationFunctionType
AX = mybir.AxisListType

P = 128
S = 256
TB = S // P
D = 2048
KB = D // P
HD = 64
A_H, B_G, C_H = 12, 8, 12
A_W, B_W, C_W = A_H * HD, B_G * HD, C_H * HD
CB = C_W // P
M_H, M_D = 4, 128
M_I = M_H * M_D
D_FF = 5632
FB = D_FF // P
REL = 32
EPS, GN_EPS = 1e-6, 64e-5
NEG = -1e30
BIG = 1e30
LAYERS = 2
Z_COLS = 3 * A_W + 2 * B_W + 3 * C_W + 384
W2_COLS = 5824
L2_HALF = 32

PARAM_BLOCKS = [("g_mix", 16), ("g_mem", 16), ("g_ffn", 16), ("g_src", 16), ("g_l0", 16), ("g_l1", 16),
                ("mu", 21), ("w0", 6), ("a0", 6), ("k_k", 6), ("k_a", 6), ("r_k", 6), ("attn_gain", 6),
                ("sgu_gain", 4), ("conv_b", 88), ("conv_w", 264), ("q_norm", 6), ("kv_norm", 4)]
PARAM_AT, _n = {}, 0
for _name, _w in PARAM_BLOCKS:
    PARAM_AT[_name] = _n
    _n += _w
N_PARAM = _n


class Program:

    ENGINES = ("pe", "act", "dve", "pool", "sp")

    def __init__(self, nc, ctx):
        self.queue = {e: [] for e in self.ENGINES}
        self.done = {e: ctx.enter_context(nc.semaphore(f"done_{e}")) for e in self.ENGINES}
        self.count = dict.fromkeys(self.ENGINES, 0)
        self.dma_sems = {}
        self.nc, self.ctx = nc, ctx

    def wait(self, engine, *after):
        for token in flat(after):
            self.queue[engine].append(lambda e, i, t=token: e.wait_ge(t[0], t[1]))

    def do(self, engine, fn, *after):
        self.wait(engine, *after)
        self.count[engine] += 1
        self.queue[engine].append(lambda e, i: fn(e).then_inc(self.done[engine], 1))
        return (self.done[engine], self.count[engine])

    def quiet(self, engine, fn, *after):
        self.wait(engine, *after)
        self.queue[engine].append(lambda e, i: fn(e))

    def dma(self, engine, out, in_, name, *after):
        if name not in self.dma_sems:
            self.dma_sems[name] = [self.ctx.enter_context(self.nc.semaphore(name)), 0]
        entry = self.dma_sems[name]
        entry[1] += 16
        self.wait(engine, *after)
        self.queue[engine].append(lambda e, i: e.dma_start(out, in_).then_inc(entry[0], 16))
        return (entry[0], entry[1])

    def all_done(self):
        return [(self.done[e], self.count[e]) for e in self.ENGINES if self.count[e]]

    def loop(self, n, bodies):
        for engine, body in bodies.items():
            def run(e, _i, body=body):
                with e.Fori(0, n) as i:
                    body(e, i)
            self.queue[engine].append(run)

    def once(self, i, bodies):
        for engine, body in bodies.items():
            self.queue[engine].append(lambda e, _i, body=body: body(e, i))


def flat(x):
    for t in x:
        if t is None:
            continue
        if isinstance(t, tuple) and len(t) == 2 and isinstance(t[1], int):
            yield t
        else:
            yield from flat(t)


def hybrid_two_blocks(nc, I, out):
    with ExitStack() as ctx:
        def sb(name, shape, dt=F32):
            return ctx.enter_context(nc.sbuf_tensor(name, shape, dt))

        prog = Program(nc, ctx)
        do, quiet, dma, wait = prog.do, prog.quiet, prog.dma, prog.wait

        base = -(-nc.sbuf_base // 32) * 32
        h_hi = sb("h_hi", [P, KB, S], F32R)
        h_lo = sb("h_lo", [P, KB, S], F32R)
        side = nc.alloc_sbuf_tensor_at("side", [P, 2 * KB * S], F32, offset=base)
        raw = sb("raw", [P, 4, 2048])
        w_hi = sb("w_hi", [P, 2, 2048], F32R)
        w_lo = sb("w_lo", [P, 2, 2048], F32R)
        x = sb("x", [P, TB, D])
        ARENA = 22400
        arena = sb("arena", [P, ARENA])
        params = sb("params", [P, N_PARAM])
        ident = sb("ident", [P, P])
        exch = sb("exch", [P, P])
        small = sb("small", [P, 512])
        PS = ctx.enter_context(nc.psum_tensor("PS", [P, 8, 512], F32))

        def view(t, at, dims):
            n = int(np.prod(dims))
            v = t[:, at:at + n]
            if len(dims) == 1:
                return v
            names = "abcd"[:len(dims)]
            return v.rearrange(f"p ({' '.join(names)}) -> p {' '.join(names)}",
                               **{c: d for c, d in zip(names[1:], dims[1:])})

        def ar(at, *dims):
            return view(arena, at, dims)

        def sd(at, *dims):
            return view(side, at, dims)

        def par(name, k=0):
            return params[:, PARAM_AT[name] + k:PARAM_AT[name] + k + 1]

        def bcast(name, at, n):
            return bass.AP(I[name].tensor, at, [[0, P], [1, n]])

        small_at = [0]

        def col(n):
            a = small_at[0]
            small_at[0] += n
            assert small_at[0] <= 512
            return small[:, a:a + n]

        sem = {n: ctx.enter_context(nc.semaphore(n)) for n in
               ("landed0", "landed1", "landed2", "landed3", "hi_made", "lo_made", "unit_used",
                "act_evac", "dve_evac")}
        landed = [sem[f"landed{j}"] for j in range(4)]
        right_landed = [ctx.enter_context(nc.semaphore(f"right_landed{j}")) for j in range(4)]
        LO_CREDIT, UNIT_CREDIT, EVAC_CREDIT = 4, 2, 2
        state = {"unit": 0, "group": 0}

        def load_unit(e, U, slot, dst_dims, src):
            e.wait_ge(sem["lo_made"], U + 1)
            dst = raw[:, slot, :dst_dims[0] * dst_dims[1]].rearrange("p (k n) -> p k n", k=dst_dims[0])
            if isinstance(src, tuple):
                half = dst_dims[1] // 2
                e.dma_start(dst[:, :, half:], src[1]).then_inc(right_landed[slot], 16)
                dst, src = dst[:, :, :half], src[0]
            e.dma_start(dst, src).then_inc(landed[slot], 16)

        def split_hi(e, U, quad, slot, n):
            e.wait_ge(landed[slot], quad * 16 + 16)
            e.wait_ge(sem["unit_used"], U + 1)
            e.activation(w_hi[:, slot % 2, :n], raw[:, slot, :n], ACT.Copy).then_inc(sem["hi_made"], 1)

        def split_lo(e, U, slot, n):
            e.wait_ge(sem["hi_made"], U + 1)
            e.tensor_tensor(w_lo[:, slot % 2, :n], raw[:, slot, :n],
                            w_hi[:, slot % 2, :n].bitcast(F32), ALU.subtract).then_inc(sem["lo_made"], 1)

        def three_pass(e, ps, l_hi, l_lo, r_hi, r_lo, start, stop, skip=False):
            e.matmul(ps, l_hi, r_hi, start=start, stop=False, skip_group_check=skip)
            e.matmul(ps, l_hi, r_lo, start=False, stop=False, skip_group_check=skip)
            return e.matmul(ps, l_lo, r_hi, start=False, stop=stop, skip_group_check=skip)

        def products(name, src, n_groups, evac_act, evac_dve, tok_cols=None, ch_cols=None, n_cols=512,
                     units=4, kb_per_unit=4, after=(), rolled=True, evac_after=(), finish=None, halves=False):
            U0, G0 = state["unit"], state["group"]
            state["unit"] += units * n_groups
            state["group"] += n_groups
            n = kb_per_unit * n_cols
            wait("pe", *after)
            wait("act", *evac_after)
            wait("dve", *evac_after)

            def group(g, parity, U, quad, first_slot):
                bank = [2 * parity, 2 * parity + 1]

                def sp(e):
                    for j in range(units):
                        load_unit(e, U + j, (first_slot + j) % 4, (kb_per_unit, n_cols), src(g, j))

                def act(e, j):
                    if halves:
                        e.wait_ge(right_landed[j], g * 16 + 16)
                    split_hi(e, U + j, quad, (first_slot + j) % 4, n)

                def dve(e, j):
                    split_lo(e, U + j, (first_slot + j) % 4, n)

                def pe(e):
                    e.wait_ge(sem["act_evac"], G0 + g + 1)
                    e.wait_ge(sem["dve_evac"], G0 + g + 1)
                    for j in range(units):
                        slot = (first_slot + j) % 2
                        e.wait_ge(sem["lo_made"], LO_CREDIT + U + j + 1)
                        wh = w_hi[:, slot, :n].rearrange("p (k n) -> p k n", k=kb_per_unit)
                        wl = w_lo[:, slot, :n].rearrange("p (k n) -> p k n", k=kb_per_unit)
                        last = None
                        if tok_cols:
                            c0, w = tok_cols
                            at_once = bool(ch_cols)
                            for t in range(TB):
                                for k in range(kb_per_unit):
                                    kk = j * kb_per_unit + k
                                    o = (PS[:, bank[1], t * w:(t + 1) * w] if at_once
                                         else PS[:, bank[t], :w])
                                    last = three_pass(
                                        e, o, h_hi[:, kk, t * P:(t + 1) * P], h_lo[:, kk, t * P:(t + 1) * P],
                                        wh[:, k, c0:c0 + w], wl[:, k, c0:c0 + w],
                                        kk == 0 and not (at_once and t), kk == units * kb_per_unit - 1,
                                        at_once)
                        if ch_cols:
                            c0, w = ch_cols
                            for c in range(w // P):
                                for k in range(kb_per_unit):
                                    kk = j * kb_per_unit + k
                                    o = PS[:, bank[c // 2], (c % 2) * S:(c % 2 + 1) * S]
                                    ws = slice(c0 + c * P, c0 + (c + 1) * P)
                                    last = three_pass(e, o, wh[:, k, ws], wl[:, k, ws], h_hi[:, kk, :],
                                                      h_lo[:, kk, :], kk == 0 and c % 2 == 0,
                                                      kk == units * kb_per_unit - 1, True)
                        last.then_inc(sem["unit_used"], 1)

                def evac(e, which):
                    e.wait_ge(sem["unit_used"], UNIT_CREDIT + U + units)
                    fn, b = (evac_act, 0) if which == "act" else (evac_dve, 1)
                    fn(e, g, parity if finish else PS[:, bank[b], :]).then_inc(sem[which + "_evac"], 1)

                def end(e, which):
                    if finish:
                        finish[which](e, g, parity)

                return {"sp": sp, "act": act, "dve": dve, "pe": pe, "evac": evac, "end": end}

            per = 2 if units == 4 else 4
            def at(g):
                U = U0 + units * g
                return group(g, (G0 + g) % 2, U, U // 4, U % 4)

            def splitter(which):
                def one(e, g, grp, prev):
                    for j in range(units):
                        grp[which](e, j)
                        if j == min(1, units - 1) and prev is not None:
                            prev["evac"](e, which)
                    if prev is not None:
                        prev["end"](e, which)
                return one

            if units == 1:
                for g in range(n_groups):
                    grp, prev = at(g), at(g - 1) if g else None
                    prog.once(0, {"sp": lambda e, i, q=grp: q["sp"](e), "pe": lambda e, i, q=grp: q["pe"](e),
                                  "act": lambda e, i, g=g, q=grp, p=prev: splitter("act")(e, g, q, p),
                                  "dve": lambda e, i, g=g, q=grp, p=prev: splitter("dve")(e, g, q, p)})
                last_group = at(n_groups - 1)
            else:
                for which in ("act", "dve"):
                    prog.once(0, {which: lambda e, i, w=which: splitter(w)(e, 0, at(0), None)})
                prog.once(0, {"sp": lambda e, i: at(0)["sp"](e), "pe": lambda e, i: at(0)["pe"](e)})
                pairs = (n_groups - 1) // 2 if rolled else 0
                if pairs < 2:
                    pairs = 0

                def body(engine):
                    def run(e, i):
                        for k in range(2):
                            g = i * 2 + (1 + k)
                            U = i * (2 * units) + (U0 + units * (1 + k))
                            quad = i * 2 + (U0 // 4 + 1 + k)
                            grp = group(g, (G0 + 1 + k) % 2, U, quad, U0 % 4)
                            if engine in ("act", "dve"):
                                Up = i * (2 * units) + (U0 + units * k)
                                gp = i * 2 + k
                                prev = group(gp, (G0 + k) % 2, Up, quad, U0 % 4)
                                splitter(engine)(e, g, grp, prev)
                            else:
                                grp[engine](e)
                    return run

                if pairs:
                    prog.loop(pairs, {en: body(en) for en in ("sp", "pe", "act", "dve")})
                for g in range(1 + 2 * pairs, n_groups):
                    grp, prev = at(g), at(g - 1)
                    prog.once(0, {"sp": lambda e, i, q=grp: q["sp"](e), "pe": lambda e, i, q=grp: q["pe"](e),
                                  "act": lambda e, i, g=g, q=grp, p=prev: splitter("act")(e, g, q, p),
                                  "dve": lambda e, i, g=g, q=grp, p=prev: splitter("dve")(e, g, q, p)})
                last_group = at(n_groups - 1)
            prog.once(0, {w: lambda e, i, w=w, q=last_group: (q["evac"](e, w), q["end"](e, w))
                          for w in ("act", "dve")})
            G1, U1 = state["group"], state["unit"]
            return [(sem["act_evac"], EVAC_CREDIT + G1), (sem["dve_evac"], EVAC_CREDIT + G1),
                    (sem["unit_used"], UNIT_CREDIT + U1)]

        def w_cols(w, col0, stride=512, n_cols=512):
            v = w.rearrange("(k p) n -> p k n", p=P)
            return lambda g, j: v[:, 4 * j:4 * j + 4, bass.ds(g * stride + col0, n_cols)]

        def evac_pair(dst_a, dst_b):
            def act(e, g, bank):
                d = dst_a(g)
                return e.activation(d, bank[:, :_n(d)], ACT.Copy)

            def dve(e, g, bank):
                d = dst_b(g)
                return e.tensor_copy(d, bank[:, :_n(d)])
            return act, dve

        def _n(ap):
            return int(np.prod(ap.shape[1:]))

        def to_tokens(dst, col0):
            return evac_pair(lambda g: dst[:, 0, bass.ds(g * 512 + col0, 512)],
                             lambda g: dst[:, 1, bass.ds(g * 512 + col0, 512)])

        def to_channels(at, blk0):
            return evac_pair(lambda g: arena[:, bass.ds(g * 1024 + (at + blk0 * S), 512)],
                             lambda g: arena[:, bass.ds(g * 1024 + (at + blk0 * S + 512), 512)])

        rs = {"n": 0}
        work_bank_free = {b: [] for b in (4, 5, 6, 7)}
        bank_turn = [0]

        def next_bank():
            b = 4 + bank_turn[0] % 4
            bank_turn[0] += 1
            return b

        def rstd_of(ssq, out_col, width, eps, n, after):
            t = do("dve", lambda e: e.tensor_scalar(out_col, ssq, 1.0 / width, eps, ALU.mult, ALU.add), after)
            t = do("dve", lambda e: e.reciprocal(out_col, out_col), t)
            return do("act", lambda e: e.activation(out_col, out_col, ACT.Sqrt), t)

        def sum_squares(src, junk, after, psum=False):
            ssq = col(2)
            if psum:
                return ssq, [do("act", lambda e, t=t: e.activation(junk(t), src(t), ACT.Square,
                                                                   accum_out=ssq[:, t:t + 1]), after)
                             for t in range(TB)]
            a = do("act", lambda e: e.activation(junk(0), src(0), ACT.Square, accum_out=ssq[:, 0:1]), after)
            b = do("dve", lambda e: e.scalar_tensor_tensor(out=junk(1), in0=src(1), scalar=1.0, in1=src(1),
                                                           op0=ALU.mult, op1=ALU.mult,
                                                           accum_out=ssq[:, 1:2]), after)
            return ssq, [a, b]

        def to_h(src, gain, after, n_blocks=KB, dst=None):
            hi, lo = dst or (h_hi, h_lo)
            made = []
            for n in range((n_blocks + 1) // 2):
                b = next_bank()
                ks = [k for k in (2 * n, 2 * n + 1) if k < n_blocks]
                wait("pe", *after, *work_bank_free[b])
                for k in ks:
                    for t in range(TB):
                        fn = (lambda e, k=k, t=t, b=b: e.transpose(
                            PS[:, b, ((k % 2) * 2 + t) * P:((k % 2) * 2 + t + 1) * P],
                            src[:, t, k * P:(k + 1) * P], ident[:, :]))
                        tok = do("pe", fn) if (k, t) == (ks[-1], TB - 1) else quiet("pe", fn)
                free = []
                if gain is None:
                    m = len(ks) * S
                    dh = hi[:, ks[0]:ks[-1] + 1, :].rearrange("p k n -> p (k n)")
                    dl = lo[:, ks[0]:ks[-1] + 1, :].rearrange("p k n -> p (k n)")
                    a = do("act", lambda e, b=b, dh=dh, m=m: e.activation(dh, PS[:, b, :m], ACT.Copy), tok, after)
                    v = do("dve", lambda e, b=b, dh=dh, dl=dl, m=m: e.tensor_tensor(
                        dl, PS[:, b, :m], dh.bitcast(F32), ALU.subtract), a)
                    free, made = [a, v], made + [a, v]
                else:
                    half = {k: PS[:, b, (k % 2) * S:(k % 2 + 1) * S] for k in ks}
                    for k in ks:
                        a = do("act", lambda e, k=k, p=half[k]: e.activation(hi[:, k, :], p, ACT.Copy,
                                                                             scale=gain(k)), tok, after)
                    for k in ks:
                        v = do("dve", lambda e, k=k, p=half[k]: e.scalar_tensor_tensor(
                            out=lo[:, k, :], in0=p, scalar=gain(k), in1=hi[:, k, :].bitcast(F32),
                            op0=ALU.mult, op1=ALU.subtract), a)
                    free, made = [a, v], made + [a, v]
                work_bank_free[b] = free
            return [made[-1], made[-2]]

        def norm_to_h(src, scaled, gain, after):
            ssq, t = sum_squares(lambda t: src[:, t, :], lambda t: scaled[:, t, :], after)
            rstd = col(2)
            t = rstd_of(ssq, rstd, D, EPS, 2, t)
            out_t = []
            for tb in range(TB):
                out_t.append(do("dve", lambda e, tb=tb: e.tensor_scalar(
                    scaled[:, tb, :], src[:, tb, :], rstd[:, tb:tb + 1], None, ALU.mult), t))
            return to_h(scaled, gain, [out_t, after])

        def add_normed(y, g_bcast, junk, after, psum=False):
            ssq, t = sum_squares(y, junk, after, psum)
            rstd = col(2)
            t = rstd_of(ssq, rstd, D, EPS, 2, t)
            last = []
            for tb in range(TB):
                a = do("dve", lambda e, tb=tb: e.scalar_tensor_tensor(
                    out=junk(tb), in0=y(tb), scalar=rstd[:, tb:tb + 1], in1=g_bcast, op0=ALU.mult,
                    op1=ALU.mult), t)
                last.append(do("dve", lambda e, tb=tb: e.tensor_tensor(
                    x[:, tb, :], x[:, tb, :], junk(tb), ALU.add), a))
            return last

        Z_QK, Z_V, Z_B, Z_C = 0, 3072, 4608, 6656
        CAT = 12032
        K_MEM, V_MEM = 16128, 17152
        HANKEL = 18176
        GAINS = 20352
        cat = ar(CAT, TB, D)
        gains = ar(GAINS, D)

        t_x = dma("act", x[:, :, :], I["x"][0].rearrange("(t p) d -> p t d", p=P), "x_in")
        t_mem = dma("act", ar(0, TB, D), I["mem"][0].rearrange("(t p) d -> p t d", p=P), "mem_in")
        dma("act", params[:, :], I["params"], "consts")
        dma("act", ident[:, :], I["ident"], "consts")
        t_const = dma("act", exch[:, :], I["exch"], "consts")
        for engine, name, n in (("sp", "lo_made", LO_CREDIT), ("pe", "unit_used", UNIT_CREDIT),
                                ("act", "act_evac", EVAC_CREDIT), ("dve", "dve_evac", EVAC_CREDIT)):
            prog.queue[engine].append(lambda e, i, s=sem[name], n=n: e.sem_inc(s, n))

        t_h = norm_to_h(ar(0, TB, D), cat, lambda k: par("g_src", k), [t_mem, t_const])
        kv = w_cols(I["mem_wkv"][0], 0)
        products("mem_k", kv, 1, *to_channels(K_MEM, 0), ch_cols=(0, 512), after=t_h)
        kv2 = w_cols(I["mem_wkv"][0], M_I)
        v_mem = ar(V_MEM, TB, M_I)
        t_used = products("mem_v", kv2, 1, *to_tokens(v_mem, 0), tok_cols=(0, 512))

        t_h = norm_to_h(x, cat, lambda k: par("g_mix", k), [t_x, t_used])
        w_in = I["w_in"][0]
        z_v, z_b = ar(Z_V, TB, A_W), ar(Z_B, TB, 2 * B_W)
        products("qk", w_cols(w_in, 0), 3, *to_channels(Z_QK, 0), ch_cols=(0, 512), after=t_h,
                 evac_after=t_h)
        products("v0", w_cols(w_in, 2 * A_W), 1, *to_tokens(z_v, 0), tok_cols=(0, 512))

        def vb(t):
            def f(e, g, bank):
                if t == 0:
                    e.activation(z_v[:, t, 512:768], bank[:, 0:256], ACT.Copy)
                    return e.activation(z_b[:, t, 0:256], bank[:, 256:512], ACT.Copy)
                e.tensor_copy(z_v[:, t, 512:768], bank[:, 0:256])
                return e.tensor_copy(z_b[:, t, 0:256], bank[:, 256:512])
            return f
        products("vb", w_cols(w_in, 2 * A_W + 512), 1, vb(0), vb(1), tok_cols=(0, 512))
        products("b1", w_cols(w_in, 3 * A_W + 256), 1, *to_tokens(z_b, 256), tok_cols=(0, 512))
        products("bc", w_cols(w_in, 3 * A_W + 768), 1,
                 lambda e, g, bank: e.activation(ar(Z_C, 512), bank, ACT.Copy),
                 lambda e, g, bank: e.tensor_copy(z_b[:, :, 768:1024],
                                                  bank.rearrange("p (t n) -> p t n", t=TB)),
                 tok_cols=(0, 256), ch_cols=(256, 256))
        C0 = 3 * A_W + 2 * B_W
        products("c", w_cols(w_in, C0 + 256), 4, *to_channels(Z_C, 2), ch_cols=(0, 512))
        t_z = products("c_end", w_cols(w_in, C0 + 256 + 2048, n_cols=384), 1,
                       *evac_pair(lambda g: ar(Z_C + 18 * S, 512), lambda g: ar(Z_C + 20 * S, 256)),
                       ch_cols=(0, 384), n_cols=384)

        TBL, ONEHOT, WROW = 0, 16, 400
        t = do("dve", lambda e: e.memset(side[32:33, TBL:TBL + A_H], 1.0), t_z)
        dma("sp", side[0:REL, TBL:TBL + A_H], I["rel_bias_table"], "rel_in", t_z)
        t_rel = dma("sp", side[0:REL + 1, ONEHOT:ONEHOT + 384], I["onehot"], "rel_in")
        b = next_bank()
        t = do("pe", lambda e, b=b: e.matmul(PS[0:A_H, b, 0:384], side[0:REL + 1, TBL:TBL + A_H],
                                        side[0:REL + 1, ONEHOT:ONEHOT + 384], start=True, stop=True),
               t, t_rel, work_bank_free[b])
        t = do("dve", lambda e, b=b: e.tensor_copy(side[0:A_H, WROW:WROW + 384], PS[0:A_H, b, 0:384]), t)
        work_bank_free[b] = [t]
        scratch = I["scratch"]
        t = dma("act", scratch, side[0:A_H, WROW:WROW + 384], "rel_out", t)
        hankel = ar(HANKEL, A_H, S)
        t_hankel = dma("act", hankel, bass.AP(scratch.tensor, 0, [[1, P], [384, A_H], [1, S]]), "rel_back", t)

        zqk = ar(Z_QK, 12, S)
        P_A, PT_A = 1024, 1792
        last_turn = [[], []]
        for h in range(A_H):
            turn, rows = h % 2, slice(HD * (h % 2), HD * (h % 2) + HD)
            sb_, pb_ = 4 + turn, 6
            p_, pt_ = sd(P_A + 384 * turn, 384), sd(PT_A + 384 * turn, 384)
            nm, den = col(2), col(2)
            blk, kblk = zqk[:, h // 2, :], zqk[:, 6 + h // 2, :]
            wait("pe", t_z, t_hankel, last_turn[turn], work_bank_free[sb_])
            for t_, (o, w) in enumerate(((0, P), (P, S))):
                quiet("pe", lambda e, t_=t_, o=o, w=w, sb_=sb_, blk=blk, kblk=kblk, rows=rows: e.matmul(
                    PS[:, sb_, o:o + w], blk[rows, t_ * P:(t_ + 1) * P], kblk[rows, 0:w],
                    start=True, stop=False))
                fn = lambda e, o=o, w=w, sb_=sb_, h=h: e.matmul(
                    PS[:, sb_, o:o + w], exch[:, :], hankel[:, h, S - w:S], start=False, stop=True)
                t_s = do("pe", fn)
            work_bank_free[sb_] = []
            t1 = do("dve", lambda e, sb_=sb_, nm=nm: e.tensor_reduce(nm[:, 0:1], PS[:, sb_, 0:P], AX.X, ALU.max), t_s)
            t2 = do("dve", lambda e, sb_=sb_, nm=nm: e.tensor_reduce(nm[:, 1:2], PS[:, sb_, P:384], AX.X, ALU.max))
            t3 = do("dve", lambda e, nm=nm: e.tensor_scalar(nm, nm, -0.125, None, ALU.mult), t1, t2)
            t_e = []
            for t_, (o, w) in enumerate(((0, P), (P, S))):
                t_e.append(do("act", lambda e, t_=t_, o=o, w=w, sb_=sb_, p_=p_, nm=nm, den=den: e.activation(
                    p_[:, o:o + w], PS[:, sb_, o:o + w], ACT.Exp, bias=nm[:, t_:t_ + 1], scale=0.125,
                    accum_out=den[:, t_:t_ + 1]), t3, last_turn[turn]))
            work_bank_free[sb_] = t_e
            t_r = do("dve", lambda e, den=den: e.reciprocal(den, den), t_e)
            wait("pe", t_e, work_bank_free[pb_])
            for o in range(3):
                fn = lambda e, o=o, p_=p_, pb_=pb_: e.transpose(
                    PS[:, pb_, o * P:(o + 1) * P], p_[:, o * P:(o + 1) * P], ident[:, :])
                t_t = do("pe", fn) if o == 2 else quiet("pe", fn)
            t_c = do("act", lambda e, pt_=pt_, pb_=pb_: e.activation(pt_, PS[:, pb_, 0:384], ACT.Copy), t_t)
            work_bank_free[pb_] = [t_c]
            wait("pe", t_c, work_bank_free[7])
            vh = slice(h * HD, h * HD + HD)
            quiet("pe", lambda e, pt_=pt_, vh=vh: e.matmul(PS[:, 7, 0:HD], pt_[:, 0:P], z_v[:, 0, vh],
                                                           start=True, stop=True))
            quiet("pe", lambda e, pt_=pt_, vh=vh: e.matmul(PS[:, 7, HD:2 * HD], pt_[:, P:2 * P], z_v[:, 0, vh],
                                                           start=True, stop=False))
            t_o = do("pe", lambda e, pt_=pt_, vh=vh: e.matmul(PS[:, 7, HD:2 * HD], pt_[:, 2 * P:3 * P],
                                                              z_v[:, 1, vh], start=False, stop=True))
            fr = [do("dve", lambda e, t_=t_, den=den, vh=vh: e.tensor_scalar(
                cat[:, t_, vh], PS[:, 7, t_ * HD:(t_ + 1) * HD], den[:, t_:t_ + 1], None, ALU.mult), t_o, t_r)
                for t_ in range(TB)]
            work_bank_free[7] = fr
            last_turn[turn] = [t_o, t_c, t_t]
        def norm_part(c0, w, junk, after):
            ssq, t = sum_squares(lambda t_: cat[:, t_, c0:c0 + w], junk, after)
            rstd = col(2)
            t = rstd_of(ssq, rstd, w, EPS, 2, t)
            return [do("dve", lambda e, t_=t_: e.tensor_scalar(
                cat[:, t_, c0:c0 + w], cat[:, t_, c0:c0 + w], rstd[:, t_:t_ + 1], None, ALU.mult), t)
                for t_ in range(TB)]
        t_a = norm_part(0, A_W, lambda t_: sd(t_ * 4096, A_W), prog.all_done())

        SW, SWT, SG, SBIAS, SNG = 0, 1024, 2048, 4096, 4112
        fence = prog.all_done()
        dma("sp", sd(SW, B_G, P), I["sgu_w"][0].rearrange("g i j -> i g j"), "sgu_in", fence, t_a)
        dma("sp", sd(SBIAS, B_G), I["sgu_b_t"], "sgu_in")
        t_sg = dma("sp", sd(SNG, B_W), bcast("sgu_norm_gain", 0, B_W), "sgu_in")
        act_b = sd(SG, TB, 2 * B_W)
        t = do("act", lambda e: e.activation(act_b, z_b, ACT.Gelu_apprx_tanh), fence, t_a)
        mean, var = col(2), col(2)
        t1 = [do("dve", lambda e, t_=t_: e.tensor_reduce(mean[:, t_:t_ + 1], act_b[:, t_, B_W:], AX.X, ALU.add), t)
              for t_ in range(TB)]
        t1 = do("dve", lambda e: e.tensor_scalar(mean, mean, 1.0 / B_W, None, ALU.mult), t1)
        t1 = [do("dve", lambda e, t_=t_: e.tensor_scalar(act_b[:, t_, B_W:], act_b[:, t_, B_W:],
                                                         mean[:, t_:t_ + 1], None, ALU.subtract), t1)
              for t_ in range(TB)]
        ssq, t1 = sum_squares(lambda t_: act_b[:, t_, B_W:], lambda t_: z_b[:, t_, 0:B_W], t1)
        t1 = rstd_of(ssq, var, B_W, EPS, 2, t1)
        t1 = [do("dve", lambda e, t_=t_: e.scalar_tensor_tensor(
            out=act_b[:, t_, B_W:], in0=act_b[:, t_, B_W:], scalar=var[:, t_:t_ + 1], in1=sd(SNG, B_W),
            op0=ALU.mult, op1=ALU.mult), t1, t_sg) for t_ in range(TB)]
        wt = sd(SWT, B_G, P)
        t_w = []
        for n in range(2):
            b = next_bank()
            wait("pe", t_sg, work_bank_free[b])
            for g in range(4):
                fn = lambda e, g=g, n=n, b=b: e.transpose(PS[:, b, g * P:(g + 1) * P], sd(SW, B_G, P)[:, 4 * n + g, :],
                                                          ident[:, :])
                t = do("pe", fn) if g == 3 else quiet("pe", fn)
            t = do("act", lambda e, n=n, b=b: e.activation(
                wt[:, 4 * n:4 * n + 4, :].rearrange("p g i -> p (g i)"), PS[:, b, :], ACT.Copy), t)
            work_bank_free[b] = [t]
            t_w.append(do("pool", lambda e, n=n: e.affine_select(
                out=wt[:, 4 * n:4 * n + 4, :], in_=wt[:, 4 * n:4 * n + 4, :], compare_op=ALU.is_ge, fill=0.0,
                base=0, pattern=[[0, 4], [1, P]], channel_multiplier=-1), t))
        t_b = []
        for t_ in range(TB):
            b = next_bank()
            wait("pe", t_w, t1, work_bank_free[b])
            for g in range(B_G):
                fn = lambda e, g=g, t_=t_, b=b: e.matmul(
                    PS[:, b, g * HD:(g + 1) * HD], wt[:, g, :], act_b[:, t_, B_W + g * HD:B_W + (g + 1) * HD],
                    start=True, stop=True)
                t = do("pe", fn) if g == B_G - 1 else quiet("pe", fn)
            u = lambda a, n: a.rearrange("p (g n) -> p g n", g=n)
            t = do("dve", lambda e, t_=t_, b=b: e.tensor_tensor(
                u(cat[:, t_, A_W:A_W + B_W], B_G), u(PS[:, b, :], B_G),
                sd(SBIAS, B_G).unsqueeze(2).to_broadcast([P, B_G, HD]), ALU.add), t)
            work_bank_free[b] = [t]
            t_b.append(do("dve", lambda e, t_=t_: e.tensor_tensor(
                cat[:, t_, A_W:A_W + B_W], cat[:, t_, A_W:A_W + B_W], act_b[:, t_, 0:B_W], ALU.mult), t))
        t_b = norm_part(A_W, B_W, lambda t_: z_b[:, t_, 0:B_W], t_b)

        fence = prog.all_done()
        wait("sp", fence)
        LORA, GUP = 18176, 18944
        MASKS, VT, YT = 0, 1796, 3332
        LE = 21056
        dma("sp", arena[0:HD, LORA:LORA + C_W], I["rwkv_w_up"][0], "lora_in")
        dma("sp", arena[HD:P, LORA:LORA + C_W], I["rwkv_a_up"][0], "lora_in")
        dma("sp", ar(GUP, 2, C_W), I["rwkv_g_up"][0].rearrange("(k p) n -> p k n", p=P), "lora_in")
        dma("sp", ar(MASKS, 1282), I["masks"], "lora_in")
        t_lora = dma("sp", arena[:, 1284:1796].bitcast(I32), I["pair_mask"], "lora_in")
        level_mask = lambda l: ar(MASKS + P * l, P)
        level0_t = ar(MASKS + 7 * P, P)
        head_sum = ar(MASKS + 8 * P, P)
        head_two = ar(MASKS + 9 * P, 2)
        pair_mask = arena[:, 1284:1796].bitcast(I32)
        all_ones = ar(MASKS + 9 * P + 2, P)
        zc = ar(Z_C, 21, S)
        diff = sd(0, 21, S)
        t1 = do("dve", lambda e: e.tensor_tensor(diff[:, :, 1:], zc[:, :, :S - 1], zc[:, :, 1:], ALU.subtract), fence)
        t2 = do("dve", lambda e: e.tensor_scalar(diff[:, :, 0:1], zc[:, :, 0:1], -1.0, None, ALU.mult))
        t_mix = [do("dve", lambda e, k=k: e.scalar_tensor_tensor(
            out=zc[:, k, :], in0=diff[:, k, :], scalar=par("mu", k), in1=zc[:, k, :], op0=ALU.mult, op1=ALU.add),
            t1, t2) for k in range(21)][-1]
        vt, yt = ar(VT, TB, C_W), ar(YT, TB, C_W)
        t_v = []
        for n in range(CB // 2):
            b = next_bank()
            wait("pe", t_mix, work_bank_free[b])
            for k in range(2):
                for t_ in range(TB):
                    fn = lambda e, k=k, t_=t_, n=n, b=b: e.transpose(
                        PS[:, b, (t_ * 2 + k) * P:(t_ * 2 + k + 1) * P],
                        zc[:, 12 + 2 * n + k, t_ * P:(t_ + 1) * P], ident[:, :])
                    t = do("pe", fn) if k and t_ else quiet("pe", fn)
            t = do("act", lambda e, n=n, b=b: e.activation(
                vt[:, :, 2 * n * P:(2 * n + 2) * P], PS[:, b, :].rearrange("p (t n) -> p t n", t=TB), ACT.Copy), t)
            work_bank_free[b] = [t]
            t_v.append(t)
        t_tanh = do("act", lambda e: e.activation(zc[0:HD, 18, :], zc[0:HD, 18, :], ACT.Tanh), t_mix)
        t_sig = do("act", lambda e: e.activation(zc[:, 19:21, :], zc[:, 19:21, :], ACT.Sigmoid), t_mix)
        one_minus_ka, bonus = col(CB), col(2 * C_H)
        t_ka = do("dve", lambda e: e.tensor_scalar(one_minus_ka, params[:, PARAM_AT["k_a"]:PARAM_AT["k_a"] + CB],
                                                   -1.0, 1.0, ALU.mult, ALU.add), fence)
        bonus3 = bonus.rearrange("p (t h) -> p t h", t=TB)
        RATE = math.exp(-0.5)
        sets = [dict(mats=sd(0, 4, 4, P), kk=sd(2048, S), a=sd(2304, S), bt=sd(2560, S), r=sd(2816, 2, P),
                     sa=sd(3072, 2, P), s1=sd(3328, HD), X=sd(3392, 4, P), XT=sd(3904, 4, P), U=sd(4416, 4, P),
                     banks=(4, 5), L=ar(LE, S), E=ar(LE + S, S)),
                dict(mats=sd(4928, 4, 4, P), kk=sd(6976, S), a=sd(7232, S), bt=sd(7488, S),
                     r=ar(20480, 2, P), sa=ar(20736, 2, P), s1=sd(7744, HD), X=ar(4868, 4, P), XT=ar(5380, 4, P),
                     U=ar(5892, 4, P), banks=(6, 7), L=ar(LE + 2 * S, S), E=ar(LE + 3 * S, S))]
        fence = prog.all_done()
        for st in sets:
            st["zeroed"] = do("pool", lambda e, m=st["mats"]: e.memset(m, 0.0), fence)
            st["free"] = []
        bc4 = lambda m: m.unsqueeze(1).to_broadcast([P, 4, P])
        cols2 = {}

        def rwkv_block(b, st):
            A, B = st["banks"]
            mats, X, XT, U, kk, a, L, E = (st[n] for n in ("mats", "X", "XT", "U", "kk", "a", "L", "E"))
            bt, R, SA, S1 = st["bt"], st["r"], st["sa"], st["s1"]
            r, k = zc[:, b, :], zc[:, CB + b, :]
            u0, u1 = U[:, 0:2, :].rearrange("p i t -> p (i t)"), U[:, 2:4, :].rearrange("p i t -> p (i t)")
            bs = slice(b * P, (b + 1) * P)
            free = st["free"]
            t = do("pe", lambda e: e.matmul(PS[:, A, 0:S], arena[0:HD, LORA + b * P:LORA + (b + 1) * P],
                                           zc[0:HD, 18, :], start=True, stop=True), t_lora, t_tanh, free)
            t = do("pe", lambda e: e.matmul(PS[:, A, S:2 * S], arena[HD:P, LORA + b * P:LORA + (b + 1) * P],
                                            zc[HD:P, 18, :], start=True, stop=True), t)
            t_s = do("act", lambda e: e.activation(E, PS[:, A, 0:S], ACT.Sigmoid, bias=par("w0", b)), t, free)
            t_a_ = do("act", lambda e: e.activation(a, PS[:, A, S:2 * S], ACT.Sigmoid, bias=par("a0", b)))
            yield
            t_l = [do("dve", lambda e, c=c: e.tensor_tensor_scan(
                L[:, c * P:(c + 1) * P], all_ones, E[:, c * P:(c + 1) * P], 0.0, ALU.mult, ALU.add), t_s)
                for c in range(TB)]
            t_k = do("dve", lambda e: e.tensor_scalar(kk, k, par("k_k", b), None, ALU.mult))
            t = do("act", lambda e: e.activation(u0, kk, ACT.Square), t_k)
            t = do("pe", lambda e: e.matmul(PS[:, B, 0:S], head_sum, u0, start=True, stop=True), t)
            yield
            t_k1 = do("dve", lambda e: e.tensor_scalar(u1, a, par("k_a", b), one_minus_ka[:, b:b + 1], ALU.mult,
                                                       ALU.add), t_a_, t_ka)
            t_k1 = do("dve", lambda e: e.tensor_tensor(k, k, u1, ALU.mult), t_k1)
            t = do("dve", lambda e: e.tensor_scalar(u1, PS[:, B, 0:S], 1e-24, None, ALU.max), t, t_k1)
            t = do("dve", lambda e: e.reciprocal(u1, u1), t)
            t = do("act", lambda e: e.activation(u1, u1, ACT.Sqrt), t)
            yield
            t_kk = do("dve", lambda e: e.tensor_tensor(kk, kk, u1, ALU.mult), t)
            t = do("dve", lambda e: e.scalar_tensor_tensor(out=u0, in0=r, scalar=par("r_k", b), in1=k,
                                                           op0=ALU.mult, op1=ALU.mult), t_k1)
            for t_ in range(TB):
                fn = lambda e, t_=t_: e.matmul(PS[:, B, S + 2 * t_:S + 2 * t_ + 2], u0[:, t_ * P:(t_ + 1) * P],
                                               head_two, start=True, stop=True)
                t = do("pe", fn, t)
            t_bo = do("dve", lambda e: e.tensor_copy(
                bonus3[:, :, 2 * b:2 * b + 2], PS[:, B, S:S + 4].rearrange("p (t h) -> p t h", t=TB)), t)
            t_b_ = do("dve", lambda e: e.tensor_tensor(a, a, kk, ALU.mult), t_kk)
            if st["banks"] not in cols2:
                cols2[st["banks"]] = (col(2), col(2), col(1))
            plus, minus, end = cols2[st["banks"]]
            mid = L.rearrange("p (c t) -> p c t", c=TB)[:, :, 63]
            t1 = do("dve", lambda e: e.tensor_scalar(plus, mid, RATE, None, ALU.mult), t_l, free)
            t2 = do("dve", lambda e: e.tensor_scalar(minus, mid, -RATE, None, ALU.mult))
            t3 = do("dve", lambda e: e.tensor_scalar(end, L[:, P - 1:P], -RATE, plus[:, 0:1], ALU.mult, ALU.add), t1)
            t3 = do("dve", lambda e: e.tensor_tensor(end, end, minus[:, 1:2], ALU.add), t3, t2)
            t_end = do("act", lambda e: e.activation(end, end, ACT.Exp), t3)
            t_f = [do("act", lambda e, c=c: e.activation(E[:, c * P:(c + 1) * P], L[:, c * P:(c + 1) * P], ACT.Exp,
                                                         scale=RATE, bias=minus[:, c:c + 1]), t1, t2)
                   for c in range(TB)]
            t_g = [do("act", lambda e, c=c: e.activation(u1[:, c * P:(c + 1) * P], L[:, c * P:(c + 1) * P], ACT.Exp,
                                                         scale=-RATE, bias=plus[:, c:c + 1]), t_kk)
                   for c in range(TB)]
            yield
            t_be = do("dve", lambda e: e.tensor_tensor(a, a, E, ALU.mult), t_f, t_b_)
            t_ka_ = do("dve", lambda e: e.tensor_tensor(k, k, E, ALU.mult), t)
            t_rh = do("dve", lambda e: e.tensor_tensor(r, r, u1, ALU.mult), t_g, t)
            t_g = [do("act", lambda e, c=c: e.activation(
                u0[:, c * P + 1:(c + 1) * P], L[:, c * P:(c + 1) * P - 1], ACT.Exp, scale=-RATE,
                bias=plus[:, c:c + 1]), t) for c in range(TB)]
            t_g += [do("act", lambda e: e.activation(u0.rearrange("p (c t) -> p c t", c=TB)[:, :, 0], plus, ACT.Exp))]
            t_al = do("dve", lambda e: e.tensor_tensor(kk, kk, u0, ALU.mult), t_g)
            yield
            t_m, bank_read = [], {A: [t_s, t_a_], B: [t_bo]}
            for i in range(4):
                c, h = i // 2, i % 2
                rows, cs, bank = slice(HD * h, HD * h + HD), slice(c * P, c * P + P), (A, B)[h]
                wait("pe", t_be, t_ka_, t_rh, t_al, bank_read[bank])
                for n, (l, rr) in enumerate(((a, kk), (a, r), (k, kk), (k, r))):
                    fn = lambda e, n=n, l=l, rr=rr, rows=rows, cs=cs, bank=bank: e.matmul(
                        PS[:, bank, n * P:(n + 1) * P], l[rows, cs], rr[rows, cs], start=True, stop=True)
                    t = do("pe", fn) if n == 3 else quiet("pe", fn)
                t = do("dve", lambda e, i=i, bank=bank: e.copy_predicated(
                    mats[:, i, :, :].rearrange("p m t -> p (m t)"), pair_mask, PS[:, bank, :]), t, st["zeroed"],
                    t_lora, free)
                bank_read[bank] = [t]
                t_m.append(t)
            yield
            quiet("pe", lambda e: e.transpose(PS[:, B, 0:P], a[:, 0:P], ident[:, :]), t_m)
            t = do("pe", lambda e: e.transpose(PS[:, B, P:2 * P], k[:, 0:P], ident[:, :]))
            t_bt = do("act", lambda e: e.activation(bt, PS[:, B, 0:2 * P], ACT.Copy), t, free)
            for i in range(4):
                fn = lambda e, i=i: e.transpose(PS[:, A, i * P:(i + 1) * P], mats[:, i, 0, :], ident[:, :])
                t = do("pe", fn) if i == 3 else quiet("pe", fn)
            psA = PS[:, A, :].rearrange("p (i t) -> p i t", i=4)
            psB = PS[:, B, :].rearrange("p (i t) -> p i t", i=4)
            t = do("dve", lambda e: e.tensor_tensor(X, psA, bc4(level_mask(0)), ALU.mult), t, t_al, free)
            t_x_ = do("dve", lambda e: e.tensor_tensor(X, X, bc4(ident[:, :]), ALU.add), t)
            t = do("dve", lambda e: e.tensor_tensor(XT, mats[:, :, 0, :], bc4(level0_t), ALU.mult))
            t_xt = do("dve", lambda e: e.tensor_tensor(XT, XT, bc4(ident[:, :]), ALU.add), t)
            t_b_read = [t_bt]
            yield
            for l in range(1, 7):
                for i in range(4):
                    fn = lambda e, i=i: e.matmul(psA[:, i, :], mats[:, i, 0, :], X[:, i, :], start=True, stop=True)
                    if i == 0:
                        wait("pe", t_x_, t_xt)
                    t = do("pe", fn) if i == 3 else quiet("pe", fn)
                yield
                t_u = do("dve", lambda e, l=l: e.tensor_tensor(U, psA, bc4(level_mask(l)), ALU.mult), t, t_al)
                wait("pe", t_u, t_b_read)
                for i in range(4):
                    fn = lambda e, i=i: e.matmul(psA[:, i, :], U[:, i, :], XT[:, i, :], start=True, stop=True)
                    t = do("pe", fn) if i == 3 else quiet("pe", fn)
                if l < 6:
                    for i in range(4):
                        fn = lambda e, i=i: e.matmul(psB[:, i, :], XT[:, i, :], U[:, i, :], start=True, stop=True)
                        t2 = do("pe", fn) if i == 3 else quiet("pe", fn)
                yield
                if l < 6:
                    t_x_ = do("dve", lambda e: e.tensor_tensor(X, X, psB, ALU.add), t2)
                    t_b_read = [t_x_]
                t_xt = do("dve", lambda e: e.tensor_tensor(XT, XT, psA, ALU.add), t, t2 if l < 6 else None)
            def solve(c, t_state):
                for h in range(2):
                    i, hs = 2 * c + h, slice(b * P + h * HD, b * P + (h + 1) * HD)
                    last = c == 0
                    fn = lambda e, i=i, hs=hs, h=h, last=last: e.matmul(
                        PS[:, B, h * HD:(h + 1) * HD], mats[:, i, 2, :], vt[:, c, hs], start=True, stop=last)
                    if h == 0:
                        wait("pe", t_v, t_b_read, t_state)
                    t = do("pe", fn, t if h else None)
                    if c == 1:
                        rows = slice(HD * h, HD * h + HD)
                        t = do("pe", lambda e, h=h, rows=rows: e.matmul(
                            PS[:, B, h * HD:(h + 1) * HD], kk[rows, P:2 * P], S1[rows, :], start=False, stop=True), t)
                t = do("act", lambda e: e.activation(R[:, c, :], PS[:, B, 0:P], ACT.Copy, scale=-1.0), t, free)
                for h in range(2):
                    fn = lambda e, h=h: e.matmul(PS[:, A, h * HD:(h + 1) * HD], XT[:, 2 * c + h, :],
                                                 R[:, c, h * HD:(h + 1) * HD], start=True, stop=True)
                    t = do("pe", fn, t, t_xt)
                return do("dve", lambda e: e.tensor_copy(SA[:, c, :], PS[:, A, 0:P]), t, free)

            t_sa0 = solve(0, [])
            yield
            quiet("pe", lambda e: e.matmul(PS[:, B, 0:P], bt[:, 0:P], SA[:, 0, :], start=True, stop=False),
                  t_sa0, t_bt)
            t = do("pe", lambda e: e.matmul(PS[:, B, 0:P], bt[:, P:2 * P], vt[:, 0, bs], start=False, stop=True))
            t_st = [do("act", lambda e, h=h: e.activation(
                S1[HD * h:HD * h + HD, :], PS[HD * h:HD * h + HD, B, HD * h:HD * h + HD], ACT.Copy,
                scale=end[HD * h:HD * h + HD, :]), t, t_end) for h in range(2)]
            yield
            t_sa1 = solve(1, t_st)
            yield
            wait("pe", t_sa1)
            for i in range(4):
                c, h = i // 2, i % 2
                rows, hs, o = slice(HD * h, HD * h + HD), slice(h * HD, (h + 1) * HD), PS[:, B, i * HD:(i + 1) * HD]
                vs = slice(b * P + h * HD, b * P + (h + 1) * HD)
                t = do("pe", lambda e, i=i, c=c, hs=hs, o=o: e.matmul(o, mats[:, i, 1, :], SA[:, c, hs], start=True,
                                                                  stop=False), t if i == 3 else None)
                t = do("pe", lambda e, i=i, c=c, vs=vs, o=o: e.matmul(o, mats[:, i, 3, :], vt[:, c, vs],
                                                                      start=False, stop=c == 0))
                if c:
                    t = do("pe", lambda e, rows=rows, o=o: e.matmul(o, r[rows, P:2 * P], S1[rows, :],
                                                                    start=False, stop=True), t)
            t = do("act", lambda e: e.activation(yt[:, :, bs], PS[:, B, 0:2 * P].rearrange(
                "p (c n) -> p c n", c=TB), ACT.Copy), t)
            st["free"] = [t, t_sa1, t_end]
            yield

        for pair in range(0, CB, 2):
            steps = [rwkv_block(pair, sets[0]), rwkv_block(pair + 1, sets[1])]
            while steps:
                steps = [s for s in steps if next(s, "end") != "end"]

        def fence_banks():
            f = prog.all_done()
            for b in work_bank_free:
                work_bank_free[b] = list(f)
            return f

        fence = fence_banks()
        LNG, LNB = 1536, 2304
        dma("sp", sd(LNG, C_W), bcast("rwkv_ln_gain", 0, C_W), "ln_in", fence)
        t_ln = dma("sp", sd(LNB, C_W), bcast("rwkv_ln_bias", 0, C_W), "ln_in")
        NH = TB * C_H
        y3, v3, tmp3 = ar(YT, NH, HD), ar(VT, NH, HD), sd(0, NH, HD)
        over = lambda c: c.unsqueeze(2).to_broadcast([P, NH, HD])
        y_mean, y_var = col(NH), col(NH)
        t = do("dve", lambda e: e.tensor_reduce(y_mean, y3, AX.X, ALU.add), fence)
        t = do("dve", lambda e: e.tensor_scalar(y_mean, y_mean, 1.0 / HD, None, ALU.mult), t)
        t_y = do("dve", lambda e: e.tensor_tensor(y3, y3, over(y_mean), ALU.subtract), t)
        t = do("act", lambda e: e.activation(tmp3, y3, ACT.Square), t_y)
        t = do("dve", lambda e: e.tensor_reduce(y_var, tmp3, AX.X, ALU.add), t)
        t = rstd_of(y_var, y_var, HD, GN_EPS, NH, t)
        t = do("dve", lambda e: e.tensor_tensor(y3, y3, over(y_var), ALU.mult), t)
        yv, tmpv = ar(YT, TB, C_W), sd(0, TB, C_W)
        rep = lambda a: sd(a, C_W).unsqueeze(1).to_broadcast([P, TB, C_W])
        t = do("dve", lambda e: e.tensor_tensor(yv, yv, rep(LNG), ALU.mult), t, t_ln)
        t = do("dve", lambda e: e.tensor_tensor(yv, yv, rep(LNB), ALU.add), t)
        t2 = do("dve", lambda e: e.tensor_tensor(tmp3, v3, over(bonus), ALU.mult))
        t = do("dve", lambda e: e.tensor_tensor(yv, yv, tmpv, ALU.add), t, t2)
        gup = ar(GUP, 2, C_W)
        HC = C_W // 2
        wait("pe", fence)
        for t_ in range(TB):
            for n in range(2):
                for k in range(2):
                    fn = lambda e, t_=t_, n=n, k=k: e.matmul(
                        PS[:, 4 + 2 * t_ + n, 0:HC], zc[:, 19 + k, t_ * P:(t_ + 1) * P],
                        gup[:, k, n * HC:(n + 1) * HC], start=k == 0, stop=k == 1)
                    t_g = do("pe", fn) if k else quiet("pe", fn)
        for t_ in range(TB):
            for n in range(2):
                t_c = do("dve", lambda e, t_=t_, n=n: e.tensor_tensor(
                    cat[:, t_, A_W + B_W + n * HC:A_W + B_W + (n + 1) * HC], yv[:, t_, n * HC:(n + 1) * HC],
                    PS[:, 4 + 2 * t_ + n, 0:HC], ALU.mult), t, t_g)
        fence = fence_banks()

        t_gain = dma("sp", gains, bcast("sandwich_gains", 1 * D, D), "gains_in", fence)
        def mix_gain(k):
            return par("attn_gain", k) if k < 6 else par("sgu_gain", k - 6) if k < 10 else 1.0
        t_h = to_h(cat, mix_gain, [fence])
        y = ar(0, TB, D)
        t_y = products("w_out", w_cols(I["w_out"][0], 0), 4, *to_tokens(y, 0), tok_cols=(0, 512), after=t_h,
                       evac_after=t_h)
        t_xn = add_normed(lambda t: y[:, t, :], gains, lambda t: cat[:, t, :], [t_y, t_gain])

        def attend(n, pairs, scale, v, put, bias=None, sink=None, after=()):
            last_turn = [[], []]
            for h in range(n):
                turn = h % 2
                bank = 4 + turn
                s_, p_, pt_ = sd(512 * turn, 512), sd(1024 + 512 * turn, 512), sd(2048 + 512 * turn, 512)
                if h < 2:
                    stat[turn] = (col(2), col(2), col(2)) if stat[turn] is None else stat[turn]
                nm, den, ex = stat[turn]
                wait("pe", after, last_turn[turn], work_bank_free[bank])
                ops = pairs(h)
                for t_ in range(TB):
                    for m, (q, k) in enumerate(ops):
                        fn = lambda e, t_=t_, q=q, k=k, m=m, bank=bank, z=len(ops): e.matmul(
                            PS[:, bank, t_ * S:(t_ + 1) * S], q[:, t_ * P:(t_ + 1) * P], k, start=m == 0,
                            stop=m == z - 1)
                        t_s = do("pe", fn)
                src = PS[:, bank, :]
                if bias:
                    dist, slope = bias(h)
                    t_s = do("dve", lambda e, dist=dist, slope=slope, s_=s_, src=src: e.scalar_tensor_tensor(
                        out=s_, in0=dist, scalar=slope, in1=src, op0=ALU.mult, op1=ALU.add), t_s, last_turn[turn])
                    src = s_
                    work_bank_free[bank] = [t_s]
                t = do("dve", lambda e, src=src, nm=nm: e.tensor_reduce(
                    nm, src.rearrange("p (t k) -> p t k", t=TB), AX.X, ALU.max), t_s, last_turn[turn])
                if sink:
                    t = do("dve", lambda e, nm=nm, h=h: e.tensor_scalar(nm, nm, scale, sink(h), ALU.mult, ALU.max), t)
                    t_m = do("dve", lambda e, nm=nm: e.tensor_scalar(nm, nm, -1.0, None, ALU.mult), t)
                else:
                    t_m = do("dve", lambda e, nm=nm: e.tensor_scalar(nm, nm, -scale, None, ALU.mult), t)
                t_e = [do("act", lambda e, t_=t_, src=src, p_=p_, nm=nm, den=den: e.activation(
                    p_[:, t_ * S:(t_ + 1) * S], src[:, t_ * S:(t_ + 1) * S], ACT.Exp, bias=nm[:, t_:t_ + 1],
                    scale=scale, accum_out=den[:, t_:t_ + 1]), t_m, last_turn[turn]) for t_ in range(TB)]
                if not bias:
                    work_bank_free[bank] = t_e
                t_r = t_e
                if sink:
                    t = do("act", lambda e, nm=nm, ex=ex, h=h: e.activation(ex, nm, ACT.Exp, bias=sink(h)), t_m)
                    t_r = do("dve", lambda e, den=den, ex=ex: e.tensor_tensor(den, den, ex, ALU.add), t, t_e)
                t_r = do("dve", lambda e, den=den: e.reciprocal(den, den), t_r)
                wait("pe", t_e, work_bank_free[6])
                for kb in range(TB):
                    for t_ in range(TB):
                        fn = lambda e, kb=kb, t_=t_, p_=p_: e.transpose(
                            PS[:, 6, (kb * TB + t_) * P:(kb * TB + t_ + 1) * P],
                            p_[:, t_ * S + kb * P:t_ * S + (kb + 1) * P], ident[:, :])
                        t_t = do("pe", fn) if kb and t_ else quiet("pe", fn)
                t_c = do("act", lambda e, pt_=pt_: e.activation(pt_, PS[:, 6, :], ACT.Copy), t_t)
                work_bank_free[6] = [t_c]
                wait("pe", t_c, work_bank_free[7])
                vv = v(h)
                for t_ in range(TB):
                    for kb in range(TB):
                        fn = lambda e, kb=kb, t_=t_, pt_=pt_, vv=vv: e.matmul(
                            PS[:, 7, t_ * P:(t_ + 1) * P], pt_[:, (kb * TB + t_) * P:(kb * TB + t_ + 1) * P],
                            vv[:, kb, :], start=kb == 0, stop=kb == TB - 1)
                        t_o = do("pe", fn) if kb and t_ else quiet("pe", fn)
                work_bank_free[7] = [put(h, t_, PS[:, 7, t_ * P:(t_ + 1) * P], den[:, t_:t_ + 1], [t_o, t_r])
                                     for t_ in range(TB)]
                last_turn[turn] = [t_o, t_t, t_c, work_bank_free[7]]
            return fence_banks()

        stat = [None, None]

        def put_in(dst):
            return lambda h, t_, ps, rden, after: do("dve", lambda e: e.tensor_scalar(
                dst[:, t_, h * P:(h + 1) * P], ps, rden, None, ALU.mult), after)

        t_h = norm_to_h(x, cat, lambda k: par("g_mem", k), [t_xn, t_y])
        t_q = products("mem_q", w_cols(I["mem_wq"][0], 0), 1, *to_channels(Z_C, 0), ch_cols=(0, 512), after=t_h,
                       evac_after=t_h)
        k_mem, q_mem, o_mem = ar(K_MEM, M_H, S), ar(Z_C, M_H, S), ar(Z_C + 1024, TB, M_I)
        t_gain = dma("sp", gains, bcast("sandwich_gains", 3 * D, D), "gains_in", t_xn)
        fence = attend(M_H, lambda h: [(q_mem[:, h, :], k_mem[:, h, :])], M_D ** -0.5,
                       lambda h: v_mem[:, :, h * P:(h + 1) * P], put_in(o_mem), after=[t_q, fence_banks()])
        t_h = to_h(o_mem, None, [fence], n_blocks=M_H)
        wo = I["mem_wo"][0].rearrange("(k p) n -> p k n", p=P)
        t_y = products("mem_o", lambda g, j: wo[:, :, g * 512:(g + 1) * 512], 4, *to_tokens(y, 0),
                       tok_cols=(0, 512), units=1, after=t_h, evac_after=t_h)
        t_xn = add_normed(lambda t: y[:, t, :], gains, lambda t: cat[:, t, :], [t_y, t_gain])

        t_h = norm_to_h(x, cat, lambda k: par("g_ffn", k), [t_xn, t_y])
        act_ff = ar(0, FB * S)
        CONV = 16128
        conv = ar(CONV, 2, 4, S)
        ff = {n: ctx.enter_context(nc.semaphore(n)) for n in ("taps", "gelu_made", "gated")}
        GATED_CREDIT = 2
        prog.queue["dve"].append(lambda e, i: e.sem_inc(ff["gated"], GATED_CREDIT))
        G0 = state["group"]

        def channel(name, g, half, c, j=0):
            at_ = PARAM_AT[name] + (j * 2 + half) * FB + c
            return params[:, bass.ds(g * 2 + at_, 1)]

        def up_act(e, g, parity):
            e.wait_ge(ff["gated"], g + 1)
            for m in range(4):
                half, c = m // 2, m % 2
                last = e.activation(conv[:, parity, m, :], PS[:, 2 * parity + half, c * S:(c + 1) * S], ACT.Identity,
                                    scale=channel("conv_w", g, half, c, 2), bias=channel("conv_b", g, half, c))
            return last

        def up_dve(e, g, parity):
            e.wait_ge(sem["act_evac"], EVAC_CREDIT + G0 + g + 1)
            for back in (1, 2):
                if back == 2:
                    e.wait_ge(ff["taps"], g + 1)
                for m in range(4):
                    half, c = m // 2, m % 2
                    d = conv[:, parity, m, back:]
                    last = e.scalar_tensor_tensor(out=d, in0=PS[:, 2 * parity + half, c * S:(c + 1) * S - back],
                                                  scalar=channel("conv_w", g, half, c, 2 - back), in1=d,
                                                  op0=ALU.mult, op1=ALU.add)
                if back == 1:
                    last.then_inc(ff["taps"], 1)
            return last

        def gate_act(e, g, parity):
            e.wait_ge(sem["dve_evac"], EVAC_CREDIT + G0 + g + 1)
            e.activation(conv[:, parity, 0:2, :], conv[:, parity, 0:2, :], ACT.Gelu_apprx_tanh)\
             .then_inc(ff["gelu_made"], 1)

        def gate_dve(e, g, parity):
            e.wait_ge(ff["gelu_made"], g + 1)
            flat2 = lambda a: a.rearrange("p c n -> p (c n)")
            e.tensor_tensor(act_ff[:, bass.ds(g * (2 * S), 2 * S)], flat2(conv[:, parity, 0:2, :]),
                            flat2(conv[:, parity, 2:4, :]), ALU.mult).then_inc(ff["gated"], 1)

        w_up = I["ffn_w_up"][0].rearrange("(k p) n -> p k n", p=P)
        t_u = products("ffn_up", lambda g, j: tuple(w_up[:, 4 * j:4 * j + 4, bass.ds(g * S + a, S)]
                                                    for a in (0, D_FF)), FB // 2,
                       up_act, up_dve, ch_cols=(0, 512), after=t_h, evac_after=t_h,
                       finish={"act": gate_act, "dve": gate_dve}, halves=True)
        t_gated = (ff["gated"], GATED_CREDIT + FB // 2)
        t_gain = dma("sp", gains, bcast("sandwich_gains", 5 * D, D), "gains_in", t_xn)

        w_down = I["ffn_w_down"][0].rearrange("(k p) n -> p k n", p=P)
        U0 = state["unit"]
        state["unit"] += FB

        def down(q, quad, U, first, final):
            def sp(e):
                for j in range(4):
                    load_unit(e, U + j, j, (1, 2048), w_down[:, bass.ds(q * 4 + j, 1), :])

            def rows(j):
                return act_ff[:, bass.ds(q * (4 * S) + j * S, S)]

            def act(e):
                for j in range(4):
                    e.wait_ge(sem["unit_used"], U + j + 1)
                    e.activation(h_hi[:, j % 2, :], rows(j), ACT.Copy).then_inc(ff_hi, 1)
                    split_hi(e, U + j, quad, j, 2048)

            def dve(e):
                for j in range(4):
                    e.wait_ge(ff_hi, q * 4 + j + 1)
                    e.tensor_tensor(h_lo[:, j % 2, :], rows(j), h_hi[:, j % 2, :].bitcast(F32), ALU.subtract)\
                     .then_inc(ff_lo, 1)
                    split_lo(e, U + j, j, 2048)

            def pe(e):
                for j in range(4):
                    s = j % 2
                    e.wait_ge(ff_lo, q * 4 + j + 1)
                    e.wait_ge(sem["lo_made"], LO_CREDIT + U + j + 1)
                    for t in range(TB):
                        for n in range(4):
                            ws = slice(n * 512, (n + 1) * 512)
                            last = three_pass(e, PS[:, 4 * t + n, :], h_hi[:, s, t * P:(t + 1) * P],
                                              h_lo[:, s, t * P:(t + 1) * P], w_hi[:, s, ws], w_lo[:, s, ws],
                                              first and j == 0, final and j == 3)
                    last.then_inc(sem["unit_used"], 1)
            return {"sp": sp, "act": act, "dve": dve, "pe": pe}

        ff_hi, ff_lo = (ctx.enter_context(nc.semaphore(n)) for n in ("ff_hi", "ff_lo"))
        fence = fence_banks()
        wait("act", t_u, t_gated)
        wait("dve", t_u, t_gated)
        wait("pe", t_u, fence)
        NQ = FB // 4
        for q, rolled in ((0, False), (1, True), (NQ - 1, False)):
            for en in ("sp", "act", "dve", "pe"):
                if rolled:
                    prog.loop(NQ - 2, {en: lambda e, i, en=en: down(i + 1, i + (U0 // 4 + 1), i * 4 + (U0 + 4),
                                                                    False, False)[en](e)})
                else:
                    prog.once(0, {en: lambda e, i, en=en, q=q: down(q, U0 // 4 + q, U0 + 4 * q, q == 0,
                                                                    q == NQ - 1)[en](e)})
        t_y = [(sem["unit_used"], UNIT_CREDIT + state["unit"])]
        t_xn = add_normed(lambda t: PS[:, 4 * t:4 * t + 4, :].rearrange("p b n -> p (b n)"), gains,
                          lambda t: cat[:, t, :], [t_y, t_gain], psum=True)
        fence = fence_banks()

        ZT, ZTOK = 0, 4608
        NT_COLS = 3520
        zt2, ztok = ar(ZT, 18, S), ar(ZTOK, TB, NT_COLS)
        W_UQ, W_UKV, DIST, DISTM = 16128, 18432, 20480, 20992
        SINK, LAM, SUBLN, TRIG, INV, POS = 21504, 21512, 21768, 21896, 22024, 22056
        w_uq, w_ukv = ar(W_UQ, 3, 768), ar(W_UKV, 2, 1024)
        dist, dist_far = ar(DIST, TB * S), ar(DISTM, TB * S)
        pos_i = arena[:, POS:POS + S + TB].bitcast(I32)
        dma("sp", pos_i[:, 0:S], bcast("positions_2", 0, S), "pos_in", fence)
        for t_ in range(TB):
            dma("sp", pos_i[:, S + t_:S + t_ + 1], bass.AP(I["positions_2"].tensor, t_ * P, [[1, P], [1, 1]]),
                "pos_in")
        t_pos = dma("sp", ar(INV, L2_HALF), bcast("inv_freq", 0, L2_HALF), "pos_in")
        d_i = arena[:, DISTM:DISTM + TB * S].bitcast(I32)
        t = [do("pool", lambda e, t_=t_: e.tensor_tensor(
            d_i[:, t_ * S:(t_ + 1) * S], pos_i[:, 0:S], pos_i[:, S + t_:S + t_ + 1].to_broadcast([P, S]),
            ALU.subtract), t_pos, fence) for t_ in range(TB)]
        t = do("dve", lambda e: e.tensor_copy(dist, d_i), t)
        t = do("act", lambda e: e.activation(dist, dist, ACT.Abs), t)
        t = do("dve", lambda e: e.tensor_scalar(dist_far, dist, float(P), BIG, ALU.is_gt, ALU.mult), t)
        t_dist = do("dve", lambda e: e.tensor_tensor(dist_far, dist_far, dist, ALU.add), t)
        pos_f = col(TB)
        trig = ar(TRIG, 2, TB, L2_HALF)
        k_i = arena[:, POS:POS + 128].bitcast(I32)
        k_f = arena[:, POS + 128:POS + 256]
        t1 = do("dve", lambda e: e.tensor_copy(pos_f, pos_i[:, S:S + TB]), t_pos)
        t1 = [do("dve", lambda e, t_=t_: e.tensor_scalar(trig[:, 0, t_, :], ar(INV, L2_HALF), pos_f[:, t_:t_ + 1],
                                                         None, ALU.mult), t1) for t_ in range(TB)]
        tr = ar(TRIG, 128)
        t1 = do("dve", lambda e: e.tensor_scalar(trig[:, 1, :, :], trig[:, 0, :, :], math.pi / 2, None, ALU.add), t1)
        t2 = do("dve", lambda e: e.tensor_scalar(k_f, tr, 1 / (2 * math.pi), None, ALU.mult), t1, t_dist)
        t2 = do("dve", lambda e: e.tensor_copy(k_i, k_f), t2)
        t2 = do("dve", lambda e: e.tensor_copy(k_f, k_i), t2)
        C1, C2 = 6.28125, 2 * math.pi - 6.28125
        for cst in (C1, C2):
            t2 = do("dve", lambda e, cst=cst: e.scalar_tensor_tensor(out=tr, in0=k_f, scalar=-cst, in1=tr,
                                                                     op0=ALU.mult, op1=ALU.add), t2)
        for cmp_, lim, turn_ in ((ALU.is_gt, math.pi, -2 * math.pi), (ALU.is_lt, -math.pi, 2 * math.pi)):
            t2 = do("dve", lambda e, c=cmp_, l=lim, u=turn_: e.tensor_scalar(k_f, tr, l, u, c, ALU.mult), t2)
            t2 = do("dve", lambda e: e.tensor_tensor(tr, tr, k_f, ALU.add), t2)
        t2 = do("dve", lambda e: e.tensor_scalar(tr, tr, 3.1415925, -3.1415925, ALU.min, ALU.max), t2)
        t_trig = do("act", lambda e: e.activation(tr, tr, ACT.Sin), t2)

        AV, AG, CQ, CKV, KR, BG, CV, CG = 0, 256, 1280, 1664, 1920, 1984, 2496, 3008
        MQ, MK, MV, QRT, KRT, CQT, CKVT = 3072, 4096, 5120, 6144, 6656, 6912, 7680
        slopes = lambda n: [2.0 ** (-8.0 * (i + 1) / n) for i in range(n)]

        t_prev = [t_xn]
        def second_layer(layer, t_prev):
            lam_init = 0.8 - 0.6 * math.exp(-0.3 * layer)
            fence = fence_banks()
            dma("sp", w_uq, I["mla_w_uq_2"][layer].rearrange("(k p) n -> p k n", p=P), "small_in", fence)
            dma("sp", w_ukv, I["mla_w_ukv_2"][layer].rearrange("(k p) n -> p k n", p=P), "small_in")
            dma("sp", ar(SINK, 8), bcast("swa_sink_2", 8 * layer, 8), "small_in")
            dma("sp", ar(SUBLN, P), bcast("diff_subln_2", P * layer, P), "small_in")
            t_small = dma("sp", ar(LAM, S), bcast("diff_lambda_2", S * layer, S), "small_in")
            t_h = norm_to_h(x, cat, lambda k: par(f"g_l{layer}", k), [t_prev, fence])
            w = I["w_in_2"][layer]
            products("q", w_cols(w, 0), 2, *to_channels(ZT, 0), ch_cols=(0, 512), after=t_h, evac_after=t_h)
            products("kv", w_cols(w, 1024), 1,
                     lambda e, g, bank: e.activation(ar(ZT + 8 * S, 512), bank, ACT.Copy),
                     lambda e, g, bank: e.tensor_copy(ztok[:, :, AV:AV + 256],
                                                      bank.rearrange("p (t n) -> p t n", t=TB)),
                     tok_cols=(256, 256), ch_cols=(0, 256))
            products("tok", w_cols(w, 1536), 4, *to_tokens(ztok, AG), tok_cols=(0, 512))
            products("tok_end", w_cols(w, 3584, n_cols=192), 1,
                     *evac_pair(lambda g: ztok[:, 0, AG + 2048:AG + 2240], lambda g: ztok[:, 1, AG + 2048:AG + 2240]),
                     tok_cols=(0, 192), n_cols=192)
            products("c_qk", w_cols(w, 3776), 2, *to_channels(ZT, 10), ch_cols=(0, 512))
            t_z = products("c_vg", w_cols(w, 4800), 2, *to_tokens(ztok, CV), tok_cols=(0, 512))
            fence = fence_banks()

            SC = P ** -0.5
            attend(8, lambda h: [(zt2[:, h, :], zt2[:, 8 + h // 4, :])], SC,
                   lambda h: ztok[:, :, AV + (h // 4) * P:AV + (h // 4 + 1) * P], put_in(cat),
                   bias=lambda h: (dist_far, -slopes(8)[h] / SC), sink=lambda h: ar(SINK, 8)[:, h:h + 1],
                   after=[t_z, t_small, t_dist, fence])

            cq_t, ckv_t = sd(CQT, 3, S), sd(CKVT, 2, S)
            t_ct = []
            for c0, nb, gname, dst in ((CQ, 3, "q_norm", cq_t), (CKV, 2, "kv_norm", ckv_t)):
                wd = nb * P
                ssq, t = sum_squares(lambda t_, c0=c0, wd=wd: ztok[:, t_, c0:c0 + wd],
                                     lambda t_, wd=wd: sd(2048 + t_ * 512, wd),
                                     prog.all_done())
                rstd = col(2)
                t = rstd_of(ssq, rstd, wd, EPS, 2, t)
                t = [do("dve", lambda e, t_=t_, c0=c0, wd=wd, rstd=rstd: e.tensor_scalar(
                    ztok[:, t_, c0:c0 + wd], ztok[:, t_, c0:c0 + wd], rstd[:, t_:t_ + 1], None, ALU.mult), t)
                    for t_ in range(TB)]
                for k in range(nb):
                    b = next_bank()
                    wait("pe", t, work_bank_free[b])
                    for t_ in range(TB):
                        fn = lambda e, t_=t_, k=k, b=b, c0=c0: e.transpose(
                            PS[:, b, t_ * P:(t_ + 1) * P], ztok[:, t_, c0 + k * P:c0 + (k + 1) * P], ident[:, :])
                        t_t = do("pe", fn) if t_ else quiet("pe", fn)
                    gk = par(gname, layer * nb + k)
                    tt = do("act", lambda e, k=k, b=b, dst=dst, gk=gk: e.activation(dst[:, k, :], PS[:, b, 0:S],
                                                                                    ACT.Copy, scale=gk), t_t)
                    work_bank_free[b] = [tt]
                    t_ct.append(tt)
            QR, ROT, TMP = 0, 640, 1408
            qr, rot = sd(QR, TB, 5, 64), sd(ROT, TB, 6, 64)
            b = next_bank()
            uq4 = w_uq.rearrange("p k (h n) -> p k h n", h=4)
            wait("pe", t_ct, work_bank_free[b])
            for t_ in range(TB):
                for k in range(3):
                    fn = lambda e, t_=t_, k=k, b=b: e.matmul(
                        PS[:, b, t_ * S:(t_ + 1) * S], cq_t[:, k, t_ * P:(t_ + 1) * P], uq4[:, k, :, P:P + 64],
                        start=k == 0, stop=k == 2)
                    t = do("pe", fn) if k == 2 else quiet("pe", fn)
            f = prog.all_done()
            t = do("act", lambda e, b=b: e.activation(qr[:, :, 0:4, :].rearrange("p t h n -> p t (h n)"),
                                                      PS[:, b, :].rearrange("p (t n) -> p t n", t=TB), ACT.Copy), t, f)
            work_bank_free[b] = [t]
            t_kr = do("dve", lambda e: e.tensor_copy(qr[:, :, 4, :], ztok[:, :, KR:KR + 64]), f)
            t_rot = []
            for t_ in range(TB):
                sin, cos = (trig[:, m, t_, :].unsqueeze(1).to_broadcast([P, 5, L2_HALF]) for m in (0, 1))
                x1, x2 = qr[:, t_, :, 0:L2_HALF], qr[:, t_, :, L2_HALF:]
                ta, tb_ = sd(TMP, 5, L2_HALF), sd(TMP + 160, 5, L2_HALF)
                for o, m1, m2, op in ((0, cos, sin, ALU.subtract), (L2_HALF, sin, cos, ALU.add)):
                    a1 = do("dve", lambda e, x1=x1, m1=m1, ta=ta: e.tensor_tensor(ta, x1, m1, ALU.mult), t, t_kr, t_trig,
                            t_rot[-1:])
                    a2 = do("dve", lambda e, x2=x2, m2=m2, tb_=tb_: e.tensor_tensor(tb_, x2, m2, ALU.mult))
                    a3 = do("dve", lambda e, t_=t_, o=o, op=op, ta=ta, tb_=tb_: e.tensor_tensor(
                        rot[:, t_, 0:5, o:o + L2_HALF], ta, tb_, op), a1, a2)
                    t_rot.append(a3)
            t_rot = do("dve", lambda e: e.tensor_copy(rot[:, :, 5, :], rot[:, :, 4, :]), t_rot)
            for blk in range(3):
                b = next_bank()
                wait("pe", t_rot, work_bank_free[b])
                for t_ in range(TB):
                    fn = lambda e, t_=t_, blk=blk, b=b: e.transpose(
                        PS[:, b, t_ * P:(t_ + 1) * P], rot[:, t_, 2 * blk:2 * blk + 2, :].rearrange("p a n -> p (a n)"),
                        ident[:, :])
                    t = do("pe", fn) if t_ else quiet("pe", fn)
                t = do("act", lambda e, blk=blk, b=b: e.activation(sd(QRT + blk * S, S), PS[:, b, 0:S], ACT.Copy), t)
                work_bank_free[b] = [t]
            for dst, wsrc, n_k, src, stride in ((MQ, w_uq, 3, cq_t, 192), (MK, w_ukv, 2, ckv_t, 256)):
                for hp in range(2):
                    b = next_bank()
                    wait("pe", t_ct, work_bank_free[b])
                    for hh in range(2):
                        for k in range(n_k):
                            h = 2 * hp + hh
                            fn = lambda e, hh=hh, h=h, k=k, b=b, wsrc=wsrc, src=src, stride=stride, n_k=n_k: e.matmul(
                                PS[:, b, hh * S:(hh + 1) * S], wsrc[:, k, h * stride:h * stride + P], src[:, k, :],
                                start=k == 0, stop=k == n_k - 1)
                            t = do("pe", fn) if hh and k == n_k - 1 else quiet("pe", fn)
                    t = do("act", lambda e, b=b, dst=dst, hp=hp: e.activation(sd(dst + hp * 512, 512), PS[:, b, :],
                                                                              ACT.Copy), t)
                    work_bank_free[b] = [t]
            ukv4 = w_ukv.rearrange("p k (h n) -> p k h n", h=4)
            for t_ in range(TB):
                b = next_bank()
                wait("pe", work_bank_free[b])
                for k in range(2):
                    fn = lambda e, t_=t_, k=k, b=b: e.matmul(PS[:, b, :], ckv_t[:, k, t_ * P:(t_ + 1) * P],
                                                             ukv4[:, k, :, P:2 * P], start=k == 0, stop=k == 1)
                    t = do("pe", fn) if k else quiet("pe", fn)
                t = do("dve", lambda e, t_=t_, b=b: e.tensor_copy(sd(MV + 512 * t_, 512), PS[:, b, :]), t)
                work_bank_free[b] = [t]
            fence = fence_banks()
            mq, mk, mv, qrt, krt = sd(MQ, 4, S), sd(MK, 4, S), sd(MV, TB, 512), sd(QRT, 2, S), sd(KRT, S)
            half = lambda h: slice(64 * (h % 2), 64 * (h % 2) + 64)
            attend(4, lambda h: [(mq[:, h, :], mk[:, h, :]), (qrt[half(h), h // 2, :], krt[half(h), :])],
                   (P + 64) ** -0.5, lambda h: mv[:, :, h * P:(h + 1) * P], put_in(cat[:, :, 1024:1536]),
                   after=[fence])

            lam = ar(LAM, 4, 64)
            e2, neg_lam = col(2), col(1)
            t = do("dve", lambda e: e.tensor_tensor(lam[:, 0, :], lam[:, 0, :], lam[:, 1, :], ALU.mult), t_small)
            t = do("dve", lambda e: e.tensor_tensor(lam[:, 1, :], lam[:, 2, :], lam[:, 3, :], ALU.mult), t)
            t = do("dve", lambda e, e2=e2: e.tensor_reduce(e2, lam[:, 0:2, :], AX.X, ALU.add), t)
            t = do("act", lambda e, e2=e2: e.activation(e2, e2, ACT.Exp), t)
            t_lam = do("dve", lambda e, e2=e2, neg_lam=neg_lam: e.tensor_scalar(
                neg_lam, e2[:, 1:2], e2[:, 0:1], -lam_init, ALU.subtract, ALU.add), t)
            t_sub = do("dve", lambda e: e.tensor_scalar(ar(SUBLN, P), ar(SUBLN, P), 1.0 - lam_init, None, ALU.mult),
                       t_small)

            def put_diff(j, t_, ps, rden, after):
                h, second = j // 2, j % 2
                d = cat[:, t_, 1536 + h * P:1536 + (h + 1) * P]
                if not second:
                    return do("dve", lambda e: e.tensor_scalar(d, ps, rden, None, ALU.mult), after)
                t = do("dve", lambda e: e.tensor_tensor(rden, rden, neg_lam, ALU.mult), after, t_lam)
                return do("dve", lambda e: e.scalar_tensor_tensor(out=d, in0=ps, scalar=rden, in1=d, op0=ALU.mult,
                                                                  op1=ALU.add), t)
            DSC = 64 ** -0.5
            half2 = lambda j: slice(64 * (j % 2), 64 * (j % 2) + 64)
            fence = attend(8, lambda j: [(zt2[half2(j), 10 + j // 2, :], zt2[half2(j), 14 + j // 2, :])], DSC,
                           lambda j: ztok[:, :, CV + (j // 2) * P:CV + (j // 2 + 1) * P], put_diff,
                           bias=lambda j: (dist, -slopes(4)[j // 2] / DSC), after=[fence_banks()])
            NV = TB * 4
            ssq, sq = col(NV), sd(0, TB, 512)
            yc = cat[:, :, 1536:2048]
            h4 = lambda a: a.rearrange("p t (h n) -> p t h n", h=4)
            t = do("act", lambda e: e.activation(sq, yc, ACT.Square), fence)
            t = do("dve", lambda e, ssq=ssq: e.tensor_reduce(ssq, sd(0, NV, P), AX.X, ALU.add), t)
            t = rstd_of(ssq, ssq, P, EPS, NV, t)
            t_n = []
            for t_ in range(TB):
                v4 = cat[:, t_, 1536:2048].rearrange("p (h n) -> p h n", h=4)
                a = do("dve", lambda e, t_=t_, v4=v4, ssq=ssq: e.tensor_tensor(
                    v4, v4, ssq[:, 4 * t_:4 * t_ + 4].unsqueeze(2).to_broadcast([P, 4, P]), ALU.mult), t)
                t_n.append(do("dve", lambda e, v4=v4: e.tensor_tensor(
                    v4, v4, ar(SUBLN, P).unsqueeze(1).to_broadcast([P, 4, P]), ALU.mult), a, t_sub))
            t_g = []
            for g0, w0_, c0 in ((AG, 1024, 0), (BG, 512, 1024), (CG, 512, 1536)):
                g_ = ztok[:, :, g0:g0 + w0_]
                t = do("act", lambda e, g_=g_: e.activation(g_, g_, ACT.Silu), fence)
                t_g.append(do("dve", lambda e, g_=g_, c0=c0, w0_=w0_: e.tensor_tensor(
                    cat[:, :, c0:c0 + w0_], cat[:, :, c0:c0 + w0_], g_, ALU.mult), t, t_n))
            t_h = to_h(cat, None, [t_g, fence_banks()])

            y2 = ar(0, D)

            def add_rows(e, g, bank):
                xs = x[:, 1, bass.ds(g * 512, 512)]
                return e.tensor_tensor(xs, xs, bank, ALU.add)
            t_y = products("w_out_2", w_cols(I["w_out_2"][layer], 0), 4,
                           evac_pair(lambda g: y2[:, bass.ds(g * 512, 512)], None)[0], add_rows,
                           tok_cols=(0, 512), after=t_h, evac_after=[t_h, prog.all_done()])
            return [do("dve", lambda e: e.tensor_tensor(x[:, 0, :], x[:, 0, :], y2, ALU.add), t_y), t_y]

        for layer in range(LAYERS):
            t_prev = second_layer(layer, t_prev)

        FG = 4096
        t_fg = dma("sp", ar(FG, D), bcast("final_norm_2", 0, D), "final_in",
                   prog.all_done(), t_prev)
        ssq, t = sum_squares(lambda t: x[:, t, :], lambda t: cat[:, t, :], t_prev)
        rstd = col(2)
        t = rstd_of(ssq, rstd, D, EPS, 2, t)
        for t_ in range(TB):
            t1 = do("dve", lambda e, t_=t_: e.scalar_tensor_tensor(
                out=cat[:, t_, :], in0=x[:, t_, :], scalar=rstd[:, t_:t_ + 1], in1=ar(FG, D), op0=ALU.mult,
                op1=ALU.mult), t, t_fg)
            t_out = dma("sp" if t_ else "act", out[0, t_ * P:(t_ + 1) * P, :], cat[:, t_, :], "out_done", t1)
        for en in ("sp", "act"):
            wait(en, t_out)

        block = ctx.enter_context(nc.Block())
        for name, deco in (("sp", block.sync), ("pe", block.tensor), ("act", block.scalar),
                           ("dve", block.vector), ("pool", block.gpsimd)):
            def run(e, name=name):
                for f in prog.queue[name]:
                    f(e, 0)
            deco(run)


_DIRECT = ["x", "mem", "rel_bias_table", "sandwich_gains", "w_in", "w_out", "sgu_norm_gain", "sgu_w",
           "rwkv_w_up", "rwkv_a_up", "rwkv_g_up", "rwkv_ln_gain", "rwkv_ln_bias", "mem_wq", "mem_wkv", "mem_wo",
           "ffn_w_up", "ffn_w_down", "positions_2", "w_in_2", "swa_sink_2", "mla_w_uq_2", "mla_w_ukv_2",
           "diff_lambda_2", "diff_subln_2", "w_out_2", "final_norm_2"]


def constants():
    c = {"ident": np.eye(P, dtype=np.float32), "exch": np.eye(P, dtype=np.float32)[::-1].copy()}
    dist = 255 - np.arange(384)
    count = ((dist >= 0) & (dist <= 128)) * 1 + ((dist >= 0) & (dist % 4 == 0)) + ((dist >= 0) & (dist % 16 == 0))
    exact = REL // 2
    d = np.maximum(dist, 0)
    scaled = np.log(np.maximum(d, 1) / exact) / np.log(2048 / exact)
    large = np.minimum(exact + (scaled * (REL - exact)).astype(np.int32), REL - 1)
    bucket = np.where(d < exact, d, large)
    onehot = np.zeros((REL + 1, 384), np.float32)
    seen = count > 0
    onehot[bucket[seen], np.nonzero(seen)[0]] = 8.0
    onehot[REL] = np.where(seen, 8.0 * np.log(np.maximum(count, 1)), 8.0 * NEG)
    c["onehot"] = onehot
    t, s = np.arange(P)[:, None], np.arange(P)[None, :]
    masks = np.zeros((P, 1282), np.float32)
    for l in range(7):
        m = (t // (2 << l) == s // (2 << l)) & ((t >> l) % 2 == 1) & ((s >> l) % 2 == 0)
        masks[:, P * l:P * (l + 1)] = -1.0 * m
        if l == 0:
            masks[:, 7 * P:8 * P] = -1.0 * m.T
    masks[:, 8 * P:9 * P] = t // HD == s // HD
    masks[:, 9 * P] = np.arange(P) < HD
    masks[:, 9 * P + 1] = np.arange(P) >= HD
    masks[:, 9 * P + 2:9 * P + 2 + P] = 1.0
    c["masks"] = masks
    strict, incl = t < s, t <= s
    c["pair_mask"] = np.concatenate([strict, incl, strict, incl], axis=1).astype(np.int32)
    c["inv_freq"] = (np.float32(10000.0) ** (-np.arange(0, 64, 2, dtype=np.float32) / np.float32(64)))\
        .astype(np.float32)[None, :]
    return c


def kernel(**inputs):
    import concourse.bacc as _bacc
    from concourse.bass_utils import run_bass_kernel_spmd as _run

    a = {n: np.asarray(v) for n, v in inputs.items()}
    g = a["sandwich_gains"][0]
    parts = [g[0], g[2], g[4], a["mem_src_gain"], a["norm_g_2"][0], a["norm_g_2"][1], a["rwkv_mu"], a["rwkv_w0"],
             a["rwkv_a0"], a["rwkv_k_k"], a["rwkv_k_a"], a["rwkv_r_k"], a["attn_out_gain"], a["sgu_out_gain"],
             a["ffn_conv_b"], a["ffn_conv_w"], a["mla_q_norm_2"], a["mla_kv_norm_2"]]
    laid = {n: a[n] for n in _DIRECT}
    laid["params"] = np.ascontiguousarray(np.concatenate([p.reshape(-1, P) for p in parts]).T)
    laid["sgu_b_t"] = np.ascontiguousarray(a["sgu_b"][0].T)
    laid.update(constants())
    nc = _bacc.Bacc("TRN2", target_bir_lowering=False, num_devices=1)
    arrays, aps = {}, {}
    for name, v in laid.items():
        v = np.ascontiguousarray(v)
        arrays[f"in_{name}"] = v
        aps[name] = nc.dram_tensor(f"in_{name}", v.shape, mybir.dt.from_np(v.dtype), kind="ExternalInput").ap()
    aps["scratch"] = nc.dram_tensor("bias_rows", (A_H, 384), F32, kind="Internal").ap()
    out = nc.dram_tensor("out_0", (1, S, D), F32, kind="ExternalOutput").ap()
    hybrid_two_blocks(nc, aps, out)
    r = _run(nc, [arrays], core_ids=[0])
    return r.results[0]["out_0"]
```

```python
from contextlib import ExitStack
import math

import numpy as np
import concourse.bass as bass
from concourse import mybir

F32 = mybir.dt.float32
F32R = mybir.dt.float32r
I32 = mybir.dt.int32
ALU = mybir.AluOpType
ACT = mybir.ActivationFunctionType
AX = mybir.AxisListType

P = 128
S = 256
TB = S // P
D = 2048
KB = D // P
HD = 64
A_H, B_G, C_H = 12, 8, 12
A_W, B_W, C_W = A_H * HD, B_G * HD, C_H * HD
CB = C_W // P
M_H, M_D = 4, 128
M_I = M_H * M_D
D_FF = 5632
FB = D_FF // P
REL = 32
EPS, GN_EPS = 1e-6, 64e-5
NEG = -1e30
BIG = 1e30
LAYERS = 2
Z_COLS = 3 * A_W + 2 * B_W + 3 * C_W + 384
W2_COLS = 5824
L2_HALF = 32

PARAM_BLOCKS = [("g_mix", 16), ("g_mem", 16), ("g_ffn", 16), ("g_src", 16), ("g_l0", 16), ("g_l1", 16),
                ("mu", 21), ("w0", 6), ("a0", 6), ("k_k", 6), ("k_a", 6), ("r_k", 6), ("attn_gain", 6),
                ("sgu_gain", 4), ("conv_b", 88), ("conv_w", 264), ("q_norm", 6), ("kv_norm", 4)]
PARAM_AT, _n = {}, 0
for _name, _w in PARAM_BLOCKS:
    PARAM_AT[_name] = _n
    _n += _w
N_PARAM = _n


class Program:

    ENGINES = ("pe", "act", "dve", "pool", "sp")

    def __init__(self, nc, ctx):
        self.queue = {e: [] for e in self.ENGINES}
        self.done = {e: ctx.enter_context(nc.semaphore(f"done_{e}")) for e in self.ENGINES}
        self.count = dict.fromkeys(self.ENGINES, 0)
        self.dma_sems = {}
        self.nc, self.ctx = nc, ctx

    def wait(self, engine, *after):
        for token in flat(after):
            self.queue[engine].append(lambda e, i, t=token: e.wait_ge(t[0], t[1]))

    def do(self, engine, fn, *after):
        self.wait(engine, *after)
        self.count[engine] += 1
        self.queue[engine].append(lambda e, i: fn(e).then_inc(self.done[engine], 1))
        return (self.done[engine], self.count[engine])

    def quiet(self, engine, fn, *after):
        self.wait(engine, *after)
        self.queue[engine].append(lambda e, i: fn(e))

    def dma(self, engine, out, in_, name, *after):
        if name not in self.dma_sems:
            self.dma_sems[name] = [self.ctx.enter_context(self.nc.semaphore(name)), 0]
        entry = self.dma_sems[name]
        entry[1] += 16
        self.wait(engine, *after)
        self.queue[engine].append(lambda e, i: e.dma_start(out, in_).then_inc(entry[0], 16))
        return (entry[0], entry[1])

    def all_done(self):
        return [(self.done[e], self.count[e]) for e in self.ENGINES if self.count[e]]

    def loop(self, n, bodies):
        for engine, body in bodies.items():
            def run(e, _i, body=body):
                with e.Fori(0, n) as i:
                    body(e, i)
            self.queue[engine].append(run)

    def once(self, i, bodies):
        for engine, body in bodies.items():
            self.queue[engine].append(lambda e, _i, body=body: body(e, i))


def flat(x):
    for t in x:
        if t is None:
            continue
        if isinstance(t, tuple) and len(t) == 2 and isinstance(t[1], int):
            yield t
        else:
            yield from flat(t)


def hybrid_two_blocks(nc, I, out):
    with ExitStack() as ctx:
        def sb(name, shape, dt=F32):
            return ctx.enter_context(nc.sbuf_tensor(name, shape, dt))

        prog = Program(nc, ctx)
        do, quiet, dma, wait = prog.do, prog.quiet, prog.dma, prog.wait

        base = -(-nc.sbuf_base // 32) * 32
        h_hi = sb("h_hi", [P, KB, S], F32R)
        h_lo = sb("h_lo", [P, KB, S], F32R)
        side = nc.alloc_sbuf_tensor_at("side", [P, 2 * KB * S], F32, offset=base)
        raw = sb("raw", [P, 4, 2048])
        w_hi = sb("w_hi", [P, 2, 2048], F32R)
        w_lo = sb("w_lo", [P, 2, 2048], F32R)
        spare = nc.alloc_sbuf_tensor_at("spare", [P, 8192], F32, offset=base + 4 * (2 * KB * S + 8192))
        x = sb("x", [P, TB, D])
        ARENA = 22400
        arena = sb("arena", [P, ARENA])
        params = sb("params", [P, N_PARAM])
        ident = sb("ident", [P, P])
        exch = sb("exch", [P, P])
        small = sb("small", [P, 512])
        PS = ctx.enter_context(nc.psum_tensor("PS", [P, 8, 512], F32))

        def view(t, at, dims):
            n = int(np.prod(dims))
            v = t[:, at:at + n]
            if len(dims) == 1:
                return v
            names = "abcd"[:len(dims)]
            return v.rearrange(f"p ({' '.join(names)}) -> p {' '.join(names)}",
                               **{c: d for c, d in zip(names[1:], dims[1:])})

        def sp_(at, *dims):
            return view(spare, at, dims)

        def ar(at, *dims):
            return view(arena, at, dims)

        def sd(at, *dims):
            return view(side, at, dims)

        def par(name, k=0):
            return params[:, PARAM_AT[name] + k:PARAM_AT[name] + k + 1]

        def bcast(name, at, n):
            return bass.AP(I[name].tensor, at, [[0, P], [1, n]])

        small_at = [0]

        def col(n):
            a = small_at[0]
            small_at[0] += n
            assert small_at[0] <= 512
            return small[:, a:a + n]

        sem = {n: ctx.enter_context(nc.semaphore(n)) for n in
               ("landed0", "landed1", "landed2", "landed3", "hi_made", "lo_made", "unit_used",
                "act_evac", "dve_evac")}
        landed = [sem[f"landed{j}"] for j in range(4)]
        right_landed = [ctx.enter_context(nc.semaphore(f"right_landed{j}")) for j in range(4)]
        LO_CREDIT, UNIT_CREDIT, EVAC_CREDIT = 4, 2, 2
        state = {"unit": 0, "group": 0, "left": None}

        def load_unit(e, U, slot, dst_dims, src):
            e.wait_ge(sem["lo_made"], U + 1)
            dst = raw[:, slot, :dst_dims[0] * dst_dims[1]].rearrange("p (k n) -> p k n", k=dst_dims[0])
            if isinstance(src, tuple):
                half = dst_dims[1] // 2
                e.dma_start(dst[:, :, half:], src[1]).then_inc(right_landed[slot], 16)
                dst, src = dst[:, :, :half], src[0]
            e.dma_start(dst, src).then_inc(landed[slot], 16)

        def split_hi(e, U, quad, slot, n):
            e.wait_ge(landed[slot], quad * 16 + 16)
            e.wait_ge(sem["unit_used"], U + 1)
            e.activation(w_hi[:, slot % 2, :n], raw[:, slot, :n], ACT.Copy).then_inc(sem["hi_made"], 1)

        def split_lo(e, U, slot, n):
            e.wait_ge(sem["hi_made"], U + 1)
            e.tensor_tensor(w_lo[:, slot % 2, :n], raw[:, slot, :n],
                            w_hi[:, slot % 2, :n].bitcast(F32), ALU.subtract).then_inc(sem["lo_made"], 1)

        def three_pass(e, ps, l_hi, l_lo, r_hi, r_lo, start, stop, skip=False):
            e.matmul(ps, l_hi, r_hi, start=start, stop=False, skip_group_check=skip)
            e.matmul(ps, l_hi, r_lo, start=False, stop=False, skip_group_check=skip)
            return e.matmul(ps, l_lo, r_hi, start=False, stop=stop, skip_group_check=skip)

        def products(name, src, n_groups, evac_act, evac_dve, tok_cols=None, ch_cols=None, n_cols=512,
                     units=4, kb_per_unit=4, after=(), rolled=True, evac_after=(), finish=None, halves=False, more=False,
                     taken_before=False, fill=None):
            U0, G0 = state["unit"], state["group"]
            state["unit"] += units * n_groups
            state["group"] += n_groups
            n = kb_per_unit * n_cols
            before, state["left"] = state["left"], None
            wait("pe", *after)
            wait("act", *evac_after)
            wait("dve", *evac_after)

            def group(g, parity, U, quad, first_slot):
                bank = [2 * parity, 2 * parity + 1]

                def sp(e):
                    for j in range(units):
                        load_unit(e, U + j, (first_slot + j) % 4, (kb_per_unit, n_cols), src(g, j))

                def act(e, j):
                    if halves:
                        e.wait_ge(right_landed[j], g * 16 + 16)
                    split_hi(e, U + j, quad, (first_slot + j) % 4, n)

                def dve(e, j):
                    split_lo(e, U + j, (first_slot + j) % 4, n)

                def pe(e, js=range(units)):
                    if 0 in js:
                        e.wait_ge(sem["act_evac"], G0 + g + 1)
                        e.wait_ge(sem["dve_evac"], G0 + g + 1)
                    for j in js:
                        slot = (first_slot + j) % 2
                        e.wait_ge(sem["lo_made"], LO_CREDIT + U + j + 1)
                        wh = w_hi[:, slot, :n].rearrange("p (k n) -> p k n", k=kb_per_unit)
                        wl = w_lo[:, slot, :n].rearrange("p (k n) -> p k n", k=kb_per_unit)
                        last = None
                        if tok_cols:
                            c0, w = tok_cols
                            at_once = bool(ch_cols)
                            for t in range(TB):
                                for k in range(kb_per_unit):
                                    kk = j * kb_per_unit + k
                                    o = (PS[:, bank[1], t * w:(t + 1) * w] if at_once
                                         else PS[:, bank[t], :w])
                                    last = three_pass(
                                        e, o, h_hi[:, kk, t * P:(t + 1) * P], h_lo[:, kk, t * P:(t + 1) * P],
                                        wh[:, k, c0:c0 + w], wl[:, k, c0:c0 + w],
                                        kk == 0 and not (at_once and t), kk == units * kb_per_unit - 1,
                                        at_once)
                        if ch_cols:
                            c0, w = ch_cols
                            for c in range(w // P):
                                for k in range(kb_per_unit):
                                    kk = j * kb_per_unit + k
                                    o = PS[:, bank[c // 2], (c % 2) * S:(c % 2 + 1) * S]
                                    ws = slice(c0 + c * P, c0 + (c + 1) * P)
                                    last = three_pass(e, o, wh[:, k, ws], wl[:, k, ws], h_hi[:, kk, :],
                                                      h_lo[:, kk, :], kk == 0 and c % 2 == 0,
                                                      kk == units * kb_per_unit - 1, True)
                        last.then_inc(sem["unit_used"], 1)

                def evac(e, which):
                    e.wait_ge(sem["unit_used"], UNIT_CREDIT + U + units)
                    fn, b = (evac_act, 0) if which == "act" else (evac_dve, 1)
                    fn(e, g, parity if finish else PS[:, bank[b], :]).then_inc(sem[which + "_evac"], 1)

                def end(e, which):
                    if finish:
                        finish[which](e, g, parity)

                return {"sp": sp, "act": act, "dve": dve, "pe": pe, "evac": evac, "end": end}

            def at(g):
                U = U0 + units * g
                return group(g, (G0 + g) % 2, U, U // 4, U % 4)

            def splitter(which):
                def one(e, g, grp, prev):
                    for j in range(units):
                        grp[which](e, j)
                        if j == min(1, units - 1) and prev is not None:
                            prev["evac"](e, which)
                    if prev is not None:
                        prev["end"](e, which)
                return one

            if fill:
                assert not rolled and units > 1
                for g in range(n_groups):
                    grp, prev = at(g), at(g - 1) if g else before
                    prog.once(0, {"sp": lambda e, i, q=grp: q["sp"](e)})
                    for j in range(units):
                        prog.once(0, {"pe": lambda e, i, q=grp, j=j: q["pe"](e, (j,)),
                                      "act": lambda e, i, q=grp, j=j: q["act"](e, j),
                                      "dve": lambda e, i, q=grp, j=j: q["dve"](e, j)})
                        if j == 1 and prev is not None:
                            prog.once(0, {w: lambda e, i, w=w, q=prev: q["evac"](e, w) for w in ("act", "dve")})
                            assert not finish
                        next(fill, None)
                last_group = at(n_groups - 1)
            elif units == 1:
                for g in range(n_groups):
                    grp, prev = at(g), at(g - 1) if g else before
                    prog.once(0, {"sp": lambda e, i, q=grp: q["sp"](e), "pe": lambda e, i, q=grp: q["pe"](e),
                                  "act": lambda e, i, g=g, q=grp, p=prev: splitter("act")(e, g, q, p),
                                  "dve": lambda e, i, g=g, q=grp, p=prev: splitter("dve")(e, g, q, p)})
                last_group = at(n_groups - 1)
            else:
                for which in ("act", "dve"):
                    prog.once(0, {which: lambda e, i, w=which: splitter(w)(e, 0, at(0), before)})
                prog.once(0, {"sp": lambda e, i: at(0)["sp"](e), "pe": lambda e, i: at(0)["pe"](e)})
                pairs = (n_groups - 1) // 2 if rolled else 0
                if pairs < 2:
                    pairs = 0

                def body(engine):
                    def run(e, i):
                        for k in range(2):
                            g = i * 2 + (1 + k)
                            U = i * (2 * units) + (U0 + units * (1 + k))
                            quad = i * 2 + (U0 // 4 + 1 + k)
                            grp = group(g, (G0 + 1 + k) % 2, U, quad, U0 % 4)
                            if engine in ("act", "dve"):
                                Up = i * (2 * units) + (U0 + units * k)
                                gp = i * 2 + k
                                prev = group(gp, (G0 + k) % 2, Up, quad, U0 % 4)
                                splitter(engine)(e, g, grp, prev)
                            else:
                                grp[engine](e)
                    return run

                if pairs:
                    prog.loop(pairs, {en: body(en) for en in ("sp", "pe", "act", "dve")})
                for g in range(1 + 2 * pairs, n_groups):
                    grp, prev = at(g), at(g - 1)
                    prog.once(0, {"sp": lambda e, i, q=grp: q["sp"](e), "pe": lambda e, i, q=grp: q["pe"](e),
                                  "act": lambda e, i, g=g, q=grp, p=prev: splitter("act")(e, g, q, p),
                                  "dve": lambda e, i, g=g, q=grp, p=prev: splitter("dve")(e, g, q, p)})
                last_group = at(n_groups - 1)
            if more:
                state["left"] = last_group
            else:
                prog.once(0, {w: lambda e, i, w=w, q=last_group: (q["evac"](e, w), q["end"](e, w))
                              for w in ("act", "dve")})
            G1, U1 = (G0, U0) if taken_before else (state["group"], state["unit"])
            return [(sem["act_evac"], EVAC_CREDIT + G1), (sem["dve_evac"], EVAC_CREDIT + G1),
                    (sem["unit_used"], UNIT_CREDIT + U1)]

        def w_cols(w, col0, stride=512, n_cols=512):
            v = w.rearrange("(k p) n -> p k n", p=P)
            return lambda g, j: v[:, 4 * j:4 * j + 4, bass.ds(g * stride + col0, n_cols)]

        def evac_pair(dst_a, dst_b):
            def act(e, g, bank):
                d = dst_a(g)
                return e.activation(d, bank[:, :_n(d)], ACT.Copy)

            def dve(e, g, bank):
                d = dst_b(g)
                return e.tensor_copy(d, bank[:, :_n(d)])
            return act, dve

        def _n(ap):
            return int(np.prod(ap.shape[1:]))

        def to_tokens(dst, col0):
            return evac_pair(lambda g: dst[:, 0, bass.ds(g * 512 + col0, 512)],
                             lambda g: dst[:, 1, bass.ds(g * 512 + col0, 512)])

        def to_channels(at, blk0):
            return evac_pair(lambda g: arena[:, bass.ds(g * 1024 + (at + blk0 * S), 512)],
                             lambda g: arena[:, bass.ds(g * 1024 + (at + blk0 * S + 512), 512)])

        rs = {"n": 0}
        work_bank_free = {b: [] for b in (4, 5, 6, 7)}
        bank_turn = [0]

        def next_bank():
            b = 4 + bank_turn[0] % 4
            bank_turn[0] += 1
            return b

        def fence_banks():
            f = prog.all_done()
            for b in work_bank_free:
                work_bank_free[b] = list(f)
            return f

        lanes = [dict(bank=2 * n, tbank=2 * n + 1, s=sp_(1024 * n, 512), p=sp_(1024 * n + 512, 512),
                      stat=(col(2), col(2), col(2)), free=[]) for n in range(4)]

        def side_by_side(*jobs):
            while jobs:
                jobs = [job for job in jobs if next(job, "end") != "end"]
                yield

        def run_lanes(jobs, on=lanes):
            jobs = list(jobs)
            running = [(lane, None) for lane in on]
            while running:
                nxt = []
                for lane, job in running:
                    if job is None:
                        if not jobs:
                            continue
                        job = jobs.pop(0)(lane)
                    nxt.append((lane, None if next(job, "end") == "end" else job))
                running = nxt

        def rstd_of(ssq, out_col, width, eps, n, after):
            t = do("dve", lambda e: e.tensor_scalar(out_col, ssq, 1.0 / width, eps, ALU.mult, ALU.add), after)
            t = do("dve", lambda e: e.reciprocal(out_col, out_col), t)
            return do("act", lambda e: e.activation(out_col, out_col, ACT.Sqrt), t)

        def sum_squares(src, junk, after, psum=False):
            ssq = col(2)
            if psum:
                return ssq, [do("act", lambda e, t=t: e.activation(junk(t), src(t), ACT.Square,
                                                                   accum_out=ssq[:, t:t + 1]), after)
                             for t in range(TB)]
            a = do("act", lambda e: e.activation(junk(0), src(0), ACT.Square, accum_out=ssq[:, 0:1]), after)
            b = do("dve", lambda e: e.scalar_tensor_tensor(out=junk(1), in0=src(1), scalar=1.0, in1=src(1),
                                                           op0=ALU.mult, op1=ALU.mult,
                                                           accum_out=ssq[:, 1:2]), after)
            return ssq, [a, b]

        def to_h(src, gain, after, n_blocks=KB, dst=None):
            hi, lo = dst or (h_hi, h_lo)
            made = []
            for n in range((n_blocks + 1) // 2):
                b = next_bank()
                ks = [k for k in (2 * n, 2 * n + 1) if k < n_blocks]
                wait("pe", *after, *work_bank_free[b])
                for k in ks:
                    for t in range(TB):
                        fn = (lambda e, k=k, t=t, b=b: e.transpose(
                            PS[:, b, ((k % 2) * 2 + t) * P:((k % 2) * 2 + t + 1) * P],
                            src[:, t, k * P:(k + 1) * P], ident[:, :]))
                        tok = do("pe", fn) if (k, t) == (ks[-1], TB - 1) else quiet("pe", fn)
                free = []
                if gain is None:
                    m = len(ks) * S
                    dh = hi[:, ks[0]:ks[-1] + 1, :].rearrange("p k n -> p (k n)")
                    dl = lo[:, ks[0]:ks[-1] + 1, :].rearrange("p k n -> p (k n)")
                    a = do("act", lambda e, b=b, dh=dh, m=m: e.activation(dh, PS[:, b, :m], ACT.Copy), tok, after)
                    v = do("dve", lambda e, b=b, dh=dh, dl=dl, m=m: e.tensor_tensor(
                        dl, PS[:, b, :m], dh.bitcast(F32), ALU.subtract), a)
                    free, made = [a, v], made + [a, v]
                else:
                    half = {k: PS[:, b, (k % 2) * S:(k % 2 + 1) * S] for k in ks}
                    for k in ks:
                        a = do("act", lambda e, k=k, p=half[k]: e.activation(hi[:, k, :], p, ACT.Copy,
                                                                             scale=gain(k)), tok, after)
                    for k in ks:
                        v = do("dve", lambda e, k=k, p=half[k]: e.scalar_tensor_tensor(
                            out=lo[:, k, :], in0=p, scalar=gain(k), in1=hi[:, k, :].bitcast(F32),
                            op0=ALU.mult, op1=ALU.subtract), a)
                    free, made = [a, v], made + [a, v]
                work_bank_free[b] = free
            return [made[-1], made[-2]]

        def norm_to_h(src, scaled, gain, after):
            ssq, t = sum_squares(lambda t: src[:, t, :], lambda t: scaled[:, t, :], after)
            rstd = col(2)
            t = rstd_of(ssq, rstd, D, EPS, 2, t)
            out_t = []
            for tb in range(TB):
                out_t.append(do("dve", lambda e, tb=tb: e.tensor_scalar(
                    scaled[:, tb, :], src[:, tb, :], rstd[:, tb:tb + 1], None, ALU.mult), t))
            return to_h(scaled, gain, [out_t, after])

        def add_normed(y, g_bcast, junk, after, psum=False):
            ssq, t = sum_squares(y, junk, after, psum)
            rstd = col(2)
            t = rstd_of(ssq, rstd, D, EPS, 2, t)
            last = []
            for tb in range(TB):
                a = do("dve", lambda e, tb=tb: e.scalar_tensor_tensor(
                    out=junk(tb), in0=y(tb), scalar=rstd[:, tb:tb + 1], in1=g_bcast, op0=ALU.mult,
                    op1=ALU.mult), t)
                last.append(do("dve", lambda e, tb=tb: e.tensor_tensor(
                    x[:, tb, :], x[:, tb, :], junk(tb), ALU.add), a))
            return last

        Z_QK, Z_V, Z_B, Z_C = 0, 3072, 4608, 6656
        CAT = 12032
        K_MEM, V_MEM = 16128, 17152
        HANKEL = 18176
        GAINS = 20352
        cat = ar(CAT, TB, D)
        gains = ar(GAINS, D)

        t_mem = dma("act", ar(0, TB, D), I["mem"][0].rearrange("(t p) d -> p t d", p=P), "mem_in")
        wait("sp", t_mem)
        dma("act", params[:, :], I["params"], "consts")
        dma("act", ident[:, :], I["ident"], "consts")
        t_const = dma("act", exch[:, :], I["exch"], "consts")
        for engine, name, n in (("sp", "lo_made", LO_CREDIT), ("pe", "unit_used", UNIT_CREDIT),
                                ("act", "act_evac", EVAC_CREDIT), ("dve", "dve_evac", EVAC_CREDIT)):
            prog.queue[engine].append(lambda e, i, s=sem[name], n=n: e.sem_inc(s, n))

        TBL, ONEHOT, WROW = 21248, 21264, 21648
        t_one = do("dve", lambda e: e.memset(arena[32:33, TBL:TBL + A_H], 1.0))
        dma("act", arena[0:REL, TBL:TBL + A_H], I["rel_bias_table"], "rel_in")
        t_rel = dma("act", arena[0:REL + 1, ONEHOT:ONEHOT + 384], I["onehot"], "rel_in")
        t_h = norm_to_h(ar(0, TB, D), cat, lambda k: par("g_src", k), [t_mem, t_const])
        kv = w_cols(I["mem_wkv"][0], 0)
        products("mem_k", kv, 1, *to_channels(K_MEM, 0), ch_cols=(0, 512), after=t_h, more=True)
        b = next_bank()
        t = do("pe", lambda e, b=b: e.matmul(PS[0:A_H, b, 0:384], arena[0:REL + 1, TBL:TBL + A_H],
                                        arena[0:REL + 1, ONEHOT:ONEHOT + 384], start=True, stop=True),
               t_one, t_rel, work_bank_free[b])
        t = do("dve", lambda e, b=b: e.tensor_copy(arena[0:A_H, WROW:WROW + 384], PS[0:A_H, b, 0:384]), t)
        work_bank_free[b] = [t]
        scratch = I["scratch"]
        t = dma("act", scratch, arena[0:A_H, WROW:WROW + 384], "rel_out", t)
        hankel = ar(HANKEL, A_H, S)
        t_hankel = dma("act", hankel, bass.AP(scratch.tensor, 0, [[1, P], [384, A_H], [1, S]]), "rel_back", t)

        t_x = dma("sp", x[:, :, :], I["x"][0].rearrange("(t p) d -> p t d", p=P), "x_in")
        kv2 = w_cols(I["mem_wkv"][0], M_I)
        v_mem = ar(V_MEM, TB, M_I)
        t_used = products("mem_v", kv2, 1, *to_tokens(v_mem, 0), tok_cols=(0, 512))

        t_h = norm_to_h(x, cat, lambda k: par("g_mix", k), [t_x, t_used])
        w_in = I["w_in"][0]
        z_v, z_b = ar(Z_V, TB, A_W), ar(Z_B, TB, 2 * B_W)
        def vb(t):
            def f(e, g, bank):
                if t == 0:
                    e.activation(z_v[:, t, 512:768], bank[:, 0:256], ACT.Copy)
                    return e.activation(z_b[:, t, 0:256], bank[:, 256:512], ACT.Copy)
                e.tensor_copy(z_v[:, t, 512:768], bank[:, 0:256])
                return e.tensor_copy(z_b[:, t, 0:256], bank[:, 256:512])
            return f
        products("bc", w_cols(w_in, 3 * A_W + 768), 1,
                 lambda e, g, bank: e.activation(ar(Z_C, 512), bank, ACT.Copy),
                 lambda e, g, bank: e.tensor_copy(z_b[:, :, 768:1024],
                                                  bank.rearrange("p (t n) -> p t n", t=TB)),
                 tok_cols=(0, 256), ch_cols=(256, 256), after=t_h, evac_after=t_h, more=True)
        C0 = 3 * A_W + 2 * B_W
        products("c", w_cols(w_in, C0 + 256), 4, *to_channels(Z_C, 2), ch_cols=(0, 512), more=True)
        products("c_end", w_cols(w_in, C0 + 256 + 2048, n_cols=384), 1,
                 *evac_pair(lambda g: ar(Z_C + 18 * S, 512), lambda g: ar(Z_C + 20 * S, 256)),
                 ch_cols=(0, 384), n_cols=384, more=True)
        t_c_out = products("vb", w_cols(w_in, 2 * A_W + 512), 1, vb(0), vb(1), tok_cols=(0, 512), more=True,
                           taken_before=True)
        zc = ar(Z_C, 21, S)
        vt = cat[:, :, A_W + B_W:]

        def shift(k0, k1, turn):
            diff, z = ar(CAT + (A_W + B_W) * turn, k1 - k0, S), zc[:, k0:k1, :]
            t1 = do("dve", lambda e: e.tensor_tensor(diff[:, :, 1:], z[:, :, :S - 1], z[:, :, 1:], ALU.subtract),
                    t_c_out, t_shift)
            t2 = do("dve", lambda e: e.tensor_scalar(diff[:, :, 0:1], z[:, :, 0:1], -1.0, None, ALU.mult))
            yield
            for k in range(k0, k1):
                t = do("dve", lambda e, k=k: e.scalar_tensor_tensor(
                    out=zc[:, k, :], in0=diff[:, k - k0, :], scalar=par("mu", k), in1=zc[:, k, :],
                    op0=ALU.mult, op1=ALU.add), t1, t2)
            t_shift[:] = [t]
            yield

        def v_to_tokens(n, b):
            wait("pe", t_shift, work_bank_free[b])
            for k in range(2):
                for t_ in range(TB):
                    fn = lambda e, k=k, t_=t_: e.transpose(
                        PS[:, b, (t_ * 2 + k) * P:(t_ * 2 + k + 1) * P],
                        zc[:, 12 + 2 * n + k, t_ * P:(t_ + 1) * P], ident[:, :])
                    t = do("pe", fn) if k and t_ else quiet("pe", fn)
            yield
            t = do("act", lambda e: e.activation(
                vt[:, :, 2 * n * P:(2 * n + 2) * P], PS[:, b, :].rearrange("p (t n) -> p t n", t=TB),
                ACT.Copy), t, t_shift)
            work_bank_free[b] = [t]
            t_v.append(t)
            yield

        def prepare_c():
            for turn, k0 in enumerate((18, 15, 12, 0, 3, 6, 9)):
                yield from shift(k0, k0 + 3, turn % 2)
            t_act.append(do("act", lambda e: e.activation(zc[0:HD, 18, :], zc[0:HD, 18, :], ACT.Tanh), t_shift))
            t_act.append(do("act", lambda e: e.activation(zc[:, 19:21, :], zc[:, 19:21, :], ACT.Sigmoid), t_shift))
            yield
            for n in range(CB // 2):
                yield from v_to_tokens(n, next_bank())

        SW, SBIAS = 21248, 22272
        ln_gain = cat[:, 1, 0:B_W]
        dma("act", ar(SW, B_G, P), I["sgu_w"][0].rearrange("g i j -> i g j"), "sgu_in", t_hankel)
        dma("act", ar(SBIAS, B_G), I["sgu_b_t"], "sgu_in")
        t_sg = dma("act", ln_gain, bcast("sgu_norm_gain", 0, B_W), "sgu_in", t_h)

        def norm_part(c0, w, junk, after):
            ssq, t = sum_squares(lambda t_: cat[:, t_, c0:c0 + w], junk, after)
            rstd = col(2)
            t = rstd_of(ssq, rstd, w, EPS, 2, t)
            return [do("dve", lambda e, t_=t_: e.tensor_scalar(
                cat[:, t_, c0:c0 + w], cat[:, t_, c0:c0 + w], rstd[:, t_:t_ + 1], None, ALU.mult), t)
                for t_ in range(TB)]

        def spatial_gating():
            wt = ar(SW, B_G, P)
            t_w = []
            for n in range(2):
                yield from mixing_matrices(n, next_bank(), wt, t_w)
            t = [do("act", lambda e, t_=t_: e.activation(z_b[:, t_, :], z_b[:, t_, :], ACT.Gelu_apprx_tanh), t_b_out)
                 for t_ in range(TB)]
            mean, var = col(2), col(2)
            yield
            t1 = [do("dve", lambda e, t_=t_: e.tensor_reduce(mean[:, t_:t_ + 1], z_b[:, t_, B_W:], AX.X, ALU.add), t)
                  for t_ in range(TB)]
            t1 = do("dve", lambda e: e.tensor_scalar(mean, mean, 1.0 / B_W, None, ALU.mult), t1)
            yield
            t1 = [do("dve", lambda e, t_=t_: e.tensor_scalar(z_b[:, t_, B_W:], z_b[:, t_, B_W:],
                                                             mean[:, t_:t_ + 1], None, ALU.subtract), t1)
                  for t_ in range(TB)]
            yield
            ssq, t1 = sum_squares(lambda t_: z_b[:, t_, B_W:], lambda t_: cat[:, t_, A_W:A_W + B_W], t1)
            yield
            t1 = rstd_of(ssq, var, B_W, EPS, 2, t1)
            yield
            t1 = [do("dve", lambda e, t_=t_: e.scalar_tensor_tensor(
                out=z_b[:, t_, B_W:], in0=z_b[:, t_, B_W:], scalar=var[:, t_:t_ + 1], in1=ln_gain,
                op0=ALU.mult, op1=ALU.mult), t1, t_sg) for t_ in range(TB)]
            yield
            for n in range(2):
                yield from mix_groups(n, next_bank(), wt, [t_w, t1])
            yield
            norm_part(A_W, B_W, lambda t_: z_b[:, t_, 0:B_W], [t_gated_b])
            yield

        def mixing_matrices(n, b, wt, made):
            part = wt[:, 4 * n:4 * n + 4, :]
            wait("pe", t_sg, work_bank_free[b])
            for g in range(4):
                fn = lambda e, g=g: e.transpose(PS[:, b, g * P:(g + 1) * P], part[:, g, :], ident[:, :])
                t = do("pe", fn) if g == 3 else quiet("pe", fn)
            yield
            t = do("act", lambda e: e.activation(part.rearrange("p g i -> p (g i)"), PS[:, b, :], ACT.Copy), t)
            work_bank_free[b] = [t]
            made.append(do("pool", lambda e: e.affine_select(
                out=part, in_=part, compare_op=ALU.is_ge, fill=0.0, base=0, pattern=[[0, 4], [1, P]],
                channel_multiplier=-1), t))
            yield

        t_gated_b = []
        def mix_groups(n, b, wt, after):
            wait("pe", after, work_bank_free[b])
            for g in range(4):
                fn = lambda e, g=g: e.matmul(
                    PS[:, b, g * P:(g + 1) * P], wt[:, 4 * n + g, :],
                    z_b[:, :, B_W + (4 * n + g) * HD:B_W + (4 * n + g + 1) * HD], start=True, stop=True)
                t = do("pe", fn) if g == 3 else quiet("pe", fn)
            yield
            c0, w = A_W + 4 * n * HD, 4 * HD
            bias = ar(SBIAS, B_G)[:, 4 * n:4 * n + 4].unsqueeze(2).to_broadcast([P, 4, HD])
            for t_ in range(TB):
                t = do("dve", lambda e, t_=t_: e.tensor_tensor(
                    cat[:, t_, c0:c0 + w].rearrange("p (g n) -> p g n", g=4),
                    PS[:, b, :].rearrange("p (g t n) -> p g t n", g=4, t=TB)[:, :, t_, :], bias, ALU.add),
                    t, t_shift, t_sg)
                t_gated_b.append(do("dve", lambda e, t_=t_: e.tensor_tensor(
                    cat[:, t_, c0:c0 + w], cat[:, t_, c0:c0 + w], z_b[:, t_, 4 * n * HD:4 * n * HD + w],
                    ALU.mult), t))
            work_bank_free[b] = [t]
            yield

        t_shift, t_act, t_v, t_b_out = [], [], [], []
        fill = prepare_c()
        t_b_out += products("b1", w_cols(w_in, 3 * A_W + 256), 1, *to_tokens(z_b, 256), tok_cols=(0, 512), more=True,
                            rolled=False, fill=fill)
        fill = side_by_side(fill, spatial_gating())
        products("qk", w_cols(w_in, 0), 3, *to_channels(Z_QK, 0), ch_cols=(0, 512), more=True, rolled=False,
                 fill=fill)
        t_z = products("v0", w_cols(w_in, 2 * A_W), 1, *to_tokens(z_v, 0), tok_cols=(0, 512), rolled=False,
                       fill=fill)
        for _ in fill:
            pass
        t_tanh, t_sig = t_act

        zqk = ar(Z_QK, 12, S)
        LORA, GUP = 4608, 18176
        MASKS, PAIR = 6144, 7426
        YT, LE = 3072, 20736
        fence = prog.all_done()
        wait("sp", t_z, fence)
        dma("sp", arena[0:HD, LORA:LORA + C_W], I["rwkv_w_up"][0], "lora_in")
        dma("sp", arena[HD:P, LORA:LORA + C_W], I["rwkv_a_up"][0], "lora_in")
        dma("sp", sp_(MASKS, 1282), I["masks"], "lora_in")
        t_lora = dma("sp", sp_(PAIR, 512).bitcast(I32), I["pair_mask"], "lora_in")
        level_mask = lambda l: sp_(MASKS + P * l, P)
        level0_t = sp_(MASKS + 7 * P, P)
        head_sum = sp_(MASKS + 8 * P, P)
        head_two = sp_(MASKS + 9 * P, 2)
        all_ones = sp_(MASKS + 9 * P + 2, P)
        pair_mask = sp_(PAIR, 512).bitcast(I32)

        def rwkv_lane(banks, mem, mats, r=None, sa=None, s1=None, solve=None, le=None):
            at_, first = mem
            return dict(banks=banks, mats=mats, kk=at_(first, S), a=at_(first + S, S), bt=at_(first + 2 * S, S),
                        r=r[0](r[1], 2, P), sa=sa[0](sa[1], 2, P), s1=s1[0](s1[1], P),
                        X=solve[0](solve[1], 4, P), XT=solve[0](solve[1] + 512, 4, P),
                        U=solve[0](solve[1] + 1024, 4, P), L=le[0](le[1], S), E=le[0](le[1] + S, S), free=[])
        sets = [rwkv_lane((4, 5), (sd, 2048), sd(0, 4, 4, P), r=(sd, 2816), sa=(sd, 3072), s1=(sd, 3328),
                          solve=(sd, 3456), le=(ar, LE)),
                rwkv_lane((6, 7), (sd, 7040), sd(4992, 4, 4, P), r=(ar, 20224), sa=(ar, 20480), s1=(sd, 7808),
                          solve=(ar, 0), le=(ar, LE + 512)),
                rwkv_lane((0, 1), (sp_, 0), sp_(4096, 4, 4, P), r=(sp_, 768), sa=(sp_, 1024), s1=(ar, 5376),
                          solve=(sp_, 1280), le=(sp_, 2816))]
        for st in sets:
            do("pool", lambda e, m=st["s1"]: e.memset(m, 0.0), t_z, fence)
            st["zeroed"] = do("pool", lambda e, m=st["mats"]: e.memset(m, 0.0))

        def dilated_head(h, lane):
            rows = slice(HD * (h % 2), HD * (h % 2) + HD)
            bank, tbank, free = lane["bank"], lane["tbank"], lane["free"]
            p_, pt_ = lane["p"][:, 0:384], lane["s"][:, 0:384]
            nm, den, _ = lane["stat"]
            blk, kblk = zqk[:, h // 2, :], zqk[:, 6 + h // 2, :]
            wait("pe", t_z, t_hankel, free)
            for t_, (o, w) in enumerate(((0, P), (P, S))):
                quiet("pe", lambda e, t_=t_, o=o, w=w: e.matmul(
                    PS[:, bank, o:o + w], blk[rows, t_ * P:(t_ + 1) * P], kblk[rows, 0:w], start=True, stop=False))
                t_s = do("pe", lambda e, o=o, w=w: e.matmul(
                    PS[:, bank, o:o + w], exch[:, :], hankel[:, h, S - w:S], start=False, stop=True))
            yield
            t1 = do("dve", lambda e: e.tensor_reduce(nm[:, 0:1], PS[:, bank, 0:P], AX.X, ALU.max), t_s, free)
            t2 = do("dve", lambda e: e.tensor_reduce(nm[:, 1:2], PS[:, bank, P:384], AX.X, ALU.max))
            t3 = do("dve", lambda e: e.tensor_scalar(nm, nm, -0.125, None, ALU.mult), t1, t2)
            t_e = [do("act", lambda e, t_=t_, o=o, w=w: e.activation(
                p_[:, o:o + w], PS[:, bank, o:o + w], ACT.Exp, bias=nm[:, t_:t_ + 1], scale=0.125,
                accum_out=den[:, t_:t_ + 1]), t3, free) for t_, (o, w) in enumerate(((0, P), (P, S)))]
            yield
            wait("pe", t_e)
            for o in range(3):
                fn = lambda e, o=o: e.transpose(PS[:, tbank, o * P:(o + 1) * P], p_[:, o * P:(o + 1) * P], ident[:, :])
                t_t = do("pe", fn) if o == 2 else quiet("pe", fn)
            yield
            t_r = do("dve", lambda e: e.reciprocal(den, den), t_e)
            t_c = do("act", lambda e: e.activation(pt_, PS[:, tbank, 0:384], ACT.Copy), t_t)
            yield
            wait("pe", t_c)
            vp = slice((h // 2) * P, (h // 2) * P + P)
            quiet("pe", lambda e: e.matmul(PS[:, bank, 0:P], pt_[:, 0:P], z_v[:, 0, vp], start=True, stop=True))
            quiet("pe", lambda e: e.matmul(PS[:, bank, P:2 * P], pt_[:, P:2 * P], z_v[:, 0, vp], start=True, stop=False))
            t_o = do("pe", lambda e: e.matmul(PS[:, bank, P:2 * P], pt_[:, 2 * P:3 * P], z_v[:, 1, vp], start=False,
                                              stop=True))
            yield
            done = [do("dve", lambda e, t_=t_: e.tensor_scalar(
                cat[:, t_, h * HD:(h + 1) * HD], PS[:, bank, t_ * P + (h % 2) * HD:t_ * P + (h % 2) * HD + HD],
                den[:, t_:t_ + 1], None, ALU.mult), t_o, t_r) for t_ in range(TB)]
            lane["free"] = [t_o, t_c, done]

        f = fence_banks()
        for lane in lanes:
            lane["free"] = [t_z, f]
        run_lanes([lambda lane, h=h: dilated_head(h, lane) for h in range(A_H)])
        fence = fence_banks()
        t_gup = dma("sp", ar(GUP, 2, C_W), I["rwkv_g_up"][0].rearrange("(k p) n -> p k n", p=P), "g_up_in", fence)
        norm_part(0, A_W, lambda t_: ar(1536 + t_ * A_W, A_W), fence)

        yt = ar(YT, TB, C_W)
        one_minus_ka, bonus = col(CB), col(2 * C_H)
        t_ka = do("dve", lambda e: e.tensor_scalar(one_minus_ka, params[:, PARAM_AT["k_a"]:PARAM_AT["k_a"] + CB],
                                                   -1.0, 1.0, ALU.mult, ALU.add), fence)
        bonus3 = bonus.rearrange("p (t h) -> p t h", t=TB)
        RATE = math.exp(-0.5)
        bc4 = lambda m: m.unsqueeze(1).to_broadcast([P, 4, P])
        cols2 = {}

        def rwkv_block(b, st):
            A, B = st["banks"]
            mats, X, XT, U, kk, a, L, E = (st[n] for n in ("mats", "X", "XT", "U", "kk", "a", "L", "E"))
            bt, R, SA, S1 = st["bt"], st["r"], st["sa"], st["s1"]
            r, k = zc[:, b, :], zc[:, CB + b, :]
            u0, u1 = U[:, 0:2, :].rearrange("p i t -> p (i t)"), U[:, 2:4, :].rearrange("p i t -> p (i t)")
            bs = slice(b * P, (b + 1) * P)
            free = st["free"]
            t = do("pe", lambda e: e.matmul(PS[:, A, 0:S], arena[0:HD, LORA + b * P:LORA + (b + 1) * P],
                                           zc[0:HD, 18, :], start=True, stop=True), t_lora, t_tanh, free)
            t = do("pe", lambda e: e.matmul(PS[:, A, S:2 * S], arena[HD:P, LORA + b * P:LORA + (b + 1) * P],
                                            zc[HD:P, 18, :], start=True, stop=True), t)
            t_s = do("act", lambda e: e.activation(E, PS[:, A, 0:S], ACT.Sigmoid, bias=par("w0", b)), t, free)
            t_a_ = do("act", lambda e: e.activation(a, PS[:, A, S:2 * S], ACT.Sigmoid, bias=par("a0", b)))
            yield
            t_l = [do("dve", lambda e, c=c: e.tensor_tensor_scan(
                L[:, c * P:(c + 1) * P], all_ones, E[:, c * P:(c + 1) * P], 0.0, ALU.mult, ALU.add), t_s)
                for c in range(TB)]
            t_k = do("dve", lambda e: e.tensor_scalar(kk, k, par("k_k", b), None, ALU.mult))
            t = do("act", lambda e: e.activation(u0, kk, ACT.Square), t_k)
            t = do("pe", lambda e: e.matmul(PS[:, B, 0:S], head_sum, u0, start=True, stop=True), t)
            yield
            t_k1 = do("dve", lambda e: e.tensor_scalar(u1, a, par("k_a", b), one_minus_ka[:, b:b + 1], ALU.mult,
                                                       ALU.add), t_a_, t_ka)
            t_k1 = do("dve", lambda e: e.tensor_tensor(k, k, u1, ALU.mult), t_k1)
            t = do("dve", lambda e: e.tensor_scalar(u1, PS[:, B, 0:S], 1e-24, None, ALU.max), t, t_k1)
            t = do("dve", lambda e: e.reciprocal(u1, u1), t)
            t = do("act", lambda e: e.activation(u1, u1, ACT.Sqrt), t)
            yield
            t_kk = do("dve", lambda e: e.tensor_tensor(kk, kk, u1, ALU.mult), t)
            t = do("dve", lambda e: e.scalar_tensor_tensor(out=u0, in0=r, scalar=par("r_k", b), in1=k,
                                                           op0=ALU.mult, op1=ALU.mult), t_k1)
            for t_ in range(TB):
                fn = lambda e, t_=t_: e.matmul(PS[:, B, S + 2 * t_:S + 2 * t_ + 2], u0[:, t_ * P:(t_ + 1) * P],
                                               head_two, start=True, stop=True)
                t = do("pe", fn, t)
            t_bo = do("dve", lambda e: e.tensor_copy(
                bonus3[:, :, 2 * b:2 * b + 2], PS[:, B, S:S + 4].rearrange("p (t h) -> p t h", t=TB)), t)
            t_b_ = do("dve", lambda e: e.tensor_tensor(a, a, kk, ALU.mult), t_kk)
            if st["banks"] not in cols2:
                cols2[st["banks"]] = (col(2), col(2), col(1))
            plus, minus, end = cols2[st["banks"]]
            mid = L.rearrange("p (c t) -> p c t", c=TB)[:, :, 63]
            t1 = do("dve", lambda e: e.tensor_scalar(plus, mid, RATE, None, ALU.mult), t_l, free)
            t2 = do("dve", lambda e: e.tensor_scalar(minus, mid, -RATE, None, ALU.mult))
            t3 = do("dve", lambda e: e.tensor_scalar(end, L[:, P - 1:P], -RATE, plus[:, 0:1], ALU.mult, ALU.add), t1)
            t3 = do("dve", lambda e: e.tensor_tensor(end, end, minus[:, 1:2], ALU.add), t3, t2)
            t_end = do("act", lambda e: e.activation(end, end, ACT.Exp), t3)
            t_f = [do("act", lambda e, c=c: e.activation(E[:, c * P:(c + 1) * P], L[:, c * P:(c + 1) * P], ACT.Exp,
                                                         scale=RATE, bias=minus[:, c:c + 1]), t1, t2)
                   for c in range(TB)]
            t_g = [do("act", lambda e, c=c: e.activation(u1[:, c * P:(c + 1) * P], L[:, c * P:(c + 1) * P], ACT.Exp,
                                                         scale=-RATE, bias=plus[:, c:c + 1]), t_kk)
                   for c in range(TB)]
            yield
            t_be = do("dve", lambda e: e.tensor_tensor(a, a, E, ALU.mult), t_f, t_b_)
            t_ka_ = do("dve", lambda e: e.tensor_tensor(k, k, E, ALU.mult), t)
            t_rh = do("dve", lambda e: e.tensor_tensor(r, r, u1, ALU.mult), t_g, t)
            t_g = [do("act", lambda e, c=c: e.activation(
                u0[:, c * P + 1:(c + 1) * P], L[:, c * P:(c + 1) * P - 1], ACT.Exp, scale=-RATE,
                bias=plus[:, c:c + 1]), t) for c in range(TB)]
            t_g += [do("act", lambda e: e.activation(u0.rearrange("p (c t) -> p c t", c=TB)[:, :, 0], plus, ACT.Exp))]
            t_al = do("dve", lambda e: e.tensor_tensor(kk, kk, u0, ALU.mult), t_g)
            yield
            t_m, bank_read = [], {A: [t_s, t_a_], B: [t_bo]}
            for i in range(4):
                c, h = i // 2, i % 2
                rows, cs, bank = slice(HD * h, HD * h + HD), slice(c * P, c * P + P), (A, B)[h]
                wait("pe", t_be, t_ka_, t_rh, t_al, bank_read[bank])
                for n, (l, rr) in enumerate(((a, kk), (a, r), (k, kk), (k, r))):
                    fn = lambda e, n=n, l=l, rr=rr, rows=rows, cs=cs, bank=bank: e.matmul(
                        PS[:, bank, n * P:(n + 1) * P], l[rows, cs], rr[rows, cs], start=True, stop=True)
                    t = do("pe", fn) if n == 3 else quiet("pe", fn)
                t = do("dve", lambda e, i=i, bank=bank: e.copy_predicated(
                    mats[:, i, :, :].rearrange("p m t -> p (m t)"), pair_mask, PS[:, bank, :]), t, st["zeroed"],
                    t_lora, free)
                bank_read[bank] = [t]
                t_m.append(t)
            yield
            quiet("pe", lambda e: e.transpose(PS[:, B, 0:P], a[:, 0:P], ident[:, :]), t_m)
            t = do("pe", lambda e: e.transpose(PS[:, B, P:2 * P], k[:, 0:P], ident[:, :]))
            t_bt = do("act", lambda e: e.activation(bt, PS[:, B, 0:2 * P], ACT.Copy), t, free)
            for i in range(4):
                fn = lambda e, i=i: e.transpose(PS[:, A, i * P:(i + 1) * P], mats[:, i, 0, :], ident[:, :])
                t = do("pe", fn) if i == 3 else quiet("pe", fn)
            psA = PS[:, A, :].rearrange("p (i t) -> p i t", i=4)
            psB = PS[:, B, :].rearrange("p (i t) -> p i t", i=4)
            t = do("dve", lambda e: e.tensor_tensor(X, psA, bc4(level_mask(0)), ALU.mult), t, t_al, free)
            t_x_ = do("dve", lambda e: e.tensor_tensor(X, X, bc4(ident[:, :]), ALU.add), t)
            t = do("dve", lambda e: e.tensor_tensor(XT, mats[:, :, 0, :], bc4(level0_t), ALU.mult))
            t_xt = do("dve", lambda e: e.tensor_tensor(XT, XT, bc4(ident[:, :]), ALU.add), t)
            t_b_read = [t_bt]
            yield
            for l in range(1, 7):
                for i in range(4):
                    fn = lambda e, i=i: e.matmul(psA[:, i, :], mats[:, i, 0, :], X[:, i, :], start=True, stop=True)
                    if i == 0:
                        wait("pe", t_x_, t_xt)
                    t = do("pe", fn) if i == 3 else quiet("pe", fn)
                yield
                t_u = do("dve", lambda e, l=l: e.tensor_tensor(U, psA, bc4(level_mask(l)), ALU.mult), t, t_al)
                wait("pe", t_u, t_b_read)
                for i in range(4):
                    fn = lambda e, i=i: e.matmul(psA[:, i, :], U[:, i, :], XT[:, i, :], start=True, stop=True)
                    t = do("pe", fn) if i == 3 else quiet("pe", fn)
                if l < 6:
                    for i in range(4):
                        fn = lambda e, i=i: e.matmul(psB[:, i, :], XT[:, i, :], U[:, i, :], start=True, stop=True)
                        t2 = do("pe", fn) if i == 3 else quiet("pe", fn)
                yield
                if l < 6:
                    t_x_ = do("dve", lambda e: e.tensor_tensor(X, X, psB, ALU.add), t2)
                    t_b_read = [t_x_]
                t_xt = do("dve", lambda e: e.tensor_tensor(XT, XT, psA, ALU.add), t, t2 if l < 6 else None)
            def own(bank, c=0):
                return PS[:, bank, :].rearrange("p (q n) -> p q n", n=HD)[:, 4 * c:4 * c + 4:3, :]

            two = lambda ap: ap.rearrange("p (h n) -> p h n", h=2)

            def solve(c, t_state, t_free):
                wait("pe", t_v, t_free, t_state, st["zeroed"])
                for h in range(2):
                    o = PS[:, B, h * P:(h + 1) * P]
                    fn = lambda e, o=o, h=h: e.matmul(o, mats[:, 2 * c + h, 2, :], vt[:, c, bs], start=True, stop=c == 0)
                    t = do("pe", fn) if h and not c else quiet("pe", fn)
                    if c:
                        fn = lambda e, o=o: e.matmul(o, kk[:, P:2 * P], S1, start=False, stop=True)
                        t = do("pe", fn) if h else quiet("pe", fn)
                t = do("act", lambda e: e.activation(two(R[:, c, :]), own(B), ACT.Copy, scale=-1.0), t, free)
                wait("pe", t, t_xt)
                for h in range(2):
                    fn = lambda e, h=h: e.matmul(PS[:, A, h * P:(h + 1) * P], XT[:, 2 * c + h, :], R[:, c, :],
                                                 start=True, stop=True)
                    t = do("pe", fn) if h else quiet("pe", fn)
                return do("dve", lambda e: e.tensor_copy(two(SA[:, c, :]), own(A)), t, free)

            t_sa0 = solve(0, [], t_b_read)
            yield
            quiet("pe", lambda e: e.matmul(PS[:, B, 0:P], bt[:, 0:P], SA[:, 0, :], start=True, stop=False),
                  t_sa0, t_bt)
            t = do("pe", lambda e: e.matmul(PS[:, B, 0:P], bt[:, P:2 * P], vt[:, 0, bs], start=False, stop=True))
            t_st = [do("act", lambda e, h=h: e.activation(
                S1[HD * h:HD * h + HD, HD * h:HD * h + HD], PS[HD * h:HD * h + HD, B, HD * h:HD * h + HD], ACT.Copy,
                scale=end[HD * h:HD * h + HD, :]), t, t_end, st["zeroed"]) for h in range(2)]
            yield
            t_sa1 = solve(1, t_st, [])
            yield
            wait("pe", t_sa1)
            for i in range(4):
                c, o = i // 2, PS[:, B, i * P:(i + 1) * P]
                quiet("pe", lambda e, i=i, c=c, o=o: e.matmul(o, mats[:, i, 1, :], SA[:, c, :], start=True, stop=False))
                fn = lambda e, i=i, c=c, o=o: e.matmul(o, mats[:, i, 3, :], vt[:, c, bs], start=False, stop=c == 0)
                quiet("pe", fn)
                if c:
                    fn = lambda e, o=o: e.matmul(o, r[:, P:2 * P], S1, start=False, stop=True)
                    t = do("pe", fn) if i == 3 else quiet("pe", fn)
            t = [do("act", lambda e, c=c: e.activation(two(yt[:, c, bs]), own(B, c), ACT.Copy), t) for c in range(TB)]
            st["free"] = [t, t_sa1, t_end]
            yield

        for st in sets:
            st["free"] = [fence]
        run_lanes([lambda st, b=b: rwkv_block(b, st) for b in range(CB)], on=sets)

        fence = fence_banks()
        LNG, LNB = 1536, 2304
        dma("sp", sd(LNG, C_W), bcast("rwkv_ln_gain", 0, C_W), "ln_in", fence)
        t_ln = dma("sp", sd(LNB, C_W), bcast("rwkv_ln_bias", 0, C_W), "ln_in")
        NH = TB * C_H
        y3, tmp3 = ar(YT, NH, HD), sd(0, NH, HD)
        over = lambda c: c.unsqueeze(2).to_broadcast([P, NH, HD])
        y_mean, y_var = col(NH), col(NH)
        t = do("dve", lambda e: e.tensor_reduce(y_mean, y3, AX.X, ALU.add), fence)
        t = do("dve", lambda e: e.tensor_scalar(y_mean, y_mean, 1.0 / HD, None, ALU.mult), t)
        t_y = do("dve", lambda e: e.tensor_tensor(y3, y3, over(y_mean), ALU.subtract), t)
        t = do("act", lambda e: e.activation(tmp3, y3, ACT.Square), t_y)
        t = do("dve", lambda e: e.tensor_reduce(y_var, tmp3, AX.X, ALU.add), t)
        t = rstd_of(y_var, y_var, HD, GN_EPS, NH, t)
        t = do("dve", lambda e: e.tensor_tensor(y3, y3, over(y_var), ALU.mult), t)
        yv, tmpv = ar(YT, TB, C_W), sd(0, TB, C_W)
        rep = lambda a: sd(a, C_W).unsqueeze(1).to_broadcast([P, TB, C_W])
        t = do("dve", lambda e: e.tensor_tensor(yv, yv, rep(LNG), ALU.mult), t, t_ln)
        t = do("dve", lambda e: e.tensor_tensor(yv, yv, rep(LNB), ALU.add), t)
        by_head = lambda a: a.rearrange("p t (h n) -> p t h n", h=C_H)
        t2 = do("dve", lambda e: e.tensor_tensor(
            by_head(tmpv), by_head(vt), bonus3.unsqueeze(3).to_broadcast([P, TB, C_H, HD]), ALU.mult))
        t = do("dve", lambda e: e.tensor_tensor(yv, yv, tmpv, ALU.add), t, t2)
        gup = ar(GUP, 2, C_W)
        HC = C_W // 2
        wait("pe", fence, t_gup)
        for t_ in range(TB):
            for n in range(2):
                for k in range(2):
                    fn = lambda e, t_=t_, n=n, k=k: e.matmul(
                        PS[:, 4 + 2 * t_ + n, 0:HC], zc[:, 19 + k, t_ * P:(t_ + 1) * P],
                        gup[:, k, n * HC:(n + 1) * HC], start=k == 0, stop=k == 1)
                    t_g = do("pe", fn) if k else quiet("pe", fn)
        for t_ in range(TB):
            for n in range(2):
                t_c = do("dve", lambda e, t_=t_, n=n: e.tensor_tensor(
                    cat[:, t_, A_W + B_W + n * HC:A_W + B_W + (n + 1) * HC], yv[:, t_, n * HC:(n + 1) * HC],
                    PS[:, 4 + 2 * t_ + n, 0:HC], ALU.mult), t, t_g)
        fence = fence_banks()

        t_gain = dma("sp", gains, bcast("sandwich_gains", 1 * D, D), "gains_in", fence)
        def mix_gain(k):
            return par("attn_gain", k) if k < 6 else par("sgu_gain", k - 6) if k < 10 else 1.0
        t_h = to_h(cat, mix_gain, [fence])
        y = ar(0, TB, D)
        t_y = products("w_out", w_cols(I["w_out"][0], 0), 4, *to_tokens(y, 0), tok_cols=(0, 512), after=t_h,
                       evac_after=t_h)
        t_xn = add_normed(lambda t: y[:, t, :], gains, lambda t: cat[:, t, :], [t_y, t_gain])

        def attend(n, pairs, scale, v, put, bias=None, sink=None, after=()):
            def head(h, lane):
                s_, p_ = lane["s"], lane["p"]
                bank, tbank, free = lane["bank"], lane["tbank"], lane["free"]
                nm, den, ex = lane["stat"]
                wait("pe", after, free)
                ops = pairs(h)
                for t_ in range(TB):
                    for m, (q, k) in enumerate(ops):
                        t_s = do("pe", lambda e, t_=t_, q=q, k=k, m=m: e.matmul(
                            PS[:, bank, t_ * S:(t_ + 1) * S], q[:, t_ * P:(t_ + 1) * P], k, start=m == 0,
                            stop=m == len(ops) - 1))
                yield
                src = PS[:, bank, :]
                if bias:
                    dist, slope = bias(h)
                    t_s = do("dve", lambda e: e.scalar_tensor_tensor(
                        out=s_, in0=dist, scalar=slope, in1=PS[:, bank, :], op0=ALU.mult, op1=ALU.add), t_s, free)
                    src = s_
                t = do("dve", lambda e: e.tensor_reduce(
                    nm, src.rearrange("p (t k) -> p t k", t=TB), AX.X, ALU.max), t_s, free)
                if sink:
                    t = do("dve", lambda e: e.tensor_scalar(nm, nm, scale, sink(h), ALU.mult, ALU.max), t)
                    t_m = do("dve", lambda e: e.tensor_scalar(nm, nm, -1.0, None, ALU.mult), t)
                else:
                    t_m = do("dve", lambda e: e.tensor_scalar(nm, nm, -scale, None, ALU.mult), t)
                t_e = [do("act", lambda e, t_=t_: e.activation(
                    p_[:, t_ * S:(t_ + 1) * S], src[:, t_ * S:(t_ + 1) * S], ACT.Exp, bias=nm[:, t_:t_ + 1],
                    scale=scale, accum_out=den[:, t_:t_ + 1]), t_m, free) for t_ in range(TB)]
                if sink:
                    t_x = do("act", lambda e: e.activation(ex, nm, ACT.Exp, bias=sink(h)))
                yield
                for kb in range(TB):
                    for t_ in range(TB):
                        fn = lambda e, kb=kb, t_=t_: e.transpose(
                            PS[:, tbank, (kb * TB + t_) * P:(kb * TB + t_ + 1) * P],
                            p_[:, t_ * S + kb * P:t_ * S + (kb + 1) * P], ident[:, :])
                        t_t = do("pe", fn, t_e) if kb and t_ else quiet("pe", fn, t_e)
                yield
                t_r = t_e
                if sink:
                    t_r = do("dve", lambda e: e.tensor_tensor(den, den, ex, ALU.add), t_x, t_e)
                t_r = do("dve", lambda e: e.reciprocal(den, den), t_r)
                t_c = do("act", lambda e: e.activation(s_, PS[:, tbank, :], ACT.Copy), t_t, t_e)
                yield
                vv = v(h)
                for t_ in range(TB):
                    for kb in range(TB):
                        fn = lambda e, kb=kb, t_=t_: e.matmul(
                            PS[:, bank, t_ * P:(t_ + 1) * P], s_[:, (kb * TB + t_) * P:(kb * TB + t_ + 1) * P],
                            vv[:, kb, :], start=kb == 0, stop=kb == TB - 1)
                        t_o = do("pe", fn, t_c) if kb and t_ else quiet("pe", fn, t_c)
                yield
                done = [put(h, t_, PS[:, bank, t_ * P:(t_ + 1) * P], den[:, t_:t_ + 1], [t_o, t_r])
                        for t_ in range(TB)]
                lane["free"] = [t_o, t_c, done]

            run_lanes([lambda lane, h=h: head(h, lane) for h in range(n)])
            return fence_banks()

        def put_in(dst):
            return lambda h, t_, ps, rden, after: do("dve", lambda e: e.tensor_scalar(
                dst[:, t_, h * P:(h + 1) * P], ps, rden, None, ALU.mult), after)

        t_h = norm_to_h(x, cat, lambda k: par("g_mem", k), [t_xn, t_y])
        t_q = products("mem_q", w_cols(I["mem_wq"][0], 0), 1, *to_channels(Z_C, 0), ch_cols=(0, 512), after=t_h,
                       evac_after=t_h)
        k_mem, q_mem, o_mem = ar(K_MEM, M_H, S), ar(Z_C, M_H, S), ar(Z_C + 1024, TB, M_I)
        t_gain = dma("sp", gains, bcast("sandwich_gains", 3 * D, D), "gains_in", t_xn)
        fence = attend(M_H, lambda h: [(q_mem[:, h, :], k_mem[:, h, :])], M_D ** -0.5,
                       lambda h: v_mem[:, :, h * P:(h + 1) * P], put_in(o_mem), after=[t_q, fence_banks()])
        t_h = to_h(o_mem, None, [fence], n_blocks=M_H)
        wo = I["mem_wo"][0].rearrange("(k p) n -> p k n", p=P)
        t_y = products("mem_o", lambda g, j: wo[:, :, g * 512:(g + 1) * 512], 4, *to_tokens(y, 0),
                       tok_cols=(0, 512), units=1, after=t_h, evac_after=t_h)
        t_xn = add_normed(lambda t: y[:, t, :], gains, lambda t: cat[:, t, :], [t_y, t_gain])

        t_h = norm_to_h(x, cat, lambda k: par("g_ffn", k), [t_xn, t_y])
        act_ff = ar(0, FB * S)
        CONV = 16128
        conv = ar(CONV, 2, 4, S)
        ff = {n: ctx.enter_context(nc.semaphore(n)) for n in ("taps", "gelu_made", "gated")}
        GATED_CREDIT = 2
        prog.queue["dve"].append(lambda e, i: e.sem_inc(ff["gated"], GATED_CREDIT))
        G0 = state["group"]

        def channel(name, g, half, c, j=0):
            at_ = PARAM_AT[name] + (j * 2 + half) * FB + c
            return params[:, bass.ds(g * 2 + at_, 1)]

        def up_act(e, g, parity):
            e.wait_ge(ff["gated"], g + 1)
            for m in range(4):
                half, c = m // 2, m % 2
                last = e.activation(conv[:, parity, m, :], PS[:, 2 * parity + half, c * S:(c + 1) * S], ACT.Identity,
                                    scale=channel("conv_w", g, half, c, 2), bias=channel("conv_b", g, half, c))
            return last

        def up_dve(e, g, parity):
            e.wait_ge(sem["act_evac"], EVAC_CREDIT + G0 + g + 1)
            for back in (1, 2):
                if back == 2:
                    e.wait_ge(ff["taps"], g + 1)
                for m in range(4):
                    half, c = m // 2, m % 2
                    d = conv[:, parity, m, back:]
                    last = e.scalar_tensor_tensor(out=d, in0=PS[:, 2 * parity + half, c * S:(c + 1) * S - back],
                                                  scalar=channel("conv_w", g, half, c, 2 - back), in1=d,
                                                  op0=ALU.mult, op1=ALU.add)
                if back == 1:
                    last.then_inc(ff["taps"], 1)
            return last

        def gate_act(e, g, parity):
            e.wait_ge(sem["dve_evac"], EVAC_CREDIT + G0 + g + 1)
            e.activation(conv[:, parity, 0:2, :], conv[:, parity, 0:2, :], ACT.Gelu_apprx_tanh)\
             .then_inc(ff["gelu_made"], 1)

        def gate_dve(e, g, parity):
            e.wait_ge(ff["gelu_made"], g + 1)
            flat2 = lambda a: a.rearrange("p c n -> p (c n)")
            e.tensor_tensor(act_ff[:, bass.ds(g * (2 * S), 2 * S)], flat2(conv[:, parity, 0:2, :]),
                            flat2(conv[:, parity, 2:4, :]), ALU.mult).then_inc(ff["gated"], 1)

        w_up = I["ffn_w_up"][0].rearrange("(k p) n -> p k n", p=P)
        t_u = products("ffn_up", lambda g, j: tuple(w_up[:, 4 * j:4 * j + 4, bass.ds(g * S + a, S)]
                                                    for a in (0, D_FF)), FB // 2,
                       up_act, up_dve, ch_cols=(0, 512), after=t_h, evac_after=t_h,
                       finish={"act": gate_act, "dve": gate_dve}, halves=True)
        t_gated = (ff["gated"], GATED_CREDIT + FB // 2)
        t_gain = dma("sp", gains, bcast("sandwich_gains", 5 * D, D), "gains_in", t_xn)

        w_down = I["ffn_w_down"][0].rearrange("(k p) n -> p k n", p=P)
        U0 = state["unit"]
        state["unit"] += FB

        def down(q, quad, U, first, final):
            def sp(e):
                for j in range(4):
                    load_unit(e, U + j, j, (1, 2048), w_down[:, bass.ds(q * 4 + j, 1), :])

            def rows(j):
                return act_ff[:, bass.ds(q * (4 * S) + j * S, S)]

            def act(e):
                for j in range(4):
                    e.wait_ge(sem["unit_used"], U + j + 1)
                    e.activation(h_hi[:, j % 2, :], rows(j), ACT.Copy).then_inc(ff_hi, 1)
                    split_hi(e, U + j, quad, j, 2048)

            def dve(e):
                for j in range(4):
                    e.wait_ge(ff_hi, q * 4 + j + 1)
                    e.tensor_tensor(h_lo[:, j % 2, :], rows(j), h_hi[:, j % 2, :].bitcast(F32), ALU.subtract)\
                     .then_inc(ff_lo, 1)
                    split_lo(e, U + j, j, 2048)

            def pe(e):
                for j in range(4):
                    s = j % 2
                    e.wait_ge(ff_lo, q * 4 + j + 1)
                    e.wait_ge(sem["lo_made"], LO_CREDIT + U + j + 1)
                    for t in range(TB):
                        for n in range(4):
                            ws = slice(n * 512, (n + 1) * 512)
                            last = three_pass(e, PS[:, 4 * t + n, :], h_hi[:, s, t * P:(t + 1) * P],
                                              h_lo[:, s, t * P:(t + 1) * P], w_hi[:, s, ws], w_lo[:, s, ws],
                                              first and j == 0, final and j == 3)
                    last.then_inc(sem["unit_used"], 1)
            return {"sp": sp, "act": act, "dve": dve, "pe": pe}

        ff_hi, ff_lo = (ctx.enter_context(nc.semaphore(n)) for n in ("ff_hi", "ff_lo"))
        fence = fence_banks()
        wait("act", t_u, t_gated)
        wait("dve", t_u, t_gated)
        wait("pe", t_u, fence)
        NQ = FB // 4
        for q, rolled in ((0, False), (1, True), (NQ - 1, False)):
            for en in ("sp", "act", "dve", "pe"):
                if rolled:
                    prog.loop(NQ - 2, {en: lambda e, i, en=en: down(i + 1, i + (U0 // 4 + 1), i * 4 + (U0 + 4),
                                                                    False, False)[en](e)})
                else:
                    prog.once(0, {en: lambda e, i, en=en, q=q: down(q, U0 // 4 + q, U0 + 4 * q, q == 0,
                                                                    q == NQ - 1)[en](e)})
        t_y = [(sem["unit_used"], UNIT_CREDIT + state["unit"])]
        t_xn = add_normed(lambda t: PS[:, 4 * t:4 * t + 4, :].rearrange("p b n -> p (b n)"), gains,
                          lambda t: cat[:, t, :], [t_y, t_gain], psum=True)
        fence = fence_banks()

        ZT, ZTOK = 0, 4608
        NT_COLS = 3520
        zt2, ztok = ar(ZT, 18, S), ar(ZTOK, TB, NT_COLS)
        W_UQ, W_UKV, DIST, DISTM = 16128, 18432, 20480, 20992
        SINK, LAM, SUBLN, TRIG, INV, POS = 21504, 21512, 21768, 21896, 22024, 22056
        w_uq, w_ukv = ar(W_UQ, 3, 768), ar(W_UKV, 2, 1024)
        dist, dist_far = ar(DIST, TB * S), ar(DISTM, TB * S)
        pos_i = arena[:, POS:POS + S + TB].bitcast(I32)
        dma("sp", pos_i[:, 0:S], bcast("positions_2", 0, S), "pos_in", fence)
        for t_ in range(TB):
            dma("sp", pos_i[:, S + t_:S + t_ + 1], bass.AP(I["positions_2"].tensor, t_ * P, [[1, P], [1, 1]]),
                "pos_in")
        t_pos = dma("sp", ar(INV, L2_HALF), bcast("inv_freq", 0, L2_HALF), "pos_in")
        def positions():
            d_i = arena[:, DISTM:DISTM + TB * S].bitcast(I32)
            t = [do("pool", lambda e, t_=t_: e.tensor_tensor(
                d_i[:, t_ * S:(t_ + 1) * S], pos_i[:, 0:S], pos_i[:, S + t_:S + t_ + 1].to_broadcast([P, S]),
                ALU.subtract), t_pos, fence) for t_ in range(TB)]
            t = do("dve", lambda e: e.tensor_copy(dist, d_i), t)
            yield
            t = do("act", lambda e: e.activation(dist, dist, ACT.Abs), t)
            yield
            t = do("dve", lambda e: e.tensor_scalar(dist_far, dist, float(P), BIG, ALU.is_gt, ALU.mult), t)
            yield
            t_dist.append(do("dve", lambda e: e.tensor_tensor(dist_far, dist_far, dist, ALU.add), t))
            yield
            pos_f = col(TB)
            k_i = arena[:, POS:POS + 128].bitcast(I32)
            k_f = arena[:, POS + 128:POS + 256]
            t1 = do("dve", lambda e: e.tensor_copy(pos_f, pos_i[:, S:S + TB]), t_pos)
            t1 = [do("dve", lambda e, t_=t_: e.tensor_scalar(trig[:, 0, t_, :], ar(INV, L2_HALF), pos_f[:, t_:t_ + 1],
                                                             None, ALU.mult), t1) for t_ in range(TB)]
            tr = ar(TRIG, 128)
            t1 = do("dve", lambda e: e.tensor_scalar(trig[:, 1, :, :], trig[:, 0, :, :], math.pi / 2, None, ALU.add), t1)
            t2 = do("dve", lambda e: e.tensor_scalar(k_f, tr, 1 / (2 * math.pi), None, ALU.mult), t1, t_dist)
            t2 = do("dve", lambda e: e.tensor_copy(k_i, k_f), t2)
            t2 = do("dve", lambda e: e.tensor_copy(k_f, k_i), t2)
            C1, C2 = 6.28125, 2 * math.pi - 6.28125
            for cst in (C1, C2):
                t2 = do("dve", lambda e, cst=cst: e.scalar_tensor_tensor(out=tr, in0=k_f, scalar=-cst, in1=tr,
                                                                         op0=ALU.mult, op1=ALU.add), t2)
            yield
            for cmp_, lim, turn_ in ((ALU.is_gt, math.pi, -2 * math.pi), (ALU.is_lt, -math.pi, 2 * math.pi)):
                t2 = do("dve", lambda e, c=cmp_, l=lim, u=turn_: e.tensor_scalar(k_f, tr, l, u, c, ALU.mult), t2)
                t2 = do("dve", lambda e: e.tensor_tensor(tr, tr, k_f, ALU.add), t2)
            t2 = do("dve", lambda e: e.tensor_scalar(tr, tr, 3.1415925, -3.1415925, ALU.min, ALU.max), t2)
            yield
            t_trig.append(do("act", lambda e: e.activation(tr, tr, ACT.Sin), t2))
            yield

        t_dist, t_trig, trig = [], [], ar(TRIG, 2, TB, L2_HALF)

        AV, AG, CQ, CKV, KR, BG, CV, CG = 0, 256, 1280, 1664, 1920, 1984, 2496, 3008
        MQ, MK, MV, QRT, KRT, CQT, CKVT = 3072, 4096, 5120, 6144, 6656, 6912, 7680
        slopes = lambda n: [2.0 ** (-8.0 * (i + 1) / n) for i in range(n)]

        t_prev = [t_xn]
        def second_layer(layer, t_prev):
            lam_init = 0.8 - 0.6 * math.exp(-0.3 * layer)
            fence = fence_banks()
            dma("sp", w_uq, I["mla_w_uq_2"][layer].rearrange("(k p) n -> p k n", p=P), "small_in", fence)
            dma("sp", w_ukv, I["mla_w_ukv_2"][layer].rearrange("(k p) n -> p k n", p=P), "small_in")
            dma("sp", ar(SINK, 8), bcast("swa_sink_2", 8 * layer, 8), "small_in")
            dma("sp", ar(SUBLN, P), bcast("diff_subln_2", P * layer, P), "small_in")
            t_small = dma("sp", ar(LAM, S), bcast("diff_lambda_2", S * layer, S), "small_in")
            t_h = norm_to_h(x, cat, lambda k: par(f"g_l{layer}", k), [t_prev, fence])
            w = I["w_in_2"][layer]
            side_work = {} if layer else {"rolled": False, "fill": positions()}
            products("q", w_cols(w, 0), 2, *to_channels(ZT, 0), ch_cols=(0, 512), after=t_h, evac_after=t_h,
                     more=True, **side_work)
            for _ in side_work.get("fill", ()):
                pass
            products("kv", w_cols(w, 1024), 1,
                     lambda e, g, bank: e.activation(ar(ZT + 8 * S, 512), bank, ACT.Copy),
                     lambda e, g, bank: e.tensor_copy(ztok[:, :, AV:AV + 256],
                                                      bank.rearrange("p (t n) -> p t n", t=TB)),
                     tok_cols=(256, 256), ch_cols=(0, 256), more=True)
            products("tok", w_cols(w, 1536), 4, *to_tokens(ztok, AG), tok_cols=(0, 512), more=True)
            products("tok_end", w_cols(w, 3584, n_cols=192), 1,
                     *evac_pair(lambda g: ztok[:, 0, AG + 2048:AG + 2240], lambda g: ztok[:, 1, AG + 2048:AG + 2240]),
                     tok_cols=(0, 192), n_cols=192, more=True)
            products("c_qk", w_cols(w, 3776), 2, *to_channels(ZT, 10), ch_cols=(0, 512), more=True)
            t_z = products("c_vg", w_cols(w, 4800), 2, *to_tokens(ztok, CV), tok_cols=(0, 512))
            fence = fence_banks()

            SC = P ** -0.5
            attend(8, lambda h: [(zt2[:, h, :], zt2[:, 8 + h // 4, :])], SC,
                   lambda h: ztok[:, :, AV + (h // 4) * P:AV + (h // 4 + 1) * P], put_in(cat),
                   bias=lambda h: (dist_far, -slopes(8)[h] / SC), sink=lambda h: ar(SINK, 8)[:, h:h + 1],
                   after=[t_z, t_small, t_dist, fence])

            cq_t, ckv_t = sd(CQT, 3, S), sd(CKVT, 2, S)
            t_ct = []
            for c0, nb, gname, dst in ((CQ, 3, "q_norm", cq_t), (CKV, 2, "kv_norm", ckv_t)):
                wd = nb * P
                ssq, t = sum_squares(lambda t_, c0=c0, wd=wd: ztok[:, t_, c0:c0 + wd],
                                     lambda t_, wd=wd: sd(2048 + t_ * 512, wd),
                                     prog.all_done())
                rstd = col(2)
                t = rstd_of(ssq, rstd, wd, EPS, 2, t)
                t = [do("dve", lambda e, t_=t_, c0=c0, wd=wd, rstd=rstd: e.tensor_scalar(
                    ztok[:, t_, c0:c0 + wd], ztok[:, t_, c0:c0 + wd], rstd[:, t_:t_ + 1], None, ALU.mult), t)
                    for t_ in range(TB)]
                for k in range(nb):
                    b = next_bank()
                    wait("pe", t, work_bank_free[b])
                    for t_ in range(TB):
                        fn = lambda e, t_=t_, k=k, b=b, c0=c0: e.transpose(
                            PS[:, b, t_ * P:(t_ + 1) * P], ztok[:, t_, c0 + k * P:c0 + (k + 1) * P], ident[:, :])
                        t_t = do("pe", fn) if t_ else quiet("pe", fn)
                    gk = par(gname, layer * nb + k)
                    tt = do("act", lambda e, k=k, b=b, dst=dst, gk=gk: e.activation(dst[:, k, :], PS[:, b, 0:S],
                                                                                    ACT.Copy, scale=gk), t_t)
                    work_bank_free[b] = [tt]
                    t_ct.append(tt)
            QR, ROT, TMP = 0, 640, 1408
            qr, rot = sd(QR, TB, 5, 64), sd(ROT, TB, 6, 64)
            b = next_bank()
            uq4 = w_uq.rearrange("p k (h n) -> p k h n", h=4)
            wait("pe", t_ct, work_bank_free[b])
            for t_ in range(TB):
                for k in range(3):
                    fn = lambda e, t_=t_, k=k, b=b: e.matmul(
                        PS[:, b, t_ * S:(t_ + 1) * S], cq_t[:, k, t_ * P:(t_ + 1) * P], uq4[:, k, :, P:P + 64],
                        start=k == 0, stop=k == 2)
                    t = do("pe", fn) if k == 2 else quiet("pe", fn)
            f = prog.all_done()
            t = do("act", lambda e, b=b: e.activation(qr[:, :, 0:4, :].rearrange("p t h n -> p t (h n)"),
                                                      PS[:, b, :].rearrange("p (t n) -> p t n", t=TB), ACT.Copy), t, f)
            work_bank_free[b] = [t]
            t_kr = do("dve", lambda e: e.tensor_copy(qr[:, :, 4, :], ztok[:, :, KR:KR + 64]), f)
            t_rot = []
            for t_ in range(TB):
                sin, cos = (trig[:, m, t_, :].unsqueeze(1).to_broadcast([P, 5, L2_HALF]) for m in (0, 1))
                x1, x2 = qr[:, t_, :, 0:L2_HALF], qr[:, t_, :, L2_HALF:]
                ta, tb_ = sd(TMP, 5, L2_HALF), sd(TMP + 160, 5, L2_HALF)
                for o, m1, m2, op in ((0, cos, sin, ALU.subtract), (L2_HALF, sin, cos, ALU.add)):
                    a1 = do("dve", lambda e, x1=x1, m1=m1, ta=ta: e.tensor_tensor(ta, x1, m1, ALU.mult), t, t_kr, t_trig,
                            t_rot[-1:])
                    a2 = do("dve", lambda e, x2=x2, m2=m2, tb_=tb_: e.tensor_tensor(tb_, x2, m2, ALU.mult))
                    a3 = do("dve", lambda e, t_=t_, o=o, op=op, ta=ta, tb_=tb_: e.tensor_tensor(
                        rot[:, t_, 0:5, o:o + L2_HALF], ta, tb_, op), a1, a2)
                    t_rot.append(a3)
            t_rot = do("dve", lambda e: e.tensor_copy(rot[:, :, 5, :], rot[:, :, 4, :]), t_rot)
            for blk in range(3):
                b = next_bank()
                wait("pe", t_rot, work_bank_free[b])
                for t_ in range(TB):
                    fn = lambda e, t_=t_, blk=blk, b=b: e.transpose(
                        PS[:, b, t_ * P:(t_ + 1) * P], rot[:, t_, 2 * blk:2 * blk + 2, :].rearrange("p a n -> p (a n)"),
                        ident[:, :])
                    t = do("pe", fn) if t_ else quiet("pe", fn)
                t = do("act", lambda e, blk=blk, b=b: e.activation(sd(QRT + blk * S, S), PS[:, b, 0:S], ACT.Copy), t)
                work_bank_free[b] = [t]
            for dst, wsrc, n_k, src, stride in ((MQ, w_uq, 3, cq_t, 192), (MK, w_ukv, 2, ckv_t, 256)):
                for hp in range(2):
                    b = next_bank()
                    wait("pe", t_ct, work_bank_free[b])
                    for hh in range(2):
                        for k in range(n_k):
                            h = 2 * hp + hh
                            fn = lambda e, hh=hh, h=h, k=k, b=b, wsrc=wsrc, src=src, stride=stride, n_k=n_k: e.matmul(
                                PS[:, b, hh * S:(hh + 1) * S], wsrc[:, k, h * stride:h * stride + P], src[:, k, :],
                                start=k == 0, stop=k == n_k - 1)
                            t = do("pe", fn) if hh and k == n_k - 1 else quiet("pe", fn)
                    t = do("act", lambda e, b=b, dst=dst, hp=hp: e.activation(sd(dst + hp * 512, 512), PS[:, b, :],
                                                                              ACT.Copy), t)
                    work_bank_free[b] = [t]
            ukv4 = w_ukv.rearrange("p k (h n) -> p k h n", h=4)
            for t_ in range(TB):
                b = next_bank()
                wait("pe", work_bank_free[b])
                for k in range(2):
                    fn = lambda e, t_=t_, k=k, b=b: e.matmul(PS[:, b, :], ckv_t[:, k, t_ * P:(t_ + 1) * P],
                                                             ukv4[:, k, :, P:2 * P], start=k == 0, stop=k == 1)
                    t = do("pe", fn) if k else quiet("pe", fn)
                t = do("dve", lambda e, t_=t_, b=b: e.tensor_copy(sd(MV + 512 * t_, 512), PS[:, b, :]), t)
                work_bank_free[b] = [t]
            fence = fence_banks()
            mq, mk, mv, qrt, krt = sd(MQ, 4, S), sd(MK, 4, S), sd(MV, TB, 512), sd(QRT, 2, S), sd(KRT, S)
            half = lambda h: slice(64 * (h % 2), 64 * (h % 2) + 64)
            attend(4, lambda h: [(mq[:, h, :], mk[:, h, :]), (qrt[half(h), h // 2, :], krt[half(h), :])],
                   (P + 64) ** -0.5, lambda h: mv[:, :, h * P:(h + 1) * P], put_in(cat[:, :, 1024:1536]),
                   after=[fence])

            lam = ar(LAM, 4, 64)
            e2, neg_lam = col(2), col(1)
            t = do("dve", lambda e: e.tensor_tensor(lam[:, 0, :], lam[:, 0, :], lam[:, 1, :], ALU.mult), t_small)
            t = do("dve", lambda e: e.tensor_tensor(lam[:, 1, :], lam[:, 2, :], lam[:, 3, :], ALU.mult), t)
            t = do("dve", lambda e, e2=e2: e.tensor_reduce(e2, lam[:, 0:2, :], AX.X, ALU.add), t)
            t = do("act", lambda e, e2=e2: e.activation(e2, e2, ACT.Exp), t)
            t_lam = do("dve", lambda e, e2=e2, neg_lam=neg_lam: e.tensor_scalar(
                neg_lam, e2[:, 1:2], e2[:, 0:1], -lam_init, ALU.subtract, ALU.add), t)
            t_sub = do("dve", lambda e: e.tensor_scalar(ar(SUBLN, P), ar(SUBLN, P), 1.0 - lam_init, None, ALU.mult),
                       t_small)

            def put_diff(j, t_, ps, rden, after):
                h, second = j // 2, j % 2
                d = cat[:, t_, 1536 + h * P:1536 + (h + 1) * P]
                if not second:
                    return do("dve", lambda e: e.tensor_scalar(d, ps, rden, None, ALU.mult), after)
                t = do("dve", lambda e: e.tensor_tensor(rden, rden, neg_lam, ALU.mult), after, t_lam)
                return do("dve", lambda e: e.scalar_tensor_tensor(out=d, in0=ps, scalar=rden, in1=d, op0=ALU.mult,
                                                                  op1=ALU.add), t)
            DSC = 64 ** -0.5
            half2 = lambda j: slice(64 * (j % 2), 64 * (j % 2) + 64)
            fence = attend(8, lambda j: [(zt2[half2(j), 10 + j // 2, :], zt2[half2(j), 14 + j // 2, :])], DSC,
                           lambda j: ztok[:, :, CV + (j // 2) * P:CV + (j // 2 + 1) * P], put_diff,
                           bias=lambda j: (dist, -slopes(4)[j // 2] / DSC), after=[fence_banks()])
            NV = TB * 4
            ssq, sq = col(NV), sd(0, TB, 512)
            yc = cat[:, :, 1536:2048]
            h4 = lambda a: a.rearrange("p t (h n) -> p t h n", h=4)
            t = do("act", lambda e: e.activation(sq, yc, ACT.Square), fence)
            t = do("dve", lambda e, ssq=ssq: e.tensor_reduce(ssq, sd(0, NV, P), AX.X, ALU.add), t)
            t = rstd_of(ssq, ssq, P, EPS, NV, t)
            t_n = []
            for t_ in range(TB):
                v4 = cat[:, t_, 1536:2048].rearrange("p (h n) -> p h n", h=4)
                a = do("dve", lambda e, t_=t_, v4=v4, ssq=ssq: e.tensor_tensor(
                    v4, v4, ssq[:, 4 * t_:4 * t_ + 4].unsqueeze(2).to_broadcast([P, 4, P]), ALU.mult), t)
                t_n.append(do("dve", lambda e, v4=v4: e.tensor_tensor(
                    v4, v4, ar(SUBLN, P).unsqueeze(1).to_broadcast([P, 4, P]), ALU.mult), a, t_sub))
            t_g = []
            for g0, w0_, c0 in ((AG, 1024, 0), (BG, 512, 1024), (CG, 512, 1536)):
                g_ = ztok[:, :, g0:g0 + w0_]
                t = do("act", lambda e, g_=g_: e.activation(g_, g_, ACT.Silu), fence)
                t_g.append(do("dve", lambda e, g_=g_, c0=c0, w0_=w0_: e.tensor_tensor(
                    cat[:, :, c0:c0 + w0_], cat[:, :, c0:c0 + w0_], g_, ALU.mult), t, t_n))
            t_h = to_h(cat, None, [t_g, fence_banks()])

            y2 = ar(0, D)

            def add_rows(e, g, bank):
                xs = x[:, 1, bass.ds(g * 512, 512)]
                return e.tensor_tensor(xs, xs, bank, ALU.add)
            t_y = products("w_out_2", w_cols(I["w_out_2"][layer], 0), 4,
                           evac_pair(lambda g: y2[:, bass.ds(g * 512, 512)], None)[0], add_rows,
                           tok_cols=(0, 512), after=t_h, evac_after=[t_h, prog.all_done()])
            return [do("dve", lambda e: e.tensor_tensor(x[:, 0, :], x[:, 0, :], y2, ALU.add), t_y), t_y]

        for layer in range(LAYERS):
            t_prev = second_layer(layer, t_prev)

        FG = 4096
        t_fg = dma("sp", ar(FG, D), bcast("final_norm_2", 0, D), "final_in",
                   prog.all_done(), t_prev)
        ssq, t = sum_squares(lambda t: x[:, t, :], lambda t: cat[:, t, :], t_prev)
        rstd = col(2)
        t = rstd_of(ssq, rstd, D, EPS, 2, t)
        for t_ in range(TB):
            t1 = do("dve", lambda e, t_=t_: e.scalar_tensor_tensor(
                out=cat[:, t_, :], in0=x[:, t_, :], scalar=rstd[:, t_:t_ + 1], in1=ar(FG, D), op0=ALU.mult,
                op1=ALU.mult), t, t_fg)
            t_out = dma("sp" if t_ else "act", out[0, t_ * P:(t_ + 1) * P, :], cat[:, t_, :], "out_done", t1)
        for en in ("sp", "act"):
            wait(en, t_out)

        block = ctx.enter_context(nc.Block())
        for name, deco in (("sp", block.sync), ("pe", block.tensor), ("act", block.scalar),
                           ("dve", block.vector), ("pool", block.gpsimd)):
            def run(e, name=name):
                for f in prog.queue[name]:
                    f(e, 0)
            deco(run)


_DIRECT = ["x", "mem", "rel_bias_table", "sandwich_gains", "w_in", "w_out", "sgu_norm_gain", "sgu_w",
           "rwkv_w_up", "rwkv_a_up", "rwkv_g_up", "rwkv_ln_gain", "rwkv_ln_bias", "mem_wq", "mem_wkv", "mem_wo",
           "ffn_w_up", "ffn_w_down", "positions_2", "w_in_2", "swa_sink_2", "mla_w_uq_2", "mla_w_ukv_2",
           "diff_lambda_2", "diff_subln_2", "w_out_2", "final_norm_2"]


def constants():
    c = {"ident": np.eye(P, dtype=np.float32), "exch": np.eye(P, dtype=np.float32)[::-1].copy()}
    dist = 255 - np.arange(384)
    count = ((dist >= 0) & (dist <= 128)) * 1 + ((dist >= 0) & (dist % 4 == 0)) + ((dist >= 0) & (dist % 16 == 0))
    exact = REL // 2
    d = np.maximum(dist, 0)
    scaled = np.log(np.maximum(d, 1) / exact) / np.log(2048 / exact)
    large = np.minimum(exact + (scaled * (REL - exact)).astype(np.int32), REL - 1)
    bucket = np.where(d < exact, d, large)
    onehot = np.zeros((REL + 1, 384), np.float32)
    seen = count > 0
    onehot[bucket[seen], np.nonzero(seen)[0]] = 8.0
    onehot[REL] = np.where(seen, 8.0 * np.log(np.maximum(count, 1)), 8.0 * NEG)
    c["onehot"] = onehot
    t, s = np.arange(P)[:, None], np.arange(P)[None, :]
    masks = np.zeros((P, 1282), np.float32)
    for l in range(7):
        m = (t // (2 << l) == s // (2 << l)) & ((t >> l) % 2 == 1) & ((s >> l) % 2 == 0)
        masks[:, P * l:P * (l + 1)] = -1.0 * m
        if l == 0:
            masks[:, 7 * P:8 * P] = -1.0 * m.T
    masks[:, 8 * P:9 * P] = t // HD == s // HD
    masks[:, 9 * P] = np.arange(P) < HD
    masks[:, 9 * P + 1] = np.arange(P) >= HD
    masks[:, 9 * P + 2:9 * P + 2 + P] = 1.0
    c["masks"] = masks
    strict, incl = t < s, t <= s
    c["pair_mask"] = np.concatenate([strict, incl, strict, incl], axis=1).astype(np.int32)
    c["inv_freq"] = (np.float32(10000.0) ** (-np.arange(0, 64, 2, dtype=np.float32) / np.float32(64)))\
        .astype(np.float32)[None, :]
    return c


def kernel(**inputs):
    import concourse.bacc as _bacc
    from concourse.bass_utils import run_bass_kernel_spmd as _run

    a = {n: np.asarray(v) for n, v in inputs.items()}
    g = a["sandwich_gains"][0]
    parts = [g[0], g[2], g[4], a["mem_src_gain"], a["norm_g_2"][0], a["norm_g_2"][1], a["rwkv_mu"], a["rwkv_w0"],
             a["rwkv_a0"], a["rwkv_k_k"], a["rwkv_k_a"], a["rwkv_r_k"], a["attn_out_gain"], a["sgu_out_gain"],
             a["ffn_conv_b"], a["ffn_conv_w"], a["mla_q_norm_2"], a["mla_kv_norm_2"]]
    laid = {n: a[n] for n in _DIRECT}
    laid["params"] = np.ascontiguousarray(np.concatenate([p.reshape(-1, P) for p in parts]).T)
    laid["sgu_b_t"] = np.ascontiguousarray(a["sgu_b"][0].T)
    laid.update(constants())
    nc = _bacc.Bacc("TRN2", target_bir_lowering=False, num_devices=1)
    arrays, aps = {}, {}
    for name, v in laid.items():
        v = np.ascontiguousarray(v)
        arrays[f"in_{name}"] = v
        aps[name] = nc.dram_tensor(f"in_{name}", v.shape, mybir.dt.from_np(v.dtype), kind="ExternalInput").ap()
    aps["scratch"] = nc.dram_tensor("bias_rows", (A_H, 384), F32, kind="Internal").ap()
    out = nc.dram_tensor("out_0", (1, S, D), F32, kind="ExternalOutput").ap()
    hybrid_two_blocks(nc, aps, out)
    r = _run(nc, [arrays], core_ids=[0])
    return r.results[0]["out_0"]
```

```python
from contextlib import ExitStack
import math

import numpy as np
import concourse.bass as bass
from concourse import mybir

F32 = mybir.dt.float32
F32R = mybir.dt.float32r
I32 = mybir.dt.int32
ALU = mybir.AluOpType
ACT = mybir.ActivationFunctionType
AX = mybir.AxisListType

P = 128
S = 256
TB = S // P
D = 2048
KB = D // P
HD = 64
A_H, B_G, C_H = 12, 8, 12
A_W, B_W, C_W = A_H * HD, B_G * HD, C_H * HD
CB = C_W // P
M_H, M_D = 4, 128
M_I = M_H * M_D
D_FF = 5632
FB = D_FF // P
REL = 32
EPS, GN_EPS = 1e-6, 64e-5
NEG = -1e30
BIG = 1e30
LAYERS = 2
L2_HALF = 32

PARAM_BLOCKS = [("g_mix", 16), ("g_mem", 16), ("g_ffn", 16), ("g_src", 16), ("g_l0", 16), ("g_l1", 16),
                ("mu", 21), ("w0", 6), ("a0", 6), ("k_k", 6), ("k_a", 6), ("r_k", 6), ("attn_gain", 6),
                ("sgu_gain", 4), ("conv_b", 88), ("conv_w", 264), ("q_norm", 6), ("kv_norm", 4)]
PARAM_AT, _n = {}, 0
for _name, _w in PARAM_BLOCKS:
    PARAM_AT[_name] = _n
    _n += _w
N_PARAM = _n


class Program:

    ENGINES = ("pe", "act", "dve", "pool", "sp")

    def __init__(self, nc, ctx):
        self.queue = {e: [] for e in self.ENGINES}
        self.done = {e: ctx.enter_context(nc.semaphore(f"done_{e}")) for e in self.ENGINES}
        self.count = dict.fromkeys(self.ENGINES, 0)
        self.dma_sems = {}
        self.nc, self.ctx = nc, ctx

    def wait(self, engine, *after):
        for token in flat(after):
            self.queue[engine].append(lambda e, i, t=token: e.wait_ge(t[0], t[1]))

    def do(self, engine, fn, *after):
        self.wait(engine, *after)
        self.count[engine] += 1
        self.queue[engine].append(lambda e, i: fn(e).then_inc(self.done[engine], 1))
        return (self.done[engine], self.count[engine])

    def quiet(self, engine, fn, *after):
        self.wait(engine, *after)
        self.queue[engine].append(lambda e, i: fn(e))

    def dma(self, engine, out, in_, name, *after):
        if name not in self.dma_sems:
            self.dma_sems[name] = [self.ctx.enter_context(self.nc.semaphore(name)), 0]
        entry = self.dma_sems[name]
        entry[1] += 16
        self.wait(engine, *after)
        self.queue[engine].append(lambda e, i: e.dma_start(out, in_).then_inc(entry[0], 16))
        return (entry[0], entry[1])

    def all_done(self):
        return [(self.done[e], self.count[e]) for e in self.ENGINES if self.count[e]]

    def loop(self, n, bodies):
        for engine, body in bodies.items():
            def run(e, _i, body=body):
                with e.Fori(0, n) as i:
                    body(e, i)
            self.queue[engine].append(run)

    def once(self, i, bodies):
        for engine, body in bodies.items():
            self.queue[engine].append(lambda e, _i, body=body: body(e, i))


def flat(x):
    for t in x:
        if t is None:
            continue
        if isinstance(t, tuple) and len(t) == 2 and isinstance(t[1], int):
            yield t
        else:
            yield from flat(t)


def hybrid_two_blocks(nc, I, out):
    with ExitStack() as ctx:
        def sb(name, shape, dt=F32):
            return ctx.enter_context(nc.sbuf_tensor(name, shape, dt))

        prog = Program(nc, ctx)
        do, quiet, dma, wait = prog.do, prog.quiet, prog.dma, prog.wait

        base = -(-nc.sbuf_base // 32) * 32
        h_hi = sb("h_hi", [P, KB, S], F32R)
        h_lo = sb("h_lo", [P, KB, S], F32R)
        side = nc.alloc_sbuf_tensor_at("side", [P, 2 * KB * S], F32, offset=base)
        raw = sb("raw", [P, 4, 2048])
        raw_flat = nc.alloc_sbuf_tensor_at("raw_flat", [P, 8192], F32, offset=base + 4 * 2 * KB * S)
        w_hi = sb("w_hi", [P, 2, 2048], F32R)
        w_lo = sb("w_lo", [P, 2, 2048], F32R)
        spare = nc.alloc_sbuf_tensor_at("spare", [P, 8192], F32, offset=base + 4 * (2 * KB * S + 8192))
        x = sb("x", [P, TB, D])
        ARENA = 22400
        arena = sb("arena", [P, ARENA])
        params = sb("params", [P, N_PARAM])
        ident = sb("ident", [P, P])
        exch = sb("exch", [P, P])
        small = sb("small", [P, 512])
        PS = ctx.enter_context(nc.psum_tensor("PS", [P, 8, 512], F32))

        def view(t, at, dims):
            n = int(np.prod(dims))
            v = t[:, at:at + n]
            if len(dims) == 1:
                return v
            names = "abcd"[:len(dims)]
            return v.rearrange(f"p ({' '.join(names)}) -> p {' '.join(names)}",
                               **{c: d for c, d in zip(names[1:], dims[1:])})

        def sp_(at, *dims):
            return view(spare, at, dims)

        def rw(at, *dims):
            return view(raw_flat, at, dims)

        def ar(at, *dims):
            return view(arena, at, dims)

        def sd(at, *dims):
            return view(side, at, dims)

        def par(name, k=0):
            return params[:, PARAM_AT[name] + k:PARAM_AT[name] + k + 1]

        def bcast(name, at, n):
            return bass.AP(I[name].tensor, at, [[0, P], [1, n]])

        small_at = [0]

        def col(n):
            a = small_at[0]
            small_at[0] += n
            assert small_at[0] <= 512
            return small[:, a:a + n]

        sem = {n: ctx.enter_context(nc.semaphore(n)) for n in
               ("landed0", "landed1", "landed2", "landed3", "hi_made", "lo_made", "unit_used",
                "act_evac", "dve_evac", "squared", "gained")}
        n_squared, n_gained = [0], [0]
        landed = [sem[f"landed{j}"] for j in range(4)]
        right_landed = [ctx.enter_context(nc.semaphore(f"right_landed{j}")) for j in range(4)]
        LO_CREDIT, UNIT_CREDIT, EVAC_CREDIT = 4, 2, 2
        state = {"unit": 0, "group": 0, "left": None, "early": set()}

        def load_unit(e, U, slot, dst_dims, src):
            e.wait_ge(sem["lo_made"], U + 1)
            dst = raw[:, slot, :dst_dims[0] * dst_dims[1]].rearrange("p (k n) -> p k n", k=dst_dims[0])
            if isinstance(src, tuple):
                half = dst_dims[1] // 2
                e.dma_start(dst[:, :, half:], src[1]).then_inc(right_landed[slot], 16)
                dst, src = dst[:, :, :half], src[0]
            e.dma_start(dst, src).then_inc(landed[slot], 16)

        def split_hi(e, U, quad, slot, n):
            e.wait_ge(landed[slot], quad * 16 + 16)
            e.wait_ge(sem["unit_used"], U + 1)
            e.activation(w_hi[:, slot % 2, :n], raw[:, slot, :n], ACT.Copy).then_inc(sem["hi_made"], 1)

        def split_lo(e, U, slot, n):
            e.wait_ge(sem["hi_made"], U + 1)
            e.tensor_tensor(w_lo[:, slot % 2, :n], raw[:, slot, :n],
                            w_hi[:, slot % 2, :n].bitcast(F32), ALU.subtract).then_inc(sem["lo_made"], 1)

        def split_early(engine, halves=False):
            U = state["unit"]
            state["early"].add(engine)
            if engine == "act":
                def run(e, i):
                    if halves:
                        e.wait_ge(right_landed[U % 4], 16)
                    split_hi(e, U, U // 4, U % 4, 2048)
            else:
                def run(e, i):
                    split_lo(e, U, U % 4, 2048)
            prog.once(0, {engine: run})

        def three_pass(e, ps, l_hi, l_lo, r_hi, r_lo, start, stop, skip=False):
            e.matmul(ps, l_hi, r_hi, start=start, stop=False, skip_group_check=skip)
            e.matmul(ps, l_hi, r_lo, start=False, stop=False, skip_group_check=skip)
            return e.matmul(ps, l_lo, r_hi, start=False, stop=stop, skip_group_check=skip)

        def products(name, src, n_groups, evac_act, evac_dve, tok_cols=None, ch_cols=None, n_cols=512,
                     units=4, kb_per_unit=4, after=(), rolled=True, evac_after=(), finish=None, halves=False, more=False,
                     taken_before=False, fill=None):
            U0, G0 = state["unit"], state["group"]
            state["unit"] += units * n_groups
            state["group"] += n_groups
            n = kb_per_unit * n_cols
            before, state["left"] = state["left"], None
            early, state["early"] = state["early"], set()
            wait("pe", *after)
            wait("act", *evac_after)
            wait("dve", *evac_after)

            def group(g, parity, U, quad, first_slot):
                bank = [2 * parity, 2 * parity + 1]

                def sp(e):
                    for j in range(units):
                        load_unit(e, U + j, (first_slot + j) % 4, (kb_per_unit, n_cols), src(g, j))

                def act(e, j):
                    if "act" in early and isinstance(g, int) and g == j == 0:
                        return
                    if halves:
                        e.wait_ge(right_landed[j], g * 16 + 16)
                    split_hi(e, U + j, quad, (first_slot + j) % 4, n)

                def dve(e, j):
                    if "dve" in early and isinstance(g, int) and g == j == 0:
                        return
                    split_lo(e, U + j, (first_slot + j) % 4, n)

                def pe(e, js=range(units)):
                    if 0 in js:
                        e.wait_ge(sem["act_evac"], G0 + g + 1)
                        e.wait_ge(sem["dve_evac"], G0 + g + 1)
                    for j in js:
                        slot = (first_slot + j) % 2
                        e.wait_ge(sem["lo_made"], LO_CREDIT + U + j + 1)
                        wh = w_hi[:, slot, :n].rearrange("p (k n) -> p k n", k=kb_per_unit)
                        wl = w_lo[:, slot, :n].rearrange("p (k n) -> p k n", k=kb_per_unit)
                        last = None
                        if tok_cols:
                            c0, w = tok_cols
                            at_once = bool(ch_cols)
                            for t in range(TB):
                                for k in range(kb_per_unit):
                                    kk = j * kb_per_unit + k
                                    o = (PS[:, bank[1], t * w:(t + 1) * w] if at_once
                                         else PS[:, bank[t], :w])
                                    last = three_pass(
                                        e, o, h_hi[:, kk, t * P:(t + 1) * P], h_lo[:, kk, t * P:(t + 1) * P],
                                        wh[:, k, c0:c0 + w], wl[:, k, c0:c0 + w],
                                        kk == 0 and not (at_once and t), kk == units * kb_per_unit - 1,
                                        at_once)
                        if ch_cols:
                            c0, w = ch_cols
                            for c in range(w // P):
                                for k in range(kb_per_unit):
                                    kk = j * kb_per_unit + k
                                    o = PS[:, bank[c // 2], (c % 2) * S:(c % 2 + 1) * S]
                                    ws = slice(c0 + c * P, c0 + (c + 1) * P)
                                    last = three_pass(e, o, wh[:, k, ws], wl[:, k, ws], h_hi[:, kk, :],
                                                      h_lo[:, kk, :], kk == 0 and c % 2 == 0,
                                                      kk == units * kb_per_unit - 1, True)
                        last.then_inc(sem["unit_used"], 1)

                def evac(e, which):
                    e.wait_ge(sem["unit_used"], UNIT_CREDIT + U + units)
                    fn, b = (evac_act, 0) if which == "act" else (evac_dve, 1)
                    fn(e, g, parity if finish else PS[:, bank[b], :]).then_inc(sem[which + "_evac"], 1)

                def end(e, which):
                    if finish:
                        finish[which](e, g, parity)

                return {"sp": sp, "act": act, "dve": dve, "pe": pe, "evac": evac, "end": end}

            def at(g):
                U = U0 + units * g
                return group(g, (G0 + g) % 2, U, U // 4, U % 4)

            def splitter(which):
                def one(e, g, grp, prev):
                    for j in range(units):
                        grp[which](e, j)
                        if j == min(1, units - 1) and prev is not None:
                            prev["evac"](e, which)
                    if prev is not None:
                        prev["end"](e, which)
                return one

            if fill:
                assert not rolled and units > 1
                for g in range(n_groups):
                    grp, prev = at(g), at(g - 1) if g else before
                    prog.once(0, {"sp": lambda e, i, q=grp: q["sp"](e)})
                    for j in range(units):
                        prog.once(0, {"pe": lambda e, i, q=grp, j=j: q["pe"](e, (j,)),
                                      "act": lambda e, i, q=grp, j=j: q["act"](e, j),
                                      "dve": lambda e, i, q=grp, j=j: q["dve"](e, j)})
                        if j == 1 and prev is not None:
                            prog.once(0, {w: lambda e, i, w=w, q=prev: q["evac"](e, w) for w in ("act", "dve")})
                            assert not finish
                        next(fill, None)
                last_group = at(n_groups - 1)
            elif units == 1:
                for g in range(n_groups):
                    grp, prev = at(g), at(g - 1) if g else before
                    prog.once(0, {"sp": lambda e, i, q=grp: q["sp"](e), "pe": lambda e, i, q=grp: q["pe"](e),
                                  "act": lambda e, i, g=g, q=grp, p=prev: splitter("act")(e, g, q, p),
                                  "dve": lambda e, i, g=g, q=grp, p=prev: splitter("dve")(e, g, q, p)})
                last_group = at(n_groups - 1)
            else:
                for which in ("act", "dve"):
                    prog.once(0, {which: lambda e, i, w=which: splitter(w)(e, 0, at(0), before)})
                prog.once(0, {"sp": lambda e, i: at(0)["sp"](e), "pe": lambda e, i: at(0)["pe"](e)})
                pairs = (n_groups - 1) // 2 if rolled else 0
                if pairs < 2:
                    pairs = 0

                def body(engine):
                    def run(e, i):
                        for k in range(2):
                            g = i * 2 + (1 + k)
                            U = i * (2 * units) + (U0 + units * (1 + k))
                            quad = i * 2 + (U0 // 4 + 1 + k)
                            grp = group(g, (G0 + 1 + k) % 2, U, quad, U0 % 4)
                            if engine in ("act", "dve"):
                                Up = i * (2 * units) + (U0 + units * k)
                                gp = i * 2 + k
                                prev = group(gp, (G0 + k) % 2, Up, quad, U0 % 4)
                                splitter(engine)(e, g, grp, prev)
                            else:
                                grp[engine](e)
                    return run

                if pairs:
                    prog.loop(pairs, {en: body(en) for en in ("sp", "pe", "act", "dve")})
                for g in range(1 + 2 * pairs, n_groups):
                    grp, prev = at(g), at(g - 1)
                    prog.once(0, {"sp": lambda e, i, q=grp: q["sp"](e), "pe": lambda e, i, q=grp: q["pe"](e),
                                  "act": lambda e, i, g=g, q=grp, p=prev: splitter("act")(e, g, q, p),
                                  "dve": lambda e, i, g=g, q=grp, p=prev: splitter("dve")(e, g, q, p)})
                last_group = at(n_groups - 1)
            if more:
                state["left"] = last_group
            else:
                prog.once(0, {w: lambda e, i, w=w, q=last_group: (q["evac"](e, w), q["end"](e, w))
                              for w in ("act", "dve")})
            G1, U1 = (G0, U0) if taken_before else (state["group"], state["unit"])
            return [(sem["act_evac"], EVAC_CREDIT + G1), (sem["dve_evac"], EVAC_CREDIT + G1),
                    (sem["unit_used"], UNIT_CREDIT + U1)]

        def w_cols(w, col0, stride=512, n_cols=512):
            v = w.rearrange("(k p) n -> p k n", p=P)
            return lambda g, j: v[:, 4 * j:4 * j + 4, bass.ds(g * stride + col0, n_cols)]

        def evac_pair(dst_a, dst_b):
            def act(e, g, bank):
                d = dst_a(g)
                return e.activation(d, bank[:, :_n(d)], ACT.Copy)

            def dve(e, g, bank):
                d = dst_b(g)
                return e.tensor_copy(d, bank[:, :_n(d)])
            return act, dve

        def _n(ap):
            return int(np.prod(ap.shape[1:]))

        def to_tokens(dst, col0):
            return evac_pair(lambda g: dst[:, 0, bass.ds(g * 512 + col0, 512)],
                             lambda g: dst[:, 1, bass.ds(g * 512 + col0, 512)])

        def to_channels(at, blk0):
            return evac_pair(lambda g: arena[:, bass.ds(g * 1024 + (at + blk0 * S), 512)],
                             lambda g: arena[:, bass.ds(g * 1024 + (at + blk0 * S + 512), 512)])

        work_bank_free = {b: [] for b in (4, 5, 6, 7)}
        bank_turn = [0]

        def next_bank():
            b = 4 + bank_turn[0] % 4
            bank_turn[0] += 1
            return b

        def fence_banks():
            f = prog.all_done()
            for b in work_bank_free:
                work_bank_free[b] = list(f)
            return f

        lanes = [dict(bank=n, s=sp_(1024 * n, 512), p=sp_(1024 * n + 512, 512),
                      stat=(col(2), col(2), col(2)), free=[]) for n in range(8)]

        def side_by_side(*jobs):
            while jobs:
                jobs = [job for job in jobs if next(job, "end") != "end"]
                yield

        def run_lanes(*groups):
            running = [(lane, None, jobs) for on, jobs in ((on, list(jobs)) for on, jobs in groups) for lane in on]
            while running:
                later = []
                for lane, job, jobs in running:
                    if job is None:
                        if not jobs:
                            continue
                        job = jobs.pop(0)(lane)
                    later.append((lane, None if next(job, "end") == "end" else job, jobs))
                running = later

        minus_half = col(1)
        t_half = do("dve", lambda e: e.memset(minus_half, -0.5))

        def power_minus_half(c, n, after):
            return do("pool", lambda e: e.tensor_tensor(c, c, minus_half.to_broadcast([P, n]), ALU.pow),
                      after, t_half)

        def rstd_of(ssq, out_col, width, eps, n, after):
            t = do("dve", lambda e: e.tensor_scalar(out_col, ssq, 1.0 / width, eps, ALU.mult, ALU.add), after)
            if n <= 8:
                return power_minus_half(out_col, n, t)
            t = do("dve", lambda e: e.reciprocal(out_col, out_col), t)
            return do("act", lambda e: e.activation(out_col, out_col, ACT.Sqrt), t)

        def sum_squares(src, junk, after):
            ssq = col(2)
            a = do("act", lambda e: e.activation(junk(0), src(0), ACT.Square, accum_out=ssq[:, 0:1]), after)
            b = do("dve", lambda e: e.scalar_tensor_tensor(out=junk(1), in0=src(1), scalar=1.0, in1=src(1),
                                                           op0=ALU.mult, op1=ALU.mult,
                                                           accum_out=ssq[:, 1:2]), after)
            return ssq, [a, b]

        def to_h(src, gain, after, n_blocks=KB, ready=None):
            block = src if callable(src) else lambda t, k: src[:, t, k * P:(k + 1) * P]
            hi, lo = h_hi, h_lo
            made = []
            for n in range((n_blocks + 1) // 2):
                b = next_bank()
                ks = [k for k in (2 * n, 2 * n + 1) if k < n_blocks]
                wait("pe", *after, *work_bank_free[b], [ready(k) for k in ks] if ready else None)
                for k in ks:
                    for t in range(TB):
                        fn = (lambda e, k=k, t=t, b=b: e.transpose(
                            PS[:, b, ((k % 2) * 2 + t) * P:((k % 2) * 2 + t + 1) * P],
                            block(t, k), ident[:, :]))
                        tok = do("pe", fn) if (k, t) == (ks[-1], TB - 1) else quiet("pe", fn)
                free = []
                if gain is None:
                    m = len(ks) * S
                    dh = hi[:, ks[0]:ks[-1] + 1, :].rearrange("p k n -> p (k n)")
                    dl = lo[:, ks[0]:ks[-1] + 1, :].rearrange("p k n -> p (k n)")
                    a = do("act", lambda e, b=b, dh=dh, m=m: e.activation(dh, PS[:, b, :m], ACT.Copy), tok, after)
                    v = do("dve", lambda e, b=b, dh=dh, dl=dl, m=m: e.tensor_tensor(
                        dl, PS[:, b, :m], dh.bitcast(F32), ALU.subtract), a)
                    free, made = [a, v], made + [a, v]
                else:
                    half = {k: PS[:, b, (k % 2) * S:(k % 2 + 1) * S] for k in ks}
                    for k in ks:
                        a = do("act", lambda e, k=k, p=half[k]: e.activation(hi[:, k, :], p, ACT.Copy,
                                                                             scale=gain(k)), tok, after)
                    for k in ks:
                        v = do("dve", lambda e, k=k, p=half[k]: e.scalar_tensor_tensor(
                            out=lo[:, k, :], in0=p, scalar=gain(k), in1=hi[:, k, :].bitcast(F32),
                            op0=ALU.mult, op1=ALU.subtract), a)
                    free, made = [a, v], made + [a, v]
                work_bank_free[b] = free
            return [made[-1], made[-2]]

        def norm_to_h(src, scaled, gain, after, early_act=False):
            done = []
            for step, _ in enumerate(scaled_rows(src, scaled, done, after)):
                if step == 0 and early_act:
                    split_early("act")
            split_early("dve")
            return to_h(scaled, gain, [after], ready=lambda k: done[min(k // 4, 2)])

        def scaled_rows(src, scaled, done, after):
            ssq, t = sum_squares(lambda t: src[:, t, :], lambda t: scaled[:, t, :], after)
            rstd = col(2)
            yield
            t = rstd_of(ssq, rstd, D, EPS, 2, t)
            yield
            for cs in (slice(0, 512), slice(512, 1024), slice(1024, 2048)):
                done.append([do("act", lambda e, cs=cs: e.activation(scaled[:, 0, cs], src[:, 0, cs], ACT.Copy,
                                                                     scale=rstd[:, 0:1]), t),
                             do("dve", lambda e, cs=cs: e.tensor_scalar(scaled[:, 1, cs], src[:, 1, cs],
                                                                        rstd[:, 1:2], None, ALU.mult), t)])
                yield

        def sandwich(y, cat, g_bcast, ssq4, t_gain):
            def chunk(a, t, g):
                return a[:, t, bass.ds(g * 512, 512)]

            def ga(g):
                return g_bcast[:, bass.ds(g * 512, 512)]

            def evac_act(e, g, bank):
                e.activation(chunk(squares, 0, g), bank, ACT.Square, accum_out=ssq4[:, 0, bass.ds(g, 1)])
                return e.activation(chunk(cat, 0, g), bank, ACT.Copy)

            def evac_dve(e, g, bank):
                e.tensor_tensor(chunk(y, 1, g), bank, ga(g), ALU.mult)
                return e.tensor_copy(chunk(cat, 1, g), bank)

            G0 = state["group"]

            def end_act(e, g, parity):
                e.wait_ge(sem["dve_evac"], EVAC_CREDIT + G0 + g + 1)
                e.activation(chunk(squares, 1, g), chunk(cat, 1, g), ACT.Square,
                             accum_out=ssq4[:, 1, bass.ds(g, 1)]).then_inc(sem["squared"], 1)

            def end_dve(e, g, parity):
                e.wait_ge(sem["act_evac"], EVAC_CREDIT + G0 + g + 1)
                e.tensor_tensor(chunk(y, 0, g), chunk(cat, 0, g), ga(g), ALU.mult).then_inc(sem["gained"], 1)
            squares = ar(SQUARES, TB, D)
            n_squared[0] += 4
            n_gained[0] += 4
            return dict(evac=(lambda e, g, p: evac_act(e, g, PS[:, 2 * p, :]), lambda e, g, p: evac_dve(e, g, PS[:, 2 * p + 1, :])),
                        finish={"act": end_act, "dve": end_dve},
                        done=[(sem["squared"], n_squared[0]), (sem["gained"], n_gained[0])])

        def add_normed(y, ssq, after):
            rstd = col(2)
            t = do("dve", lambda e: e.tensor_reduce(rstd, ssq, AX.X, ALU.add), after)
            t = rstd_of(rstd, rstd, D, EPS, 2, t)
            return [do("dve", lambda e, tb=tb: e.scalar_tensor_tensor(
                out=x[:, tb, :], in0=y[:, tb, :], scalar=rstd[:, tb:tb + 1], in1=x[:, tb, :], op0=ALU.mult,
                op1=ALU.add), t) for tb in range(TB)]

        Z_QK, Z_V, Z_B, Z_C = 0, 3072, 4608, 6656
        CAT = 12032
        K_MEM, V_MEM = 16128, 17152
        HANKEL = 18176
        SQUARES = 4096
        GAINS = 20352
        cat = ar(CAT, TB, D)
        gains = ar(GAINS, D)

        t_mem = dma("act", ar(0, TB, D), I["mem"][0].rearrange("(t p) d -> p t d", p=P), "mem_in")
        wait("sp", t_mem)
        dma("act", params[:, :], I["params"], "consts")
        dma("act", ident[:, :], I["ident"], "consts")
        t_const = dma("act", exch[:, :], I["exch"], "consts")
        for engine, name, n in (("sp", "lo_made", LO_CREDIT), ("pe", "unit_used", UNIT_CREDIT),
                                ("act", "act_evac", EVAC_CREDIT), ("dve", "dve_evac", EVAC_CREDIT)):
            prog.queue[engine].append(lambda e, i, s=sem[name], n=n: e.sem_inc(s, n))

        TBL, ONEHOT, WROW = 21248, 21264, 21648
        t_one = do("dve", lambda e: e.memset(arena[32:33, TBL:TBL + A_H], 1.0))
        dma("act", arena[0:REL, TBL:TBL + A_H], I["rel_bias_table"], "rel_in")
        t_rel = dma("act", arena[0:REL + 1, ONEHOT:ONEHOT + 384], I["onehot"], "rel_in")
        b = next_bank()
        t = do("pe", lambda e, b=b: e.matmul(PS[0:A_H, b, 0:384], arena[0:REL + 1, TBL:TBL + A_H],
                                        arena[0:REL + 1, ONEHOT:ONEHOT + 384], start=True, stop=True),
               t_one, t_rel, work_bank_free[b])
        t = do("dve", lambda e, b=b: e.tensor_copy(arena[0:A_H, WROW:WROW + 384], PS[0:A_H, b, 0:384]), t)
        work_bank_free[b] = [t]
        scratch = I["scratch"]
        t_rows = dma("act", scratch, arena[0:A_H, WROW:WROW + 384], "rel_out", t)

        t_h = norm_to_h(ar(0, TB, D), cat, lambda k: par("g_src", k), [t_mem, t_const], early_act=True)
        hankel = ar(HANKEL, A_H, S)
        t_hankel = dma("act", hankel, bass.AP(scratch.tensor, 0, [[1, P], [384, A_H], [1, S]]), "rel_back", t_rows)
        kv = w_cols(I["mem_wkv"][0], 0)
        products("mem_k", kv, 1, *to_channels(K_MEM, 0), ch_cols=(0, 512), after=t_h, more=True)
        t_x = dma("sp", x[:, :, :], I["x"][0].rearrange("(t p) d -> p t d", p=P), "x_in")
        kv2 = w_cols(I["mem_wkv"][0], M_I)
        v_mem = ar(V_MEM, TB, M_I)
        x_rows = []
        fill = scaled_rows(x, cat, x_rows, [t_x, t_h])
        t_used = products("mem_v", kv2, 1, *to_tokens(v_mem, 0), tok_cols=(0, 512), rolled=False, fill=fill)
        for _ in fill:
            pass

        for engine in ("act", "dve"):
            split_early(engine)
        t_h = to_h(cat, lambda k: par("g_mix", k), [t_used], ready=lambda k: x_rows[min(k // 4, 2)])
        w_in = I["w_in"][0]
        z_v, z_b = ar(Z_V, TB, A_W), ar(Z_B, TB, 2 * B_W)
        def vb(t):
            def f(e, g, bank):
                if t == 0:
                    e.activation(z_v[:, t, 512:768], bank[:, 0:256], ACT.Copy)
                    return e.activation(z_b[:, t, 0:256], bank[:, 256:512], ACT.Copy)
                e.tensor_copy(z_v[:, t, 512:768], bank[:, 0:256])
                return e.tensor_copy(z_b[:, t, 0:256], bank[:, 256:512])
            return f
        products("bc", w_cols(w_in, 3 * A_W + 768), 1,
                 lambda e, g, bank: e.activation(ar(Z_C, 512), bank, ACT.Copy),
                 lambda e, g, bank: e.tensor_copy(z_b[:, :, 768:1024],
                                                  bank.rearrange("p (t n) -> p t n", t=TB)),
                 tok_cols=(0, 256), ch_cols=(256, 256), after=t_h, evac_after=t_h, more=True)
        C0 = 3 * A_W + 2 * B_W
        products("c", w_cols(w_in, C0 + 256), 4, *to_channels(Z_C, 2), ch_cols=(0, 512), more=True)
        products("c_end", w_cols(w_in, C0 + 256 + 2048, n_cols=384), 1,
                 *evac_pair(lambda g: ar(Z_C + 18 * S, 512), lambda g: ar(Z_C + 20 * S, 256)),
                 ch_cols=(0, 384), n_cols=384, more=True)
        t_c_out = products("vb", w_cols(w_in, 2 * A_W + 512), 1, vb(0), vb(1), tok_cols=(0, 512), more=True,
                           taken_before=True)
        zc = ar(Z_C, 21, S)
        vt = cat[:, :, A_W + B_W:]

        def shift(k0, k1, turn):
            diff, z = ar(CAT + (A_W + B_W) * turn, k1 - k0, S), zc[:, k0:k1, :]
            t1 = do("dve", lambda e: e.tensor_tensor(diff[:, :, 1:], z[:, :, :S - 1], z[:, :, 1:], ALU.subtract),
                    t_c_out, t_shift)
            t2 = do("dve", lambda e: e.tensor_scalar(diff[:, :, 0:1], z[:, :, 0:1], -1.0, None, ALU.mult))
            yield
            for k in range(k0, k1):
                t = do("dve", lambda e, k=k: e.scalar_tensor_tensor(
                    out=zc[:, k, :], in0=diff[:, k - k0, :], scalar=par("mu", k), in1=zc[:, k, :],
                    op0=ALU.mult, op1=ALU.add), t1, t2)
            t_shift[:] = [t]
            yield

        def v_to_tokens(n, b):
            wait("pe", t_shift, work_bank_free[b])
            for k in range(2):
                for t_ in range(TB):
                    fn = lambda e, k=k, t_=t_: e.transpose(
                        PS[:, b, (t_ * 2 + k) * P:(t_ * 2 + k + 1) * P],
                        zc[:, 12 + 2 * n + k, t_ * P:(t_ + 1) * P], ident[:, :])
                    t = do("pe", fn) if k and t_ else quiet("pe", fn)
            yield
            t = do("act", lambda e: e.activation(
                vt[:, :, 2 * n * P:(2 * n + 2) * P], PS[:, b, :].rearrange("p (t n) -> p t n", t=TB),
                ACT.Copy), t, t_shift)
            work_bank_free[b] = [t]
            t_v.append(t)
            yield

        def prepare_c():
            for turn, k0 in enumerate((18, 15, 12, 0, 3, 6, 9)):
                yield from shift(k0, k0 + 3, turn % 2)
            t_act.append(do("act", lambda e: e.activation(zc[0:HD, 18, :], zc[0:HD, 18, :], ACT.Tanh), t_shift))
            t_act.append(do("act", lambda e: e.activation(zc[:, 19:21, :], zc[:, 19:21, :], ACT.Sigmoid), t_shift))
            yield
            for n in range(CB // 2):
                yield from v_to_tokens(n, next_bank())

        SW, SBIAS = 21248, 22272
        ln_gain = cat[:, 1, 0:B_W]
        dma("act", ar(SW, B_G, P), I["sgu_w"][0].rearrange("g i j -> i g j"), "sgu_in", t_hankel)
        dma("act", ar(SBIAS, B_G), I["sgu_b_t"], "sgu_in")
        t_sg = dma("act", ln_gain, bcast("sgu_norm_gain", 0, B_W), "sgu_in", t_h)

        def norm_part(c0, w, junk, after):
            ssq, t = sum_squares(lambda t_: cat[:, t_, c0:c0 + w], junk, after)
            rstd = col(2)
            t = rstd_of(ssq, rstd, w, EPS, 2, t)
            return [do("dve", lambda e, t_=t_: e.tensor_scalar(
                cat[:, t_, c0:c0 + w], cat[:, t_, c0:c0 + w], rstd[:, t_:t_ + 1], None, ALU.mult), t)
                for t_ in range(TB)]

        def spatial_gating():
            wt = ar(SW, B_G, P)
            t_w = []
            for n in range(2):
                yield from mixing_matrices(n, next_bank(), wt, t_w)
            t = [do("act", lambda e, t_=t_: e.activation(z_b[:, t_, :], z_b[:, t_, :], ACT.Gelu_apprx_tanh), t_b_out)
                 for t_ in range(TB)]
            mean, var = col(2), col(2)
            yield
            t1 = [do("dve", lambda e, t_=t_: e.tensor_reduce(mean[:, t_:t_ + 1], z_b[:, t_, B_W:], AX.X, ALU.add), t)
                  for t_ in range(TB)]
            t1 = do("dve", lambda e: e.tensor_scalar(mean, mean, 1.0 / B_W, None, ALU.mult), t1)
            yield
            t1 = [do("dve", lambda e, t_=t_: e.tensor_scalar(z_b[:, t_, B_W:], z_b[:, t_, B_W:],
                                                             mean[:, t_:t_ + 1], None, ALU.subtract), t1)
                  for t_ in range(TB)]
            yield
            ssq, t1 = sum_squares(lambda t_: z_b[:, t_, B_W:], lambda t_: cat[:, t_, A_W:A_W + B_W], t1)
            yield
            t1 = rstd_of(ssq, var, B_W, EPS, 2, t1)
            yield
            t1 = [do("dve", lambda e, t_=t_: e.scalar_tensor_tensor(
                out=z_b[:, t_, B_W:], in0=z_b[:, t_, B_W:], scalar=var[:, t_:t_ + 1], in1=ln_gain,
                op0=ALU.mult, op1=ALU.mult), t1, t_sg) for t_ in range(TB)]
            yield
            for n in range(2):
                yield from mix_groups(n, next_bank(), wt, [t_w, t1])
            yield
            norm_part(A_W, B_W, lambda t_: z_b[:, t_, 0:B_W], [t_gated_b])
            yield

        def mixing_matrices(n, b, wt, made):
            part = wt[:, 4 * n:4 * n + 4, :]
            wait("pe", t_sg, work_bank_free[b])
            for g in range(4):
                fn = lambda e, g=g: e.transpose(PS[:, b, g * P:(g + 1) * P], part[:, g, :], ident[:, :])
                t = do("pe", fn) if g == 3 else quiet("pe", fn)
            yield
            t = do("act", lambda e: e.activation(part.rearrange("p g i -> p (g i)"), PS[:, b, :], ACT.Copy), t)
            work_bank_free[b] = [t]
            made.append(do("pool", lambda e: e.affine_select(
                out=part, in_=part, compare_op=ALU.is_ge, fill=0.0, base=0, pattern=[[0, 4], [1, P]],
                channel_multiplier=-1), t))
            yield

        t_gated_b = []
        def mix_groups(n, b, wt, after):
            wait("pe", after, work_bank_free[b])
            for g in range(4):
                fn = lambda e, g=g: e.matmul(
                    PS[:, b, g * P:(g + 1) * P], wt[:, 4 * n + g, :],
                    z_b[:, :, B_W + (4 * n + g) * HD:B_W + (4 * n + g + 1) * HD], start=True, stop=True)
                t = do("pe", fn) if g == 3 else quiet("pe", fn)
            yield
            c0, w = A_W + 4 * n * HD, 4 * HD
            bias = ar(SBIAS, B_G)[:, 4 * n:4 * n + 4].unsqueeze(2).to_broadcast([P, 4, HD])
            for t_ in range(TB):
                t = do("dve", lambda e, t_=t_: e.tensor_tensor(
                    cat[:, t_, c0:c0 + w].rearrange("p (g n) -> p g n", g=4),
                    PS[:, b, :].rearrange("p (g t n) -> p g t n", g=4, t=TB)[:, :, t_, :], bias, ALU.add),
                    t, t_shift, t_sg)
                t_gated_b.append(do("dve", lambda e, t_=t_: e.tensor_tensor(
                    cat[:, t_, c0:c0 + w], cat[:, t_, c0:c0 + w], z_b[:, t_, 4 * n * HD:4 * n * HD + w],
                    ALU.mult), t))
            work_bank_free[b] = [t]
            yield

        t_shift, t_act, t_v, t_b_out = [], [], [], []
        fill = prepare_c()
        t_b_out += products("b1", w_cols(w_in, 3 * A_W + 256), 1, *to_tokens(z_b, 256), tok_cols=(0, 512), more=True,
                            rolled=False, fill=fill)
        fill = side_by_side(fill, spatial_gating())
        products("qk", w_cols(w_in, 0), 3, *to_channels(Z_QK, 0), ch_cols=(0, 512), more=True, rolled=False,
                 fill=fill)
        t_z = products("v0", w_cols(w_in, 2 * A_W), 1, *to_tokens(z_v, 0), tok_cols=(0, 512), rolled=False,
                       fill=fill)
        for _ in fill:
            pass
        t_tanh, t_sig = t_act

        zqk = ar(Z_QK, 12, S)
        LORA = 4608
        MASKS, PAIR = 6144, 7426
        GUP, YT, LE = 4608, 0, 3584
        LNG, LNB = 6144, 6912
        wait("sp", t_z)
        dma("sp", sp_(MASKS, 1282), I["masks"], "masks_in")
        t_masks = dma("sp", sp_(PAIR, 512).bitcast(I32), I["pair_mask"], "masks_in")
        fence = prog.all_done()
        dma("sp", arena[0:HD, LORA:LORA + C_W], I["rwkv_w_up"][0], "lora_in", fence)
        t_lora = dma("sp", arena[HD:P, LORA:LORA + C_W], I["rwkv_a_up"][0], "lora_in")
        t_gup = dma("sp", rw(GUP, 2, C_W), I["rwkv_g_up"][0].rearrange("(k p) n -> p k n", p=P), "g_up_in")
        dma("sp", rw(LNG, C_W), bcast("rwkv_ln_gain", 0, C_W), "ln_in")
        t_ln = dma("sp", rw(LNB, C_W), bcast("rwkv_ln_bias", 0, C_W), "ln_in")
        gup = rw(GUP, 2, C_W)
        level_mask = lambda l: sp_(MASKS + P * l, P)
        level0_t = sp_(MASKS + 7 * P, P)
        head_two = sp_(MASKS + 9 * P, 2)
        all_ones = sp_(MASKS + 9 * P + 2, P)
        pair_mask = sp_(PAIR, 512).bitcast(I32)

        def rwkv_lane(banks, mem, mats, r=None, sa=None, s1=None, solve=None, le=None):
            at_, first = mem
            return dict(banks=banks, mats=mats, kk=at_(first, S), a=at_(first + S, S), bt=at_(first + 2 * S, S),
                        r=r[0](r[1], 2, P), sa=sa[0](sa[1], 2, P), s1=s1[0](s1[1], P),
                        X=solve[0](solve[1], 4, P), XT=solve[0](solve[1] + 512, 4, P),
                        U=solve[0](solve[1] + 1024, 4, P), L=le[0](le[1], S), E=le[0](le[1] + S, S), free=[])
        sets = [rwkv_lane((4, 5), (sd, 2048), sd(0, 4, 4, P), r=(sd, 2816), sa=(sd, 3072), s1=(sd, 3328),
                          solve=(sd, 3456), le=(rw, LE)),
                rwkv_lane((6, 7), (sd, 7040), sd(4992, 4, 4, P), r=(rw, 3072), sa=(rw, 3328), s1=(sd, 7808),
                          solve=(rw, 1536), le=(rw, LE + 512)),
                rwkv_lane((0, 1), (sp_, 0), sp_(4096, 4, 4, P), r=(sp_, 768), sa=(sp_, 1024), s1=(ar, 5376),
                          solve=(sp_, 1280), le=(sp_, 2816))]
        for st in sets:
            do("pool", lambda e, m=st["s1"]: e.memset(m, 0.0), t_z, fence)
            st["zeroed"] = do("pool", lambda e, m=st["mats"]: e.memset(m, 0.0))

        def dilated_head(h, lane):
            rows = slice(HD * (h % 2), HD * (h % 2) + HD)
            bank, free = lane["bank"], lane["free"]
            p_, pt_ = lane["p"][:, 0:384], lane["s"][:, 0:384]
            nm, den, _ = lane["stat"]
            blk, kblk = zqk[:, h // 2, :], zqk[:, 6 + h // 2, :]
            wait("pe", t_z, t_hankel, free)
            for t_, (o, w) in enumerate(((0, P), (P, S))):
                quiet("pe", lambda e, t_=t_, o=o, w=w: e.matmul(
                    PS[:, bank, o:o + w], blk[rows, t_ * P:(t_ + 1) * P], kblk[rows, 0:w], start=True, stop=False))
                t_s = do("pe", lambda e, o=o, w=w: e.matmul(
                    PS[:, bank, o:o + w], exch[:, :], hankel[:, h, S - w:S], start=False, stop=True))
            yield
            t1 = do("dve", lambda e: e.tensor_reduce(nm[:, 0:1], PS[:, bank, 0:P], AX.X, ALU.max), t_s, free)
            t2 = do("dve", lambda e: e.tensor_reduce(nm[:, 1:2], PS[:, bank, P:384], AX.X, ALU.max))
            t3 = do("dve", lambda e: e.tensor_scalar(nm, nm, -0.125, None, ALU.mult), t1, t2)
            t_e = [do("act", lambda e, t_=t_, o=o, w=w: e.activation(
                p_[:, o:o + w], PS[:, bank, o:o + w], ACT.Exp, bias=nm[:, t_:t_ + 1], scale=0.125,
                accum_out=den[:, t_:t_ + 1]), t3, free) for t_, (o, w) in enumerate(((0, P), (P, S)))]
            yield
            wait("pe", t_e)
            for o in range(3):
                fn = lambda e, o=o: e.transpose(PS[:, bank, o * P:(o + 1) * P], p_[:, o * P:(o + 1) * P], ident[:, :])
                t_t = do("pe", fn) if o == 2 else quiet("pe", fn)
            yield
            t_r = do("dve", lambda e: e.reciprocal(den, den), t_e)
            t_c = do("act", lambda e: e.activation(pt_, PS[:, bank, 0:384], ACT.Copy), t_t)
            yield
            wait("pe", t_c)
            vp = slice((h // 2) * P, (h // 2) * P + P)
            quiet("pe", lambda e: e.matmul(PS[:, bank, 0:P], pt_[:, 0:P], z_v[:, 0, vp], start=True, stop=True))
            quiet("pe", lambda e: e.matmul(PS[:, bank, P:2 * P], pt_[:, P:2 * P], z_v[:, 0, vp], start=True, stop=False))
            t_o = do("pe", lambda e: e.matmul(PS[:, bank, P:2 * P], pt_[:, 2 * P:3 * P], z_v[:, 1, vp], start=False,
                                              stop=True))
            yield
            done = [do("dve", lambda e, t_=t_: e.tensor_scalar(
                cat[:, t_, h * HD:(h + 1) * HD], PS[:, bank, t_ * P + (h % 2) * HD:t_ * P + (h % 2) * HD + HD],
                den[:, t_:t_ + 1], None, ALU.mult), t_o, t_r) for t_ in range(TB)]
            lane["free"] = [t_o, t_c, done]

        yt = rw(YT, TB, C_W)
        one_minus_ka, bonus = col(CB), col(2 * C_H)
        t_ka = do("dve", lambda e: e.tensor_scalar(one_minus_ka, params[:, PARAM_AT["k_a"]:PARAM_AT["k_a"] + CB],
                                                   -1.0, 1.0, ALU.mult, ALU.add), fence)
        bonus3 = bonus.rearrange("p (t h) -> p t h", t=TB)
        RATE = math.exp(-0.5)
        bc4 = lambda m: m.unsqueeze(1).to_broadcast([P, 4, P])
        cols2 = {}

        def rwkv_block(b, st):
            A, B = st["banks"]
            if st["banks"] not in cols2:
                cols2[st["banks"]] = (col(2), col(2), col(1), col(2 * TB), col(2 * TB), col(2 * TB))
            mats, X, XT, U, kk, a, L, E = (st[n] for n in ("mats", "X", "XT", "U", "kk", "a", "L", "E"))
            bt, R, SA, S1 = st["bt"], st["r"], st["sa"], st["s1"]
            r, k = zc[:, b, :], zc[:, CB + b, :]
            u0, u1 = U[:, 0:2, :].rearrange("p i t -> p (i t)"), U[:, 2:4, :].rearrange("p i t -> p (i t)")
            bs = slice(b * P, (b + 1) * P)
            free = st["free"]
            t = do("pe", lambda e: e.matmul(PS[:, A, 0:S], arena[0:HD, LORA + b * P:LORA + (b + 1) * P],
                                           zc[0:HD, 18, :], start=True, stop=True), t_lora, t_masks, t_tanh, free)
            t = do("pe", lambda e: e.matmul(PS[:, A, S:2 * S], arena[HD:P, LORA + b * P:LORA + (b + 1) * P],
                                            zc[HD:P, 18, :], start=True, stop=True), t)
            t_s = do("act", lambda e: e.activation(E, PS[:, A, 0:S], ACT.Sigmoid, bias=par("w0", b)), t, free)
            t_a_ = do("act", lambda e: e.activation(a, PS[:, A, S:2 * S], ACT.Sigmoid, bias=par("a0", b)))
            yield
            t_l = [do("dve", lambda e, c=c: e.tensor_tensor_scan(
                L[:, c * P:(c + 1) * P], all_ones, E[:, c * P:(c + 1) * P], 0.0, ALU.mult, ALU.add), t_s)
                for c in range(TB)]
            t_k = do("dve", lambda e: e.tensor_scalar(kk, k, par("k_k", b), None, ALU.mult))
            t = do("act", lambda e: e.activation(u0, kk, ACT.Square), t_k)
            for c in range(TB):
                fn = lambda e, c=c: e.matmul(PS[:, B, 2 * c:2 * c + 2], u0[:, c * P:(c + 1) * P], head_two,
                                             start=True, stop=True)
                t = do("pe", fn, t) if c else quiet("pe", fn, t)
            yield
            t_k1 = do("dve", lambda e: e.tensor_scalar(u1, a, par("k_a", b), one_minus_ka[:, b:b + 1], ALU.mult,
                                                       ALU.add), t_a_, t_ka)
            t_k1 = do("dve", lambda e: e.tensor_tensor(k, k, u1, ALU.mult), t_k1)
            norm = cols2[st["banks"]][3]
            t = do("dve", lambda e: e.tensor_scalar(norm, PS[:, B, 0:2 * TB], 1e-24, None, ALU.max), t, free)
            t = power_minus_half(norm, 2 * TB, t)
            t = do("act", lambda e: e.activation(u1.rearrange("p (c n) -> p c n", n=HD),
                                                 norm.unsqueeze(2).to_broadcast([P, 2 * TB, HD]), ACT.Copy), t, t_k1)
            yield
            for c in range(TB):
                fn = lambda e, c=c: e.matmul(
                    PS[:, B, c * P:(c + 1) * P], u1[:, c * P:(c + 1) * P], ident[:, :], start=True, stop=True)
                t = do("pe", fn, t) if c else quiet("pe", fn, t)
            yield
            t_kk = do("dve", lambda e: e.tensor_tensor(kk, kk, PS[:, B, 0:S], ALU.mult), t, t_k1)
            t = do("dve", lambda e: e.scalar_tensor_tensor(out=u0, in0=r, scalar=par("r_k", b), in1=k,
                                                           op0=ALU.mult, op1=ALU.mult), t_k1)
            for t_ in range(TB):
                fn = lambda e, t_=t_: e.matmul(PS[:, B, S + 2 * t_:S + 2 * t_ + 2], u0[:, t_ * P:(t_ + 1) * P],
                                               head_two, start=True, stop=True)
                t = do("pe", fn, t)
            t_bo = do("dve", lambda e: e.tensor_copy(
                bonus3[:, :, 2 * b:2 * b + 2], PS[:, B, S:S + 4].rearrange("p (t h) -> p t h", t=TB)), t)
            t_b_ = do("dve", lambda e: e.tensor_tensor(a, a, kk, ALU.mult), t_kk)
            plus, minus, end = cols2[st["banks"]][:3]
            mid = L.rearrange("p (c t) -> p c t", c=TB)[:, :, 63]
            t1 = do("dve", lambda e: e.tensor_scalar(plus, mid, RATE, None, ALU.mult), t_l, free)
            t2 = do("dve", lambda e: e.tensor_scalar(minus, mid, -RATE, None, ALU.mult))
            t3 = do("dve", lambda e: e.tensor_scalar(end, L[:, P - 1:P], -RATE, plus[:, 0:1], ALU.mult, ALU.add), t1)
            t3 = do("dve", lambda e: e.tensor_tensor(end, end, minus[:, 1:2], ALU.add), t3, t2)
            t_end = do("act", lambda e: e.activation(end, end, ACT.Exp), t3)
            t_f = [do("act", lambda e, c=c: e.activation(E[:, c * P:(c + 1) * P], L[:, c * P:(c + 1) * P], ACT.Exp,
                                                         scale=RATE, bias=minus[:, c:c + 1]), t1, t2)
                   for c in range(TB)]
            t_g = [do("act", lambda e, c=c: e.activation(u1[:, c * P:(c + 1) * P], L[:, c * P:(c + 1) * P], ACT.Exp,
                                                         scale=-RATE, bias=plus[:, c:c + 1]), t_kk)
                   for c in range(TB)]
            yield
            t_be = do("dve", lambda e: e.tensor_tensor(a, a, E, ALU.mult), t_f, t_b_)
            t_ka_ = do("dve", lambda e: e.tensor_tensor(k, k, E, ALU.mult), t)
            t_rh = do("dve", lambda e: e.tensor_tensor(r, r, u1, ALU.mult), t_g, t)
            t_g = [do("act", lambda e, c=c: e.activation(
                u0[:, c * P + 1:(c + 1) * P], L[:, c * P:(c + 1) * P - 1], ACT.Exp, scale=-RATE,
                bias=plus[:, c:c + 1]), t) for c in range(TB)]
            t_g += [do("act", lambda e: e.activation(u0.rearrange("p (c t) -> p c t", c=TB)[:, :, 0], plus, ACT.Exp))]
            t_al = do("dve", lambda e: e.tensor_tensor(kk, kk, u0, ALU.mult), t_g)
            yield
            t_m, bank_read = [], {A: [t_s, t_a_], B: [t_bo]}
            for i in range(4):
                c, h = i // 2, i % 2
                rows, cs, bank = slice(HD * h, HD * h + HD), slice(c * P, c * P + P), (A, B)[h]
                wait("pe", t_be, t_ka_, t_rh, t_al, bank_read[bank])
                for n, (l, rr) in enumerate(((a, kk), (a, r), (k, kk), (k, r))):
                    fn = lambda e, n=n, l=l, rr=rr, rows=rows, cs=cs, bank=bank: e.matmul(
                        PS[:, bank, n * P:(n + 1) * P], l[rows, cs], rr[rows, cs], start=True, stop=True)
                    t = do("pe", fn) if n == 3 else quiet("pe", fn)
                t = do("dve", lambda e, i=i, bank=bank: e.copy_predicated(
                    mats[:, i, :, :].rearrange("p m t -> p (m t)"), pair_mask, PS[:, bank, :]), t, st["zeroed"],
                    t_masks, free)
                bank_read[bank] = [t]
                t_m.append(t)
            yield
            quiet("pe", lambda e: e.transpose(PS[:, B, 0:P], a[:, 0:P], ident[:, :]), t_m)
            t = do("pe", lambda e: e.transpose(PS[:, B, P:2 * P], k[:, 0:P], ident[:, :]))
            t_bt = do("act", lambda e: e.activation(bt, PS[:, B, 0:2 * P], ACT.Copy), t, free)
            for i in range(4):
                fn = lambda e, i=i: e.transpose(PS[:, A, i * P:(i + 1) * P], mats[:, i, 0, :], ident[:, :])
                t = do("pe", fn) if i == 3 else quiet("pe", fn)
            psA = PS[:, A, :].rearrange("p (i t) -> p i t", i=4)
            psB = PS[:, B, :].rearrange("p (i t) -> p i t", i=4)
            t = do("dve", lambda e: e.tensor_tensor(X, psA, bc4(level_mask(0)), ALU.mult), t, t_al, free)
            t_x_ = do("dve", lambda e: e.tensor_tensor(X, X, bc4(ident[:, :]), ALU.add), t)
            t = do("dve", lambda e: e.tensor_tensor(XT, mats[:, :, 0, :], bc4(level0_t), ALU.mult))
            t_xt = do("dve", lambda e: e.tensor_tensor(XT, XT, bc4(ident[:, :]), ALU.add), t)
            t_b_read = [t_bt]
            yield
            for l in range(1, 7):
                wait("pe", t_x_, t_xt)
                if l > 1:
                    for i in range(4):
                        fn = lambda e, i=i: e.transpose(psB[:, i, :], X[:, i, :], ident[:, :])
                        t = do("pe", fn) if i == 3 else quiet("pe", fn)
                    t_xt = do("act", lambda e: e.activation(XT, psB, ACT.Copy), t)
                    t_b_read = [t_xt]
                for i in range(4):
                    fn = lambda e, i=i: e.matmul(psA[:, i, :], mats[:, i, 0, :], X[:, i, :], start=True, stop=True)
                    t = do("pe", fn) if i == 3 else quiet("pe", fn)
                yield
                t_u = do("dve", lambda e, l=l: e.tensor_tensor(U, psA, bc4(level_mask(l)), ALU.mult), t, t_al)
                wait("pe", t_u, t_b_read)
                for i in range(4):
                    fn = ((lambda e, i=i: e.matmul(psB[:, i, :], XT[:, i, :], U[:, i, :], start=True, stop=True))
                          if l < 6 else
                          (lambda e, i=i: e.matmul(psA[:, i, :], U[:, i, :], XT[:, i, :], start=True, stop=True)))
                    t = do("pe", fn) if i == 3 else quiet("pe", fn)
                yield
                if l < 6:
                    t_x_ = do("dve", lambda e: e.tensor_tensor(X, X, psB, ALU.add), t)
                else:
                    t_xt = do("dve", lambda e: e.tensor_tensor(XT, XT, psA, ALU.add), t)
            def own(bank, c=0):
                return PS[:, bank, :].rearrange("p (q n) -> p q n", n=HD)[:, 4 * c:4 * c + 4:3, :]

            two = lambda ap: ap.rearrange("p (h n) -> p h n", h=2)

            def solve(c, t_state, t_free):
                wait("pe", t_v, t_free, t_state, st["zeroed"])
                for h in range(2):
                    o = PS[:, B, h * P:(h + 1) * P]
                    fn = lambda e, o=o, h=h: e.matmul(o, mats[:, 2 * c + h, 2, :], vt[:, c, bs], start=True, stop=c == 0)
                    t = do("pe", fn) if h and not c else quiet("pe", fn)
                    if c:
                        fn = lambda e, o=o: e.matmul(o, kk[:, P:2 * P], S1, start=False, stop=True)
                        t = do("pe", fn) if h else quiet("pe", fn)
                t = do("act", lambda e: e.activation(two(R[:, c, :]), own(B), ACT.Copy, scale=-1.0), t, free)
                wait("pe", t, t_xt)
                for h in range(2):
                    fn = lambda e, h=h: e.matmul(PS[:, A, h * P:(h + 1) * P], XT[:, 2 * c + h, :], R[:, c, :],
                                                 start=True, stop=True)
                    t = do("pe", fn) if h else quiet("pe", fn)
                return do("dve", lambda e: e.tensor_copy(two(SA[:, c, :]), own(A)), t, free)

            t_sa0 = solve(0, [], t_b_read)
            yield
            quiet("pe", lambda e: e.matmul(PS[:, B, 0:P], bt[:, 0:P], SA[:, 0, :], start=True, stop=False),
                  t_sa0, t_bt)
            t = do("pe", lambda e: e.matmul(PS[:, B, 0:P], bt[:, P:2 * P], vt[:, 0, bs], start=False, stop=True))
            t_st = [do("act", lambda e, h=h: e.activation(
                S1[HD * h:HD * h + HD, HD * h:HD * h + HD], PS[HD * h:HD * h + HD, B, HD * h:HD * h + HD], ACT.Copy,
                scale=end[HD * h:HD * h + HD, :]), t, t_end, st["zeroed"]) for h in range(2)]
            yield
            t_sa1 = solve(1, t_st, [])
            yield
            wait("pe", t_sa1)
            for i in range(4):
                c, o = i // 2, PS[:, B, i * P:(i + 1) * P]
                quiet("pe", lambda e, i=i, c=c, o=o: e.matmul(o, mats[:, i, 1, :], SA[:, c, :], start=True, stop=False))
                fn = lambda e, i=i, c=c, o=o: e.matmul(o, mats[:, i, 3, :], vt[:, c, bs], start=False, stop=c == 0)
                quiet("pe", fn)
                if c:
                    fn = lambda e, o=o: e.matmul(o, r[:, P:2 * P], S1, start=False, stop=True)
                    t = do("pe", fn) if i == 3 else quiet("pe", fn)
            t = [do("act", lambda e, c=c: e.activation(two(yt[:, c, bs]), own(B, c), ACT.Copy), t) for c in range(TB)]
            y_made[b] = [t, t_bo]
            st["free"] = [t, t_sa1, t_end]
            yield
            if b >= len(sets):
                yield from finish_block(b, A, L, E, cols2[st["banks"]][4:6], st)

        def finish_block(b, bank, sq, vb_, stats, lane):
            after, bs = y_made[b], slice(b * P, (b + 1) * P)
            by_head = lambda ap: ap.rearrange("p c (h n) -> p c h n", h=2)
            over = lambda ap: ap.rearrange("p (c h) -> p c h", c=TB).unsqueeze(3).to_broadcast([P, TB, 2, HD])
            wide = lambda a: rw(a + b * P, P).unsqueeze(1).to_broadcast([P, TB, P])
            y, v, out_ = yt[:, :, bs], vt[:, :, bs], cat[:, :, A_W + B_W + b * P:A_W + B_W + (b + 1) * P]
            sq, vb_ = (m.rearrange("p (c n) -> p c n", c=TB) for m in (sq, vb_))
            y4, (mean, var), free = by_head(y), stats, lane["free"]
            seg = lambda col_: col_.rearrange("p (c h) -> p c h", c=TB)
            t_vb = do("pool", lambda e: e.tensor_tensor(
                by_head(vb_), by_head(v), bonus3[:, :, 2 * b:2 * b + 2].unsqueeze(3).to_broadcast([P, TB, 2, HD]),
                ALU.mult), after, free)
            t = do("dve", lambda e: e.tensor_reduce(seg(mean), y4, AX.X, ALU.add), after, free)
            t = do("dve", lambda e: e.tensor_scalar(mean, mean, 1.0 / HD, None, ALU.mult), t)
            t_y = do("dve", lambda e: e.tensor_tensor(y4, y4, over(mean), ALU.subtract), t)
            wait("pe", t_sig, t_gup, after, free)
            for c in range(TB):
                for k_ in range(2):
                    fn = lambda e, c=c, k_=k_: e.matmul(
                        PS[:, bank, c * P:(c + 1) * P], zc[:, 19 + k_, c * P:(c + 1) * P], gup[:, k_, bs],
                        start=k_ == 0, stop=k_ == 1)
                    t_g = do("pe", fn) if c and k_ else quiet("pe", fn)
            yield
            t = do("act", lambda e: e.activation(sq, y, ACT.Square), t_y, free)
            yield
            t = do("dve", lambda e: e.tensor_reduce(seg(var), by_head(sq), AX.X, ALU.add), t)
            t = rstd_of(var, var, HD, GN_EPS, 2 * TB, t)
            yield
            t = do("dve", lambda e: e.tensor_tensor(y4, y4, over(var), ALU.mult), t)
            t = do("dve", lambda e: e.tensor_tensor(y, y, wide(LNG), ALU.mult), t, t_ln)
            t = do("dve", lambda e: e.tensor_tensor(y, y, wide(LNB), ALU.add), t)
            t = do("dve", lambda e: e.tensor_tensor(y, y, vb_, ALU.add), t, t_vb)
            t = do("dve", lambda e: e.tensor_tensor(out_, y, PS[:, bank, 0:S].rearrange("p (c n) -> p c n", c=TB),
                                                    ALU.mult), t, t_g)
            lane["free"] = [t]
            yield

        y_made = {}
        finish_stats = {2: (col(2 * TB), col(2 * TB)), 3: (col(2 * TB), col(2 * TB))}

        def finish_early(b):
            def run(lane):
                while b not in y_made:
                    yield
                yield from finish_block(b, lane["bank"], lane["s"][:, 0:S], lane["p"][:, 0:S],
                                        finish_stats[lane["bank"]], lane)
            return run

        fence = fence_banks()
        head_lanes = [dict(lanes[0], bank=2, s=sp_(3328, 384), p=sp_(3712, 384)),
                      dict(lanes[1], bank=3, s=ar(21248, 384), p=ar(21632, 384))]
        for lane in sets + head_lanes:
            lane["free"] = [t_z, fence]

        def attention_norm(lane):
            norm_part(0, A_W, lambda t_: ar(18176 + t_ * A_W, A_W), [a["free"] for a in head_lanes])
            yield
        run_lanes((sets, [lambda st, b=b: rwkv_block(b, st) for b in range(CB)]),
                  (head_lanes, [lambda lane, h=h: dilated_head(h, lane) for h in range(A_H)] + [attention_norm]
                   + [finish_early(b) for b in range(len(sets))]))

        fence = fence_banks()

        t_gain = dma("sp", gains, bcast("sandwich_gains", 1 * D, D), "gains_in", fence)
        def mix_gain(k):
            return par("attn_gain", k) if k < 6 else par("sgu_gain", k - 6) if k < 10 else 1.0
        t_h = to_h(cat, mix_gain, [fence])
        y = ar(0, TB, D)
        ssq4 = [col(TB * 4).rearrange("p (t g) -> p t g", t=TB) for _ in range(2)]
        out_rows = sandwich(y, cat, gains, ssq4[0], t_gain)
        t_y = products("w_out", w_cols(I["w_out"][0], 0), 4, *out_rows["evac"], tok_cols=(0, 512), after=t_h,
                       evac_after=[t_h, t_gain], finish=out_rows["finish"])
        split_early("act")
        t_xn = add_normed(y, ssq4[0], [t_y, out_rows["done"]])

        def heads(n, pairs, scale, v, put, bias=None, sink=None, after=()):
            def head(h, lane):
                s_, p_ = lane["s"], lane["p"]
                bank, free = lane["bank"], lane["free"]
                nm, den, ex = lane["stat"]
                wait("pe", after, free)
                ops = pairs(h)
                for t_ in range(TB):
                    for m, (q, k) in enumerate(ops):
                        t_s = do("pe", lambda e, t_=t_, q=q, k=k, m=m: e.matmul(
                            PS[:, bank, t_ * S:(t_ + 1) * S], q[:, t_ * P:(t_ + 1) * P], k, start=m == 0,
                            stop=m == len(ops) - 1))
                yield
                src = PS[:, bank, :]
                if bias:
                    dist, slope = bias(h)
                    t_s = do("dve", lambda e: e.scalar_tensor_tensor(
                        out=s_, in0=dist, scalar=slope, in1=PS[:, bank, :], op0=ALU.mult, op1=ALU.add), t_s, free)
                    src = s_
                t = do("dve", lambda e: e.tensor_reduce(
                    nm, src.rearrange("p (t k) -> p t k", t=TB), AX.X, ALU.max), t_s, free)
                if sink:
                    t = do("dve", lambda e: e.tensor_scalar(nm, nm, scale, sink(h), ALU.mult, ALU.max), t)
                    t_m = do("dve", lambda e: e.tensor_scalar(nm, nm, -1.0, None, ALU.mult), t)
                else:
                    t_m = do("dve", lambda e: e.tensor_scalar(nm, nm, -scale, None, ALU.mult), t)
                t_e = [do("act", lambda e, t_=t_: e.activation(
                    p_[:, t_ * S:(t_ + 1) * S], src[:, t_ * S:(t_ + 1) * S], ACT.Exp, bias=nm[:, t_:t_ + 1],
                    scale=scale, accum_out=den[:, t_:t_ + 1]), t_m, free) for t_ in range(TB)]
                if sink:
                    t_x = do("act", lambda e: e.activation(ex, nm, ACT.Exp, bias=sink(h)))
                yield
                for kb in range(TB):
                    for t_ in range(TB):
                        fn = lambda e, kb=kb, t_=t_: e.transpose(
                            PS[:, bank, (kb * TB + t_) * P:(kb * TB + t_ + 1) * P],
                            p_[:, t_ * S + kb * P:t_ * S + (kb + 1) * P], ident[:, :])
                        t_t = do("pe", fn, t_e) if kb and t_ else quiet("pe", fn, t_e)
                yield
                t_r = t_e
                if sink:
                    t_r = do("dve", lambda e: e.tensor_tensor(den, den, ex, ALU.add), t_x, t_e)
                t_r = do("dve", lambda e: e.reciprocal(den, den), t_r)
                t_c = do("act", lambda e: e.activation(s_, PS[:, bank, :], ACT.Copy), t_t, t_e)
                yield
                vv = v(h)
                for t_ in range(TB):
                    for kb in range(TB):
                        fn = lambda e, kb=kb, t_=t_: e.matmul(
                            PS[:, bank, t_ * P:(t_ + 1) * P], s_[:, (kb * TB + t_) * P:(kb * TB + t_ + 1) * P],
                            vv[:, kb, :], start=kb == 0, stop=kb == TB - 1)
                        t_o = do("pe", fn, t_c) if kb and t_ else quiet("pe", fn, t_c)
                yield
                done = [put(h, t_, PS[:, bank, t_ * P:(t_ + 1) * P], den[:, t_:t_ + 1], [t_o, t_r])
                        for t_ in range(TB)]
                lane["free"] = [t_o, t_c, done]

            return [lambda lane, h=h: head(h, lane) for h in range(n)]

        def put_in(dst):
            return lambda h, t_, ps, rden, after: do("dve", lambda e: e.tensor_scalar(
                dst[:, t_, h * P:(h + 1) * P], ps, rden, None, ALU.mult), after)

        t_h = norm_to_h(x, cat, lambda k: par("g_mem", k), [t_xn, t_y])
        t_q = products("mem_q", w_cols(I["mem_wq"][0], 0), 1, *to_channels(Z_C, 0), ch_cols=(0, 512), after=t_h,
                       evac_after=t_h)
        k_mem, q_mem, o_mem = ar(K_MEM, M_H, S), ar(Z_C, M_H, S), ar(Z_C + 1024, TB, M_I)
        t_gain = dma("sp", gains, bcast("sandwich_gains", 3 * D, D), "gains_in", t_xn)
        run_lanes((lanes, heads(M_H, lambda h: [(q_mem[:, h, :], k_mem[:, h, :])], M_D ** -0.5,
                        lambda h: v_mem[:, :, h * P:(h + 1) * P], put_in(o_mem), after=[t_q, fence_banks()])))
        fence = fence_banks()
        for engine in ("act", "dve"):
            wait(engine, fence)
            split_early(engine)
        t_h = to_h(o_mem, None, [fence], n_blocks=M_H)
        wo = I["mem_wo"][0].rearrange("(k p) n -> p k n", p=P)
        out_rows = sandwich(y, cat, gains, ssq4[1], t_gain)
        t_y = products("mem_o", lambda g, j: wo[:, :, g * 512:(g + 1) * 512], 4, *out_rows["evac"],
                       tok_cols=(0, 512), units=1, after=t_h, evac_after=[t_h, t_gain], finish=out_rows["finish"])
        split_early("act", halves=True)
        t_xn = add_normed(y, ssq4[1], [t_y, out_rows["done"]])

        t_h = norm_to_h(x, cat, lambda k: par("g_ffn", k), [t_xn, t_y])
        act_ff = ar(0, FB * S)
        CONV = 16128
        conv = ar(CONV, 2, 4, S)
        ff = {n: ctx.enter_context(nc.semaphore(n)) for n in ("taps", "gelu_made", "gated")}
        GATED_CREDIT = 2
        prog.queue["dve"].append(lambda e, i: e.sem_inc(ff["gated"], GATED_CREDIT))
        G0 = state["group"]

        def channel(name, g, half, c, j=0):
            at_ = PARAM_AT[name] + (j * 2 + half) * FB + c
            return params[:, bass.ds(g * 2 + at_, 1)]

        def up_act(e, g, parity):
            e.wait_ge(ff["gated"], g + 1)
            for m in range(4):
                half, c = m // 2, m % 2
                last = e.activation(conv[:, parity, m, :], PS[:, 2 * parity + half, c * S:(c + 1) * S], ACT.Identity,
                                    scale=channel("conv_w", g, half, c, 2), bias=channel("conv_b", g, half, c))
            return last

        def up_dve(e, g, parity):
            e.wait_ge(sem["act_evac"], EVAC_CREDIT + G0 + g + 1)
            for back in (1, 2):
                if back == 2:
                    e.wait_ge(ff["taps"], g + 1)
                for m in range(4):
                    half, c = m // 2, m % 2
                    d = conv[:, parity, m, back:]
                    last = e.scalar_tensor_tensor(out=d, in0=PS[:, 2 * parity + half, c * S:(c + 1) * S - back],
                                                  scalar=channel("conv_w", g, half, c, 2 - back), in1=d,
                                                  op0=ALU.mult, op1=ALU.add)
                if back == 1:
                    last.then_inc(ff["taps"], 1)
            return last

        def gate_act(e, g, parity):
            e.wait_ge(sem["dve_evac"], EVAC_CREDIT + G0 + g + 1)
            e.activation(conv[:, parity, 0:2, :], conv[:, parity, 0:2, :], ACT.Gelu_apprx_tanh)\
             .then_inc(ff["gelu_made"], 1)

        def gate_dve(e, g, parity):
            e.wait_ge(ff["gelu_made"], g + 1)
            flat2 = lambda a: a.rearrange("p c n -> p (c n)")
            e.tensor_tensor(act_ff[:, bass.ds(g * (2 * S), 2 * S)], flat2(conv[:, parity, 0:2, :]),
                            flat2(conv[:, parity, 2:4, :]), ALU.mult).then_inc(ff["gated"], 1)

        w_up = I["ffn_w_up"][0].rearrange("(k p) n -> p k n", p=P)
        t_u = products("ffn_up", lambda g, j: tuple(w_up[:, 4 * j:4 * j + 4, bass.ds(g * S + a, S)]
                                                    for a in (0, D_FF)), FB // 2,
                       up_act, up_dve, ch_cols=(0, 512), after=t_h, evac_after=t_h,
                       finish={"act": gate_act, "dve": gate_dve}, halves=True, more=True)
        last_group, state["left"] = state["left"], None
        for engine in ("act", "dve"):
            split_early(engine)
        state["early"] = set()
        prog.once(0, {w: lambda e, i, w=w: (last_group["evac"](e, w), last_group["end"](e, w))
                      for w in ("act", "dve")})
        t_gated = (ff["gated"], GATED_CREDIT + FB // 2)
        t_gain = dma("sp", gains, bcast("sandwich_gains", 5 * D, D), "gains_in", t_xn)

        w_down = I["ffn_w_down"][0].rearrange("(k p) n -> p k n", p=P)
        U0 = state["unit"]
        state["unit"] += FB

        def down(q, quad, U, first, final):
            def sp(e):
                for j in range(4):
                    load_unit(e, U + j, j, (1, 2048), w_down[:, bass.ds(q * 4 + j, 1), :])

            def rows(j):
                return act_ff[:, bass.ds(q * (4 * S) + j * S, S)]

            def act(e):
                for j in range(4):
                    e.wait_ge(sem["unit_used"], U + j + 1)
                    e.activation(h_hi[:, j % 2, :], rows(j), ACT.Copy).then_inc(ff_hi, 1)
                    if not (first and j == 0):
                        split_hi(e, U + j, quad, j, 2048)

            def dve(e):
                for j in range(4):
                    e.wait_ge(ff_hi, q * 4 + j + 1)
                    e.tensor_tensor(h_lo[:, j % 2, :], rows(j), h_hi[:, j % 2, :].bitcast(F32), ALU.subtract)\
                     .then_inc(ff_lo, 1)
                    if not (first and j == 0):
                        split_lo(e, U + j, j, 2048)

            def pe(e):
                for j in range(4):
                    s = j % 2
                    e.wait_ge(ff_lo, q * 4 + j + 1)
                    e.wait_ge(sem["lo_made"], LO_CREDIT + U + j + 1)
                    for t in range(TB):
                        for n in range(4):
                            ws = slice(n * 512, (n + 1) * 512)
                            last = three_pass(e, PS[:, 4 * t + n, :], h_hi[:, s, t * P:(t + 1) * P],
                                              h_lo[:, s, t * P:(t + 1) * P], w_hi[:, s, ws], w_lo[:, s, ws],
                                              first and j == 0, final and j == 3)
                    last.then_inc(sem["unit_used"], 1)
            return {"sp": sp, "act": act, "dve": dve, "pe": pe}

        ff_hi, ff_lo = (ctx.enter_context(nc.semaphore(n)) for n in ("ff_hi", "ff_lo"))
        fence = fence_banks()
        wait("act", t_u, t_gated)
        wait("dve", t_u, t_gated)
        wait("pe", t_u, fence)
        NQ = FB // 4
        for q, rolled in ((0, False), (1, True), (NQ - 1, False)):
            for en in ("sp", "act", "dve", "pe"):
                if rolled:
                    prog.loop(NQ - 2, {en: lambda e, i, en=en: down(i + 1, i + (U0 // 4 + 1), i * 4 + (U0 + 4),
                                                                    False, False)[en](e)})
                else:
                    prog.once(0, {en: lambda e, i, en=en, q=q: down(q, U0 // 4 + q, U0 + 4 * q, q == 0,
                                                                    q == NQ - 1)[en](e)})
        t_y = [(sem["unit_used"], UNIT_CREDIT + state["unit"])]
        ssq_ff = col(TB)
        rows_of = lambda t: PS[:, 4 * t:4 * t + 4, :].rearrange("p b n -> p (b n)")
        t_sq, t_yg = [t_y, t_gain], [t_y, t_gain]
        for n in range(TB):
            a, b = n, 1 - n
            t_sq, t_yg = (
                [do("act", lambda e, a=a: e.activation(cat[:, a, :], rows_of(a), ACT.Square,
                                                       accum_out=ssq_ff[:, a:a + 1]), t_yg)],
                [do("dve", lambda e, b=b: e.tensor_tensor(y[:, b, :], rows_of(b), gains, ALU.mult), t_sq)])
        split_early("act")
        t_xn = add_normed(y, ssq_ff.unsqueeze(2), [t_sq, t_yg])
        fence = fence_banks()

        ZT, ZTOK = 0, 4608
        NT_COLS = 3520
        zt2, ztok = ar(ZT, 18, S), ar(ZTOK, TB, NT_COLS)
        W_UQ, W_UKV, DIST, DISTM = 16128, 18432, 20480, 20992
        SINK, LAM, SUBLN, TRIG, INV, POS = 21504, 21512, 21768, 21896, 22024, 22056
        w_uq, w_ukv = ar(W_UQ, 3, 768), ar(W_UKV, 2, 1024)
        dist, dist_far = ar(DIST, TB * S), ar(DISTM, TB * S)
        pos_i = arena[:, POS:POS + S + TB].bitcast(I32)
        dma("act", pos_i[:, 0:S], bcast("positions_2", 0, S), "pos_in", fence)
        for t_ in range(TB):
            dma("act", pos_i[:, S + t_:S + t_ + 1], bass.AP(I["positions_2"].tensor, t_ * P, [[1, P], [1, 1]]),
                "pos_in")
        t_pos = dma("act", ar(INV, L2_HALF), bcast("inv_freq", 0, L2_HALF), "pos_in")
        def positions():
            d_i = arena[:, DISTM:DISTM + TB * S].bitcast(I32)
            t = [do("pool", lambda e, t_=t_: e.tensor_tensor(
                d_i[:, t_ * S:(t_ + 1) * S], pos_i[:, 0:S], pos_i[:, S + t_:S + t_ + 1].to_broadcast([P, S]),
                ALU.subtract), t_pos, fence) for t_ in range(TB)]
            t = do("dve", lambda e: e.tensor_copy(dist, d_i), t)
            yield
            t = do("act", lambda e: e.activation(dist, dist, ACT.Abs), t)
            yield
            t = do("dve", lambda e: e.tensor_scalar(dist_far, dist, float(P), BIG, ALU.is_gt, ALU.mult), t)
            yield
            t_dist.append(do("dve", lambda e: e.tensor_tensor(dist_far, dist_far, dist, ALU.add), t))
            yield
            pos_f = col(TB)
            k_i = arena[:, POS:POS + 128].bitcast(I32)
            k_f = arena[:, POS + 128:POS + 256]
            t1 = do("dve", lambda e: e.tensor_copy(pos_f, pos_i[:, S:S + TB]), t_pos)
            t1 = [do("dve", lambda e, t_=t_: e.tensor_scalar(trig[:, 0, t_, :], ar(INV, L2_HALF), pos_f[:, t_:t_ + 1],
                                                             None, ALU.mult), t1) for t_ in range(TB)]
            tr = ar(TRIG, 128)
            t1 = do("dve", lambda e: e.tensor_scalar(trig[:, 1, :, :], trig[:, 0, :, :], math.pi / 2, None, ALU.add), t1)
            t2 = do("dve", lambda e: e.tensor_scalar(k_f, tr, 1 / (2 * math.pi), None, ALU.mult), t1, t_dist)
            t2 = do("dve", lambda e: e.tensor_copy(k_i, k_f), t2)
            t2 = do("dve", lambda e: e.tensor_copy(k_f, k_i), t2)
            C1, C2 = 6.28125, 2 * math.pi - 6.28125
            for cst in (C1, C2):
                t2 = do("dve", lambda e, cst=cst: e.scalar_tensor_tensor(out=tr, in0=k_f, scalar=-cst, in1=tr,
                                                                         op0=ALU.mult, op1=ALU.add), t2)
            yield
            for cmp_, lim, turn_ in ((ALU.is_gt, math.pi, -2 * math.pi), (ALU.is_lt, -math.pi, 2 * math.pi)):
                t2 = do("dve", lambda e, c=cmp_, l=lim, u=turn_: e.tensor_scalar(k_f, tr, l, u, c, ALU.mult), t2)
                t2 = do("dve", lambda e: e.tensor_tensor(tr, tr, k_f, ALU.add), t2)
            t2 = do("dve", lambda e: e.tensor_scalar(tr, tr, 3.1415925, -3.1415925, ALU.min, ALU.max), t2)
            yield
            t_trig.append(do("act", lambda e: e.activation(tr, tr, ACT.Sin), t2))
            yield

        t_dist, t_trig, trig = [], [], ar(TRIG, 2, TB, L2_HALF)

        AV, AG, CQ, CKV, KR, BG, CV, CG = 0, 256, 1280, 1664, 1920, 1984, 2496, 3008
        MQ, MK, MV = 3072, 4096, 5120
        CQT, CKVT, QR, ROT, TMP, QRT, KRT = (CAT + n for n in (0, 768, 1280, 1920, 2688, 3008, 3520))
        DIFF = QR
        slopes = lambda n: [2.0 ** (-8.0 * (i + 1) / n) for i in range(n)]

        t_prev = [t_xn]
        def second_layer(layer, t_prev):
            lam_init = 0.8 - 0.6 * math.exp(-0.3 * layer)
            fence = fence_banks()
            t_h = norm_to_h(x, cat, lambda k: par(f"g_l{layer}", k), [t_prev, fence], early_act=layer > 0)
            dma("act", w_uq, I["mla_w_uq_2"][layer].rearrange("(k p) n -> p k n", p=P), "small_in", fence)
            dma("act", w_ukv, I["mla_w_ukv_2"][layer].rearrange("(k p) n -> p k n", p=P), "small_in")
            dma("act", ar(SINK, 8), bcast("swa_sink_2", 8 * layer, 8), "small_in")
            dma("act", ar(SUBLN, P), bcast("diff_subln_2", P * layer, P), "small_in")
            t_small = dma("act", ar(LAM, S), bcast("diff_lambda_2", S * layer, S), "small_in")
            w = I["w_in_2"][layer]
            side_work = {} if layer else {"rolled": False, "fill": positions()}
            products("q", w_cols(w, 0), 2, *to_channels(ZT, 0), ch_cols=(0, 512), after=t_h, evac_after=t_h,
                     more=True, **side_work)
            for _ in side_work.get("fill", ()):
                pass
            products("kv", w_cols(w, 1024), 1,
                     lambda e, g, bank: e.activation(ar(ZT + 8 * S, 512), bank, ACT.Copy),
                     lambda e, g, bank: e.tensor_copy(ztok[:, :, AV:AV + 256],
                                                      bank.rearrange("p (t n) -> p t n", t=TB)),
                     tok_cols=(256, 256), ch_cols=(0, 256), more=True)
            products("tok", w_cols(w, 1536), 4, *to_tokens(ztok, AG), tok_cols=(0, 512), more=True)
            t_tok = products("tok_end", w_cols(w, 3584, n_cols=192), 1,
                     *evac_pair(lambda g: ztok[:, 0, AG + 2048:AG + 2240], lambda g: ztok[:, 1, AG + 2048:AG + 2240]),
                     tok_cols=(0, 192), n_cols=192, more=True)
            lam, e2, neg_lam, subln = ar(LAM, 4, 64), col(2), col(1), ar(SUBLN, P)
            t_gates = []

            def gates_and_lambda():
                yield
                for g0, w0_ in ((AG, 512), (AG + 512, 512), (BG, 512)):
                    g_ = ztok[:, :, g0:g0 + w0_]
                    t_gates.append(do("act", lambda e, g_=g_: e.activation(g_, g_, ACT.Silu), t_tok))
                    yield
                t = do("dve", lambda e: e.tensor_tensor(lam[:, 0, :], lam[:, 0, :], lam[:, 1, :], ALU.mult), t_small)
                t = do("dve", lambda e: e.tensor_tensor(lam[:, 1, :], lam[:, 2, :], lam[:, 3, :], ALU.mult), t)
                t = do("dve", lambda e: e.tensor_reduce(e2, lam[:, 0:2, :], AX.X, ALU.add), t)
                yield
                t = do("act", lambda e: e.activation(e2, e2, ACT.Exp), t)
                yield
                t_lam.append(do("dve", lambda e: e.tensor_scalar(neg_lam, e2[:, 1:2], e2[:, 0:1], -lam_init,
                                                                 ALU.subtract, ALU.add), t))
                t_lam.append(do("dve", lambda e: e.tensor_scalar(subln, subln, 1.0 - lam_init, None, ALU.mult),
                                t_small))
            t_lam = []
            cq_t, ckv_t = ar(CQT, 3, S), ar(CKVT, 2, S)
            t_ct, t_rotated = [], []

            def ranks():
                start = [t_tok, t_small, t_trig, t_h]
                own_bank, bank_free = next_bank, work_bank_free
                yield

                for c0, nb, gname, dst in ((CQ, 3, "q_norm", cq_t), (CKV, 2, "kv_norm", ckv_t)):
                    wd = nb * P
                    ssq, t = sum_squares(lambda t_, c0=c0, wd=wd: ztok[:, t_, c0:c0 + wd],
                                         lambda t_, wd=wd: ar(QR + t_ * 512, wd),
                                         [start, t_ct])
                    rstd = col(2)
                    yield
                    t = rstd_of(ssq, rstd, wd, EPS, 2, t)
                    t = [do("dve", lambda e, t_=t_, c0=c0, wd=wd, rstd=rstd: e.tensor_scalar(
                        ztok[:, t_, c0:c0 + wd], ztok[:, t_, c0:c0 + wd], rstd[:, t_:t_ + 1], None, ALU.mult), t)
                        for t_ in range(TB)]
                    for k in range(nb):
                        b = own_bank()
                        wait("pe", t, bank_free[b])
                        for t_ in range(TB):
                            fn = lambda e, t_=t_, k=k, b=b, c0=c0: e.transpose(
                                PS[:, b, t_ * P:(t_ + 1) * P], ztok[:, t_, c0 + k * P:c0 + (k + 1) * P], ident[:, :])
                            t_t = do("pe", fn) if t_ else quiet("pe", fn)
                        gk = par(gname, layer * nb + k)
                        yield
                        tt = do("act", lambda e, k=k, b=b, dst=dst, gk=gk: e.activation(dst[:, k, :], PS[:, b, 0:S],
                                                                                        ACT.Copy, scale=gk), t_t)
                        bank_free[b] = [tt]
                        t_ct.append(tt)
                qr, rot = ar(QR, TB, 5, 64), ar(ROT, TB, 6, 64)
                b = own_bank()
                uq4 = w_uq.rearrange("p k (h n) -> p k h n", h=4)
                wait("pe", t_ct, bank_free[b])
                for t_ in range(TB):
                    for k in range(3):
                        fn = lambda e, t_=t_, k=k, b=b: e.matmul(
                            PS[:, b, t_ * S:(t_ + 1) * S], cq_t[:, k, t_ * P:(t_ + 1) * P], uq4[:, k, :, P:P + 64],
                            start=k == 0, stop=k == 2)
                        t = do("pe", fn) if k == 2 else quiet("pe", fn)
                f = start
                yield
                t = do("act", lambda e, b=b: e.activation(qr[:, :, 0:4, :].rearrange("p t h n -> p t (h n)"),
                                                          PS[:, b, :].rearrange("p (t n) -> p t n", t=TB), ACT.Copy), t, f)
                bank_free[b] = [t]
                t_kr = do("dve", lambda e: e.tensor_copy(qr[:, :, 4, :], ztok[:, :, KR:KR + 64]), f)
                t_rot = []
                for t_ in range(TB):
                    sin, cos = (trig[:, m, t_, :].unsqueeze(1).to_broadcast([P, 5, L2_HALF]) for m in (0, 1))
                    yield
                    x1, x2 = qr[:, t_, :, 0:L2_HALF], qr[:, t_, :, L2_HALF:]
                    ta, tb_ = ar(TMP, 5, L2_HALF), ar(TMP + 160, 5, L2_HALF)
                    for o, m1, m2, op in ((0, cos, sin, ALU.subtract), (L2_HALF, sin, cos, ALU.add)):
                        a1 = do("dve", lambda e, x1=x1, m1=m1, ta=ta: e.tensor_tensor(ta, x1, m1, ALU.mult), t, t_kr, t_trig,
                                t_rot[-1:])
                        a2 = do("dve", lambda e, x2=x2, m2=m2, tb_=tb_: e.tensor_tensor(tb_, x2, m2, ALU.mult))
                        a3 = do("dve", lambda e, t_=t_, o=o, op=op, ta=ta, tb_=tb_: e.tensor_tensor(
                            rot[:, t_, 0:5, o:o + L2_HALF], ta, tb_, op), a1, a2)
                        t_rot.append(a3)
                t_rot = do("dve", lambda e: e.tensor_copy(rot[:, :, 5, :], rot[:, :, 4, :]), t_rot)
                for blk in range(3):
                    b = own_bank()
                    wait("pe", t_rot, bank_free[b])
                    for t_ in range(TB):
                        fn = lambda e, t_=t_, blk=blk, b=b: e.transpose(
                            PS[:, b, t_ * P:(t_ + 1) * P], rot[:, t_, 2 * blk:2 * blk + 2, :].rearrange("p a n -> p (a n)"),
                            ident[:, :])
                        t = do("pe", fn) if t_ else quiet("pe", fn)
                    yield
                    t = do("act", lambda e, blk=blk, b=b: e.activation(ar(QRT + blk * S, S), PS[:, b, 0:S], ACT.Copy), t)
                    bank_free[b] = [t]
                    t_rotated.append(t)

            fill = side_by_side(gates_and_lambda(), ranks())
            products("c_qk", w_cols(w, 3776), 2, *to_channels(ZT, 10), ch_cols=(0, 512), more=True,
                     rolled=False, fill=fill)
            t_z = products("c_vg", w_cols(w, 4800), 2, *to_tokens(ztok, CV), tok_cols=(0, 512), rolled=False,
                           fill=fill)
            for _ in fill:
                pass
            fence = fence_banks()
            t = do("act", lambda e: e.activation(ztok[:, :, CG:CG + 512], ztok[:, :, CG:CG + 512], ACT.Silu), t_z)
            t_cg = [do("pool", lambda e, t_=t_: e.tensor_tensor(
                ztok[:, t_, CG:CG + 512].rearrange("p (h n) -> p h n", h=4),
                ztok[:, t_, CG:CG + 512].rearrange("p (h n) -> p h n", h=4),
                subln.unsqueeze(1).to_broadcast([P, 4, P]), ALU.mult), t, t_lam) for t_ in range(TB)]

            def gated(g0):
                def put(h, t_, ps, rden, after):
                    g_ = ztok[:, t_, g0 + h * P:g0 + (h + 1) * P]
                    return do("dve", lambda e: e.scalar_tensor_tensor(out=g_, in0=ps, scalar=rden, in1=g_,
                                                                      op0=ALU.mult, op1=ALU.mult), after, t_gates)
                return put

            SC = P ** -0.5
            swa = heads(
                8, lambda h: [(zt2[:, h, :], zt2[:, 8 + h // 4, :])], SC,
                lambda h: ztok[:, :, AV + (h // 4) * P:AV + (h // 4 + 1) * P], gated(AG),
                bias=lambda h: (dist_far, -slopes(8)[h] / SC), sink=lambda h: ar(SINK, 8)[:, h:h + 1],
                after=[t_z, t_small, t_dist, fence])

            def latents(lane):
                b, bank_free = lane["bank"], [lane["free"], fence]
                for dst, wsrc, n_k, src, stride in ((MQ, w_uq, 3, cq_t, 192), (MK, w_ukv, 2, ckv_t, 256)):
                    for hp in range(2):
                        yield
                        wait("pe", t_ct, bank_free)
                        for hh in range(2):
                            for k in range(n_k):
                                h = 2 * hp + hh
                                fn = lambda e, hh=hh, h=h, k=k, wsrc=wsrc, src=src, stride=stride, n_k=n_k: e.matmul(
                                    PS[:, b, hh * S:(hh + 1) * S], wsrc[:, k, h * stride:h * stride + P], src[:, k, :],
                                    start=k == 0, stop=k == n_k - 1)
                                t = do("pe", fn) if hh and k == n_k - 1 else quiet("pe", fn)
                        yield
                        t = do("act", lambda e, dst=dst, hp=hp: e.activation(sd(dst + hp * 512, 512), PS[:, b, :],
                                                                                  ACT.Copy), t, fence)
                        bank_free = [t]
                ukv4 = w_ukv.rearrange("p k (h n) -> p k h n", h=4)
                for t_ in range(TB):
                    yield
                    wait("pe", bank_free)
                    for k in range(2):
                        fn = lambda e, t_=t_, k=k: e.matmul(PS[:, b, :], ckv_t[:, k, t_ * P:(t_ + 1) * P],
                                                                 ukv4[:, k, :, P:2 * P], start=k == 0, stop=k == 1)
                        t = do("pe", fn) if k else quiet("pe", fn)
                    yield
                    t = do("dve", lambda e, t_=t_: e.tensor_copy(sd(MV + 512 * t_, 512), PS[:, b, :]), t, fence)
                    bank_free = [t]
                lane["free"] = bank_free
                t_latents.append(prog.all_done())
            t_latents = []
            mq, mk, mv, qrt, krt = sd(MQ, 4, S), sd(MK, 4, S), sd(MV, TB, 512), ar(QRT, 2, S), ar(KRT, S)
            half = lambda h: slice(64 * (h % 2), 64 * (h % 2) + 64)
            mla = heads(
                4, lambda h: [(mq[:, h, :], mk[:, h, :]), (qrt[half(h), h // 2, :], krt[half(h), :])],
                   (P + 64) ** -0.5, lambda h: mv[:, :, h * P:(h + 1) * P], gated(BG),
                   after=[t_latents, t_rotated])

            ssq = col(TB * 4)

            first_put, diff_out = {}, ar(DIFF, TB, 512)

            def put_diff(j, t_, ps, rden, after):
                h, second = j // 2, j % 2
                d = diff_out[:, t_, h * P:(h + 1) * P]
                if not second:
                    first_put[t_, h] = do("dve", lambda e: e.tensor_scalar(d, ps, rden, None, ALU.mult), after)
                    return first_put[t_, h]
                t = do("dve", lambda e: e.tensor_tensor(rden, rden, neg_lam, ALU.mult), after, t_lam)
                t = do("dve", lambda e: e.scalar_tensor_tensor(out=d, in0=ps, scalar=rden, in1=d, op0=ALU.mult,
                                                               op1=ALU.add), t, first_put[t_, h])
                return t, do("act", lambda e: e.activation(sd(P * (4 * t_ + h), P), d, ACT.Square,
                                                           accum_out=ssq[:, 4 * t_ + h:4 * t_ + h + 1]), t)
            DSC = 64 ** -0.5
            half2 = lambda j: slice(64 * (j % 2), 64 * (j % 2) + 64)
            diff = heads(
                8, lambda j: [(zt2[half2(j), 10 + j // 2, :], zt2[half2(j), 14 + j // 2, :])], DSC,
                           lambda j: ztok[:, :, CV + (j // 2) * P:CV + (j // 2 + 1) * P], put_diff,
                           bias=lambda j: (dist, -slopes(4)[j // 2] / DSC), after=[t_z, t_small, t_dist, fence, t_lam, t_rotated])
            def behind_latents(job):
                def run(lane):
                    while not t_latents:
                        yield
                    yield from job(lane)
                return run
            run_lanes((lanes, [latents] + swa + diff + [behind_latents(job) for job in mla]))
            fence = fence_banks()
            wait("act", fence)
            split_early("act")
            t = rstd_of(ssq, ssq, P, EPS, TB * 4, fence)
            t_n = []
            for t_ in range(TB):
                v4 = diff_out[:, t_, :].rearrange("p (h n) -> p h n", h=4)
                a = do("dve", lambda e, t_=t_, v4=v4: e.tensor_tensor(
                    v4, v4, ssq[:, 4 * t_:4 * t_ + 4].unsqueeze(2).to_broadcast([P, 4, P]), ALU.mult), t)
                t_n.append(do("dve", lambda e, t_=t_: e.tensor_tensor(
                    diff_out[:, t_, :], diff_out[:, t_, :], ztok[:, t_, CG:CG + 512], ALU.mult), a, t_cg))

            def mixed_block(t_, k):
                return (ztok[:, t_, AG + k * P:AG + (k + 1) * P] if k < 8 else
                        ztok[:, t_, BG + (k - 8) * P:BG + (k - 7) * P] if k < 12 else
                        diff_out[:, t_, (k - 12) * P:(k - 11) * P])
            split_early("dve")
            t_h = to_h(mixed_block, None, [fence], ready=lambda k: t_n if k >= 12 else None)

            y2 = ar(0, D)

            G0 = state["group"]

            def copy_rows(e, g, parity):
                return e.activation(y2[:, bass.ds(g * 512, 512)], PS[:, 2 * parity, :], ACT.Copy)

            def add_rows(e, g, parity):
                xs = x[:, 1, bass.ds(g * 512, 512)]
                return e.tensor_tensor(xs, xs, PS[:, 2 * parity + 1, :], ALU.add)

            def add_copied(e, g, parity):
                e.wait_ge(sem["act_evac"], EVAC_CREDIT + G0 + g + 1)
                xs = x[:, 0, bass.ds(g * 512, 512)]
                e.tensor_tensor(xs, xs, y2[:, bass.ds(g * 512, 512)], ALU.add).then_inc(sem["gained"], 1)

            t_y = products("w_out_2", w_cols(I["w_out_2"][layer], 0), 4, copy_rows, add_rows,
                           tok_cols=(0, 512), after=t_h, evac_after=[t_h, prog.all_done()],
                           finish={"act": lambda e, g, parity: None, "dve": add_copied})
            n_gained[0] += 4
            return [t_y, (sem["gained"], n_gained[0])]

        for layer in range(LAYERS):
            t_prev = second_layer(layer, t_prev)

        FG = 4096
        t_fg = dma("sp", ar(FG, D), bcast("final_norm_2", 0, D), "final_in",
                   prog.all_done(), t_prev)
        ssq, t = sum_squares(lambda t: x[:, t, :], lambda t: cat[:, t, :], t_prev)
        rstd = col(2)
        t = rstd_of(ssq, rstd, D, EPS, 2, t)
        for t_ in range(TB):
            t1 = do("dve", lambda e, t_=t_: e.scalar_tensor_tensor(
                out=cat[:, t_, :], in0=x[:, t_, :], scalar=rstd[:, t_:t_ + 1], in1=ar(FG, D), op0=ALU.mult,
                op1=ALU.mult), t, t_fg)
            t_out = dma("sp" if t_ else "act", out[0, t_ * P:(t_ + 1) * P, :], cat[:, t_, :], "out_done", t1)
        for en in ("sp", "act"):
            wait(en, t_out)

        block = ctx.enter_context(nc.Block())
        for name, deco in (("sp", block.sync), ("pe", block.tensor), ("act", block.scalar),
                           ("dve", block.vector), ("pool", block.gpsimd)):
            def run(e, name=name):
                for f in prog.queue[name]:
                    f(e, 0)
            deco(run)


_DIRECT = ["x", "mem", "rel_bias_table", "sandwich_gains", "w_in", "w_out", "sgu_norm_gain", "sgu_w",
           "rwkv_w_up", "rwkv_a_up", "rwkv_g_up", "rwkv_ln_gain", "rwkv_ln_bias", "mem_wq", "mem_wkv", "mem_wo",
           "ffn_w_up", "ffn_w_down", "positions_2", "w_in_2", "swa_sink_2", "mla_w_uq_2", "mla_w_ukv_2",
           "diff_lambda_2", "diff_subln_2", "w_out_2", "final_norm_2"]


def constants():
    c = {"ident": np.eye(P, dtype=np.float32), "exch": np.eye(P, dtype=np.float32)[::-1].copy()}
    dist = 255 - np.arange(384)
    count = ((dist >= 0) & (dist <= 128)) * 1 + ((dist >= 0) & (dist % 4 == 0)) + ((dist >= 0) & (dist % 16 == 0))
    exact = REL // 2
    d = np.maximum(dist, 0)
    scaled = np.log(np.maximum(d, 1) / exact) / np.log(2048 / exact)
    large = np.minimum(exact + (scaled * (REL - exact)).astype(np.int32), REL - 1)
    bucket = np.where(d < exact, d, large)
    onehot = np.zeros((REL + 1, 384), np.float32)
    seen = count > 0
    onehot[bucket[seen], np.nonzero(seen)[0]] = 8.0
    onehot[REL] = np.where(seen, 8.0 * np.log(np.maximum(count, 1)), 8.0 * NEG)
    c["onehot"] = onehot
    t, s = np.arange(P)[:, None], np.arange(P)[None, :]
    masks = np.zeros((P, 1282), np.float32)
    for l in range(7):
        m = (t // (2 << l) == s // (2 << l)) & ((t >> l) % 2 == 1) & ((s >> l) % 2 == 0)
        masks[:, P * l:P * (l + 1)] = -1.0 * m
        if l == 0:
            masks[:, 7 * P:8 * P] = -1.0 * m.T
    masks[:, 8 * P:9 * P] = t // HD == s // HD
    masks[:, 9 * P] = np.arange(P) < HD
    masks[:, 9 * P + 1] = np.arange(P) >= HD
    masks[:, 9 * P + 2:9 * P + 2 + P] = 1.0
    c["masks"] = masks
    strict, incl = t < s, t <= s
    c["pair_mask"] = np.concatenate([strict, incl, strict, incl], axis=1).astype(np.int32)
    c["inv_freq"] = (np.float32(10000.0) ** (-np.arange(0, 64, 2, dtype=np.float32) / np.float32(64)))\
        .astype(np.float32)[None, :]
    return c


def kernel(**inputs):
    import concourse.bacc as _bacc
    from concourse.bass_utils import run_bass_kernel_spmd as _run

    a = {n: np.asarray(v) for n, v in inputs.items()}
    g = a["sandwich_gains"][0]
    parts = [g[0], g[2], g[4], a["mem_src_gain"], a["norm_g_2"][0], a["norm_g_2"][1], a["rwkv_mu"], a["rwkv_w0"],
             a["rwkv_a0"], a["rwkv_k_k"], a["rwkv_k_a"], a["rwkv_r_k"], a["attn_out_gain"], a["sgu_out_gain"],
             a["ffn_conv_b"], a["ffn_conv_w"], a["mla_q_norm_2"], a["mla_kv_norm_2"]]
    laid = {n: a[n] for n in _DIRECT}
    laid["params"] = np.ascontiguousarray(np.concatenate([p.reshape(-1, P) for p in parts]).T)
    laid["sgu_b_t"] = np.ascontiguousarray(a["sgu_b"][0].T)
    laid.update(constants())
    nc = _bacc.Bacc("TRN2", target_bir_lowering=False, num_devices=1)
    arrays, aps = {}, {}
    for name, v in laid.items():
        v = np.ascontiguousarray(v)
        arrays[f"in_{name}"] = v
        aps[name] = nc.dram_tensor(f"in_{name}", v.shape, mybir.dt.from_np(v.dtype), kind="ExternalInput").ap()
    aps["scratch"] = nc.dram_tensor("bias_rows", (A_H, 384), F32, kind="Internal").ap()
    out = nc.dram_tensor("out_0", (1, S, D), F32, kind="ExternalOutput").ap()
    hybrid_two_blocks(nc, aps, out)
    r = _run(nc, [arrays], core_ids=[0])
    return r.results[0]["out_0"]
```
